# Optimizing a Trainium2 kernel written in Bass

```python
import math
import jax, jax.numpy as jnp
from jax import lax
import numpy as np

D_MODEL = 1024
BATCH = 1
SEQ = 512
DEPTH = 1

CHUNK = 64
D_MIX = D_MODEL
RET_WIDTH = D_MIX // 2
RET_HEADS = 4
RET_HEAD_DIM = RET_WIDTH // RET_HEADS
POOL_WIDTH = D_MIX - RET_WIDTH
POOL_WINDOWS = (2, 4, 8, 16)
POOL_GROUPS = len(POOL_WINDOWS)
POOL_GROUP_WIDTH = POOL_WIDTH // POOL_GROUPS
D_IN = 4 * RET_WIDTH + POOL_WIDTH
ROPE_BASE = 10000.0
N_EXPERTS = 32
TOP_K = 4
D_FF_EXPERT = D_MODEL
SWIGLU_LIMIT = 7.0
SWIGLU_ALPHA = 1.702
MOE_BLOCK = 128
EPS = 1e-6

kernel_name = "hybrid_retention_pool_moe_block"

def rms_norm(x, w):
    x32 = x.astype(jnp.float32)
    y = x32 * lax.rsqrt(jnp.mean(x32 * x32, axis=-1, keepdims=True) + EPS)
    return (y * w.astype(jnp.float32)).astype(x.dtype)

def rope_tables(seq_len, dim):
    half = dim // 2
    inv = ROPE_BASE ** (-jnp.arange(half, dtype=jnp.float32) / half)
    ang = jnp.arange(seq_len, dtype=jnp.float32)[:, None] * inv[None, :]
    return jnp.cos(ang), jnp.sin(ang)

def apply_rope(t, cos, sin):
    half = t.shape[-1] // 2
    t1, t2 = t[..., :half], t[..., half:]
    c, s = cos.astype(t.dtype), sin.astype(t.dtype)
    return jnp.concatenate([t1 * c - t2 * s, t1 * s + t2 * c], axis=-1)

def retention(q, k, v):
    B, S, _ = q.shape
    H, d, C = RET_HEADS, RET_HEAD_DIM, CHUNK
    NC = S // C

    def heads(t):
        return t.reshape(B, S, H, d).transpose(0, 2, 1, 3)

    cos, sin = rope_tables(S, d)
    qh = apply_rope(heads(q), cos, sin)
    kh = apply_rope(heads(k), cos, sin) * (d ** -0.5)
    vh = heads(v)
    qc = qh.reshape(B, H, NC, C, d)
    kc = kh.reshape(B, H, NC, C, d)
    vc = vh.reshape(B, H, NC, C, d)

    log_g = jnp.log1p(-jnp.exp2(-5.0 - jnp.arange(H, dtype=jnp.float32)))
    pos = jnp.arange(C, dtype=jnp.float32)
    dt = q.dtype

    inner_decay = jnp.exp(log_g[:, None, None] * jnp.abs(pos[:, None] - pos[None, :])).astype(dt)
    scores = jnp.einsum('bhcnd,bhcmd->bhcnm', qc, kc) * inner_decay[None, :, None]
    inner = jnp.einsum('bhcnm,bhcmv->bhcnv', scores, vc)

    k_decay = jnp.exp(log_g[:, None] * (C - 1 - pos)[None, :]).astype(dt)
    U = jnp.einsum('bhcmd,bhcmv->cbhdv', kc * k_decay[None, :, None, :, None], vc)
    chunk_decay = jnp.exp(log_g * C).astype(U.dtype)[None, :, None, None]

    def step(R, U_c):
        return chunk_decay * R + U_c, R

    _, R_prev = lax.scan(step, jnp.zeros_like(U[0]), U)
    q_decay = jnp.exp(log_g[:, None] * (pos + 1.0)[None, :]).astype(dt)
    cross = jnp.einsum('bhcnd,cbhdv->bhcnv', qc * q_decay[None, :, None, :, None], R_prev)

    o = (inner + cross).reshape(B, H, S, d).astype(jnp.float32)
    o = o * lax.rsqrt(jnp.mean(o * o, axis=-1, keepdims=True) + EPS)
    return o.transpose(0, 2, 1, 3).reshape(B, S, H * d).astype(dt)

def pool_mixer(p, w_pool, pool_scale):
    B, S, _ = p.shape
    cs = jnp.cumsum(p.astype(jnp.float32), axis=1)
    t = jnp.arange(S, dtype=jnp.int32)
    outs = []
    for g, w in enumerate(POOL_WINDOWS):
        c = cs[..., g * POOL_GROUP_WIDTH:(g + 1) * POOL_GROUP_WIDTH]
        lagged = jnp.pad(c, ((0, 0), (w, 0), (0, 0)))[:, :S]
        count = jnp.minimum(t + 1, w).astype(jnp.float32)[None, :, None]
        outs.append((c - lagged) / count)
    pooled = jnp.stack(outs, axis=2) - p.astype(jnp.float32).reshape(B, S, POOL_GROUPS, POOL_GROUP_WIDTH)
    mixed = jnp.einsum('bsgc,gcd->bsgd', pooled.astype(p.dtype), w_pool)
    return mixed.reshape(B, S, POOL_WIDTH) * pool_scale

def moe(h, w_router, b_router, w_gu, b_gu, w_down, b_down):
    B, S, D = h.shape
    N = B * S
    A = N * TOP_K
    F = D_FF_EXPERT
    xt = h.reshape(N, D)
    logits = (xt @ w_router + b_router).astype(jnp.float32)
    top_vals, top_idx = lax.top_k(logits, TOP_K)
    gates = jax.nn.softmax(top_vals, axis=-1).astype(h.dtype)

    e_flat = top_idx.reshape(A).astype(jnp.int32)
    g_flat = gates.reshape(A)
    tok_flat = jnp.arange(A, dtype=jnp.int32) // TOP_K
    order = jnp.argsort(e_flat)
    e_sorted = e_flat[order]
    counts = jnp.zeros((N_EXPERTS,), jnp.int32).at[e_flat].add(1)
    padded = ((counts + MOE_BLOCK - 1) // MOE_BLOCK) * MOE_BLOCK
    pad_end = jnp.cumsum(padded)
    pad_start = pad_end - padded
    start = jnp.cumsum(counts) - counts
    dest = pad_start[e_sorted] + (jnp.arange(A, dtype=jnp.int32) - start[e_sorted])

    n_blocks = (A + MOE_BLOCK - 1) // MOE_BLOCK + N_EXPERTS
    P = n_blocks * MOE_BLOCK
    row_tok = jnp.full((P,), N, jnp.int32).at[dest].set(tok_flat[order])
    row_gate = jnp.zeros((P,), h.dtype).at[dest].set(g_flat[order])
    block_start = jnp.arange(n_blocks, dtype=jnp.int32) * MOE_BLOCK
    block_exp = jnp.minimum(jnp.searchsorted(pad_end, block_start, side='right'), N_EXPERTS - 1)

    x_pad = jnp.concatenate([xt, jnp.zeros((1, D), xt.dtype)], axis=0)
    xb = x_pad[row_tok].reshape(n_blocks, MOE_BLOCK, D)

    def expert_block(args):
        xblk, e = args
        gu = xblk @ w_gu[e] + b_gu[e]
        x_glu = jnp.minimum(gu[:, :F], SWIGLU_LIMIT)
        x_lin = jnp.clip(gu[:, F:], -SWIGLU_LIMIT, SWIGLU_LIMIT)
        act = x_glu * jax.nn.sigmoid(SWIGLU_ALPHA * x_glu) * (x_lin + 1.0)
        return act @ w_down[e] + b_down[e]

    yb = lax.map(expert_block, (xb, block_exp))
    y = yb.reshape(P, D) * row_gate[:, None]
    out = jax.ops.segment_sum(y, row_tok, num_segments=N + 1)[:N]
    return out.reshape(B, S, D)

def setup_inputs(seed: int = 0) -> dict:
    key = jax.random.key(seed)
    ks = jax.random.split(key, 16)
    f32 = jnp.float32
    L, E, D, F = DEPTH, N_EXPERTS, D_MODEL, D_FF_EXPERT
    return {
        "x": jax.random.normal(ks[0], (BATCH, SEQ, D), f32),
        "norm_mix_w": 1.0 + 0.02 * jax.random.normal(ks[1], (L, D), f32),
        "w_in": jax.random.normal(ks[2], (L, D, D_IN), f32) * D ** -0.5,
        "ret_norm_w": 1.0 + 0.02 * jax.random.normal(ks[3], (L, RET_WIDTH), f32),
        "w_pool": jax.random.normal(ks[4], (L, POOL_GROUPS, POOL_GROUP_WIDTH, POOL_GROUP_WIDTH), f32) * POOL_GROUP_WIDTH ** -0.5,
        "pool_scale": 1.0 + 0.02 * jax.random.normal(ks[5], (L, POOL_WIDTH), f32),
        "w_out": jax.random.normal(ks[6], (L, D_MIX, D), f32) * D_MIX ** -0.5,
        "norm_ffn_w": 1.0 + 0.02 * jax.random.normal(ks[7], (L, D), f32),
        "w_router": jax.random.normal(ks[8], (L, D, E), f32) * D ** -0.5,
        "b_router": 0.01 * jax.random.normal(ks[9], (L, E), f32),
        "w_gu": jax.random.normal(ks[10], (L, E, D, 2 * F), f32) * D ** -0.5,
        "b_gu": 0.02 * jax.random.normal(ks[11], (L, E, 2 * F), f32),
        "w_down": jax.random.normal(ks[12], (L, E, F, D), f32) * F ** -0.5,
        "b_down": 0.02 * jax.random.normal(ks[13], (L, E, D), f32),
        "norm_final_w": 1.0 + 0.02 * jax.random.normal(ks[14], (D,), f32),
    }

def reference(x, norm_mix_w, w_in, ret_norm_w, w_pool, pool_scale, w_out, norm_ffn_w,
              w_router, b_router, w_gu, b_gu, w_down, b_down, norm_final_w):
    for l in range(DEPTH):
        h = rms_norm(x, norm_mix_w[l])
        z = h @ w_in[l]
        q, k, v, g, p = jnp.split(z, [RET_WIDTH, 2 * RET_WIDTH, 3 * RET_WIDTH, 4 * RET_WIDTH], axis=-1)
        ret = retention(q, k, v) * ret_norm_w[l] * jax.nn.silu(g)
        pool = pool_mixer(p, w_pool[l], pool_scale[l])
        x = x + jnp.concatenate([ret, pool], axis=-1) @ w_out[l]
        h2 = rms_norm(x, norm_ffn_w[l])
        x = x + moe(h2, w_router[l], b_router[l], w_gu[l], b_gu[l], w_down[l], b_down[l])
    return rms_norm(x, norm_final_w)


_drawn_inputs = setup_inputs


def setup_inputs(seed=0):
    import zlib

    import numpy as np

    out = dict(_drawn_inputs(seed))
    spreads = {}
    factors = {'ret_norm_w': 3.325, 'b_gu': 6.197, 'b_down': 7.044, 'norm_final_w': 2.87}
    for name, (base, spread) in spreads.items():
        noise = np.random.default_rng([zlib.crc32(name.encode()), seed]).standard_normal(out[name].shape)
        drawn = base * np.exp(spread * noise) if base else spread * noise
        out[name] = __import__('jax').numpy.asarray(drawn.astype(out[name].dtype))
    for name, factor in factors.items():
        out[name] = (out[name] * factor).astype(out[name].dtype)
    return out
```

```python
from contextlib import ExitStack

import concourse.bass as bass
from concourse import mybir

ALU = mybir.AluOpType
ACT = mybir.ActivationFunctionType
AX_X = mybir.AxisListType.X
F32 = mybir.dt.float32
BF16 = mybir.dt.bfloat16
I32 = mybir.dt.int32
U32 = mybir.dt.uint32

P = 128
CAP = 96
EPS = 1e-6
TOP_K = 4
WINDOWS = (2, 4, 8, 16)
LIMIT = 7.0
ALPHA = 1.702
CHUNK = 64


def build_program(nc, x, norm_mix_w, w_in, ret_norm_w, w_pool, pool_scale, w_out, norm_ffn_w, w_router,
                  b_router, w_gu, b_gu, w_down, b_down, norm_final_w, rope, decay, small, out):
    _, S, D = x.shape
    E = w_router.shape[2]
    F = w_down.shape[2]
    NT = S // P
    KD = D // P
    W = w_in.shape[2] // 5
    H = W // P
    NF = 2 * F // P
    BLOCKS = -(-S // CAP)
    RANKS = BLOCKS * CAP
    FIRST = E * CAP
    GU_CH = KD
    DN_CH = F // P // 2
    CH = GU_CH + DN_CH
    SLOT = 2 * F
    GB = 4
    PER = NF // GB
    assert D == F and W == 512 and H == 4 and NT == 4 and GU_CH == 8 and S == 512 and PER * CAP <= 512

    y_rows = nc.dram_tensor("y_rows", [BLOCKS * FIRST, D], F32, kind="Internal").ap()

    with ExitStack() as ctx:
        def sb(name, shape, dt=F32):
            return ctx.enter_context(nc.sbuf_tensor(name, shape, dt))

        def sem(name):
            return ctx.enter_context(nc.semaphore(name))

        ring = sb("ring", [P, CH, SLOT])
        arena = sb("arena", [P, 24160])
        at = [0]

        def region(cols):
            at[0] += cols
            return arena[:, at[0] - cols:at[0]]

        x_sb = region(NT * D).rearrange("p (t d) -> p t d", t=NT)
        reg_h = region(KD * S)
        reg_vg = region(2048 + 2048 + 2560)
        reg_d = region(2048)
        reg_r = region(2048)
        reg_p = region(2112 + 1056 + 2048)

        hT = reg_h.rearrange("p (k s) -> p k s", k=KD)
        mixT = hT
        v_sb = reg_vg[:, 0:2048].rearrange("p (t c) -> p t c", t=NT)
        gate_sb = reg_vg[:, 2048:4096].rearrange("p (t c) -> p t c", t=NT)
        sT = reg_vg[:, 4096:6656].rearrange("p (b c) -> p b c", b=2)
        xn1 = reg_vg[:, 0:2048].rearrange("p (b c) -> p b c", b=2)
        dec = reg_d.rearrange("p (h c) -> p h c", h=H)
        rope_c = reg_r[:, 0:512].rearrange("p (t c) -> p t c", t=NT)
        rope_s = reg_r[:, 512:1024].rearrange("p (t c) -> p t c", t=NT)
        rot = reg_r[:, 1024:2048].rearrange("p (b c) -> p b c", b=2)
        PADS = 16
        pT = reg_p[:, 0:2112].rearrange("p (g c) -> p g c", g=H)
        psum_a = reg_p[:, 2112:2112 + 528]
        psum_b = reg_p[:, 2640:2640 + 528]
        mixtok = reg_p[:, 3168:5216].rearrange("p (h c) -> p h c", h=H)
        qT = ring[:, 10, :].rearrange("p (h s) -> p h s", h=H)
        kT = ring[:, 11, :].rearrange("p (h s) -> p h s", h=H)
        bgu_raw = mixtok[:, 0, :]
        parts = reg_vg[:, 0:6144].bitcast(BF16).rearrange("p (i t d) -> p i t d", i=3, t=NT)
        h2T = reg_d.rearrange("p (b k c) -> p b k c", b=2, k=KD)
        xn2 = reg_r.rearrange("p (b c) -> p b c", b=2)
        rest = reg_p[:, 0:1024]
        xT = reg_h[:, 0:KD * CAP].rearrange("p (k c) -> p k c", k=KD)
        actT = reg_h[:, 768:768 + KD * CAP].rearrange("p (k c) -> p k c", k=KD)
        yT = reg_h[:, 1536:1536 + KD * CAP].rearrange("p (k c) -> p k c", k=KD)
        gub = reg_h[:, 2304:2304 + 2 * PER * CAP].rearrange("p (b h c) -> p b h c", b=2, h=2)
        prod = reg_h[:, 3072:3072 + PER * CAP].rearrange("p (b c) -> p b c", b=2)
        sig = reg_h[:, 3456:3456 + PER * CAP].rearrange("p (b c) -> p b c", b=2)
        zeros = reg_p[:, 0:1024]
        y_row = reg_p[:, 1024:2048]
        onehot = reg_p[:, 2048:2048 + NT * CAP // 2].bitcast(BF16).rearrange("p (t c) -> p t c", t=NT)
        got = ring[:, :, :].rearrange("p s (a d) -> p (s a) d", a=2)
        o_row = reg_vg[:, 0:4096].rearrange("p (t d) -> p t d", t=NT)
        fin_w = reg_h[:, 0:1024]
        bd_sb = reg_h[0:E, 1024:2048]
        gdT = reg_h[0:E, 2048:2048 + S]

        sm = sb("sm", [P, small.shape[1]])
        ident = sm[:, 0:128]
        tri_f = sm[:, 128:256]
        iota32 = sm[:, 256:288]
        e_base = sm[:, 288:320]
        corr = sm[:, 320:384].rearrange("p (g c) -> p g c", g=H)
        ranks = sm[:, 384:384 + RANKS]
        tri = sb("tri", [P, P], BF16)
        ones = sb("ones", [P, P], BF16)
        wp_sb = sb("wp_sb", [P, H, P])
        wr_sb = sb("wr_sb", [P, KD, E])
        br_sb = sb("br_sb", [P, E])
        rw_sb = sb("rw_sb", [P, W])
        bguT = sb("bguT", [P, E, NF])
        nm_w = sb("nm_w", [P, KD])
        nf_w = sb("nf_w", [P, KD])
        ps_w = sb("ps_w", [P, H])
        eps_t = sb("eps_t", [P, 1])
        ss = sb("ss", [P, 16, 4])
        var = sb("var", [P, 16, 4])
        std = sb("std", [P, 16, 4])
        rstd = sb("rstd", [P, 16, 4])
        nwt = sb("nwt", [P, 4])
        logit = sb("logit", [P, NT, E])
        top8 = sb("top8", [P, NT, 8])
        idx8 = sb("idx8", [P, NT, 8], U32)
        idxf = sb("idxf", [P, NT, 8])
        negmax = sb("negmax", [P, NT])
        expo = sb("expo", [P, NT, TOP_K])
        esum = sb("esum", [P, NT])
        einv = sb("einv", [P, NT])
        gates = sb("gates", [P, NT, TOP_K])
        chosen = sb("chosen", [P, NT, E])
        chosen_b = sb("chosen_b", [P, NT, E], BF16)
        rank1 = sb("rank1", [P, E, NT])
        rank_row = sb("rank_row", [P, NT, E])
        pick = sb("pick", [P, E])
        passed_b = sb("passed_b", [P, NT, E])
        row_f = sb("row_f", [P, NT * TOP_K])
        row_u = sb("row_u", [P, NT * TOP_K], U32)
        gdense = sb("gdense", [P, NT, E])
        gtmp = sb("gtmp", [P, E])
        count_i = sb("count_i", [P, E], I32)
        count_max = sb("count_max", [P, 1])
        count_max_i = sb("count_max_i", [P, 1], I32)

        ps = ctx.enter_context(nc.psum_tensor("ps", [P, 8, 512], F32))

        wide = [("z", n) for n in range(16)]
        for h in range(H):
            wide += [("pv", h), ("z", 16 + h)]
        wide += [("pool", g) for g in range(H)] + [("out", m) for m in range(2 * NT)]
        turned = [("bgu", j) for j in range(4)] + [("x", t, i) for t in range(NT) for i in range(2)]
        turned += [("qk", n) for n in range(8)]
        turned += [("s", h, i) for h in range(H) for i in range(NT)]
        turned += [("mix", h) for h in range(H)]
        for t in range(NT - 1):
            turned += [("h2", t, 0), ("h2", t, 1), ("log", t, 0), ("log", t, 1)]
        turned += [("h2", 3, 0), ("h2", 3, 1), ("log", 3, 0), ("pos", 0)]
        bank_of, turn_of = {}, {}
        for first, order in ((0, wide), (4, turned)):
            for n, key in enumerate(order):
                bank_of[key], turn_of[key] = first + n % 4, n // 4
        empty = {key for key in turned if key[0] == "log" and key[2] == 1}
        uses = [0] * 8
        for key in wide + turned:
            if key not in empty:
                turn_of[key] = uses[bank_of[key]]
                uses[bank_of[key]] += 1
        bank_free = [sem(f"bank_free{b}") for b in range(8)]

        def bank(key):
            return ps[:, bank_of[key], :]

        def take(pe, key):
            if turn_of[key]:
                pe.wait_ge(bank_free[bank_of[key]], turn_of[key])

        def emptied(eng, key):
            eng.wait_ge(bank_free[bank_of[key]], turn_of[key] + 1)

        def free(ins, key):
            ins.then_inc(bank_free[bank_of[key]], 1)

        x_loaded = [sem(f"x_loaded{t}") for t in range(NT)]
        win_loaded = [sem(f"win_loaded{c}") for c in range(5)]
        wout_loaded = [sem(f"wout_loaded{c}") for c in range(2)]
        small_loaded = sem("small_loaded")
        rope_loaded = sem("rope_loaded")
        dec_loaded = sem("dec_loaded")
        norms_loaded = sem("norms_loaded")
        wpool_loaded = sem("wpool_loaded")
        router_loaded = sem("router_loaded")
        bgu_loaded = sem("bgu_loaded")
        rw_loaded = sem("rw_loaded")
        consts_made = sem("consts_made")
        bgu_turned = sem("bgu_turned")
        ss_ready = sem("ss_ready")
        std_ready = sem("std_ready")
        xn_ready = sem("xn_ready")
        x_turned = sem("x_turned")
        hT_ready = sem("hT_ready")
        z_done = sem("z_done")
        rot_ready = sem("rot_ready")
        qk_turned = sem("qk_turned")
        sig_gate = sem("sig_gate")
        silu_ready = sem("silu_ready")
        gate_ready = sem("gate_ready")
        pad_ready = sem("pad_ready")
        scores_done = sem("scores_done")
        sT_ready = sem("sT_ready")
        pv_done = sem("pv_done")
        mixtok_ready = sem("mixtok_ready")
        mix_turned = sem("mix_turned")
        pool_step = sem("pool_step")
        window_ready = sem("window_ready")
        pooled_ready = sem("pooled_ready")
        pool_done = sem("pool_done")
        out_done = sem("out_done")
        x2_ready = sem("x2_ready")
        xn2_ready = sem("xn2_ready")
        hi_ready = sem("hi_ready")
        rest_ready = sem("rest_ready")
        mid_ready = sem("mid_ready")
        parts_ready = sem("parts_ready")
        h2_turned = sem("h2_turned")
        h2T_ready = sem("h2T_ready")
        logits_done = sem("logits_done")
        top_ready = sem("top_ready")
        exp_ready = sem("exp_ready")
        chosen_ready = sem("chosen_ready")
        pos_done = sem("pos_done")
        dve_step = sem("dve_step")
        routed = sem("routed")
        counts_ready = sem("counts_ready")
        slot_loaded = [sem(f"slot_loaded{s}") for s in range(CH)]
        chunk_used = sem("chunk_used")
        onehot_ready = sem("onehot_ready")
        gathered = sem("gathered")
        xT_ready = sem("xT_ready")
        gu_done = sem("gu_done")
        gu_taken = sem("gu_taken")
        glu_ready = sem("glu_ready")
        lin_ready = sem("lin_ready")
        prod_ready = sem("prod_ready")
        sig_ready = sem("sig_ready")
        act_ready = sem("act_ready")
        y_done = sem("y_done")
        yT_ready = sem("yT_ready")
        row_turned = sem("row_turned")
        row_ready = sem("row_ready")
        rows_stored = sem("rows_stored")
        more = {k: sem(f"more_{k}") for k in ("weights", "onehot", "gathered", "xT", "gu", "biased", "glu",
                                              "prod", "sig", "act", "y", "yT", "turned", "row", "stored")}
        passed = sem("passed")
        zeros_ready = sem("zeros_ready")
        cleared = sem("cleared")
        tail_loaded = sem("tail_loaded")
        gd_turned = sem("gd_turned")
        gdT_ready = sem("gdT_ready")
        bias_done = sem("bias_done")
        got_rows = [sem(f"got_rows{t}") for t in range(NT)]
        acc_ready = sem("acc_ready")
        out_ready = sem("out_ready")
        out_stored = sem("out_stored")

        xt_d = x[0].rearrange("(t p) d -> p t d", p=P)
        out_d = out[0].rearrange("(t p) d -> p t d", p=P)
        win_cols = [0, 1, 3, 2, 4]

        def win(c):
            return ring[:, 2 * c:2 * c + 2, :].rearrange("p s c -> p (s c)").rearrange("p (k c) -> p k c", k=KD)

        def wout(k):
            j = (k + 4) % 8
            return ring[:, 4 + j // 2, (j % 2) * D:(j % 2 + 1) * D]

        def load_chunk(sp, s, e):
            if s < GU_CH:
                src = w_gu[0, bass.ds(e, 1), s * P:(s + 1) * P, :].rearrange("a p c -> (a p) c")
                return sp.dma_start(ring[:, s, :], src)
            r = (s - GU_CH) * 2 * P
            src = w_down[0, bass.ds(e, 1), r:r + 2 * P, :].rearrange("a (j p) c -> p (a j) c", p=P)
            return sp.dma_start(ring[:, s, :].rearrange("p (j c) -> p j c", j=2), src)

        MISC = ps[:, 6:8, :]
        GU = ps[:, 0:4, 0:PER * CAP]
        YT = ps[:, 4:6, 0:4 * CAP]

        def pe_gather(pe):
            for d in range(KD):
                o = MISC[:, d // 4, (d % 4) * CAP:(d % 4 + 1) * CAP]
                for i in range(3):
                    for t in range(NT):
                        mm = pe.matmul(o, parts[:, i, t, d * P:(d + 1) * P], onehot[:, t, :],
                                       start=(i == 0 and t == 0), stop=(i == 2 and t == NT - 1),
                                       skip_group_check=True)
            return mm

        def gu_tile(b, j):
            return 2 * b + j if j < 2 else NF // 2 + 2 * b + j - 2

        def pe_gu(pe, k, b):
            for j in range(PER):
                f = gu_tile(b, j)
                mm = pe.matmul(GU[:, b, j * CAP:(j + 1) * CAP], ring[:, k, f * P:(f + 1) * P], xT[:, k, :],
                               start=(k == 0 and j == 0), stop=(k == KD - 1), skip_group_check=True)
            return mm

        def pe_down(pe, f):
            for d in range(KD):
                w = ring[:, GU_CH + f // 2, (f % 2) * D + d * P:(f % 2) * D + (d + 1) * P]
                mm = pe.matmul(YT[:, d // 4, (d % 4) * CAP:(d % 4 + 1) * CAP], w, actT[:, f, :],
                               start=(f == 0 and d % 4 == 0), stop=(f == KD - 1), skip_group_check=True)
            return mm

        def pe_turn_rows(pe):
            for d in range(KD):
                mm = pe.transpose(MISC[0:CAP, d // 4, (d % 4) * P:(d % 4 + 1) * P], yT[:, d, :], ident)
            return mm

        def dve_onehot(dve, e, first_rank):
            return dve.tensor_tensor(
                onehot, ranks[:, bass.ds(first_rank, CAP)].unsqueeze(1).to_broadcast([P, NT, CAP]),
                rank1[:, bass.ds(e, 1), :].rearrange("p a t -> p (a t)").unsqueeze(2).to_broadcast([P, NT, CAP]),
                ALU.is_equal)

        def dve_xT(dve):
            return dve.tensor_tensor(
                xT.rearrange("p (a k) c -> p a k c", a=2), MISC[:, :, 0:4 * CAP].rearrange("p a (k c) -> p a k c", k=4),
                nf_w[:, :].rearrange("p (a k) -> p a k", a=2).unsqueeze(3).to_broadcast([P, 2, 4, CAP]), ALU.mult)

        def dve_bias(dve, e, b):
            return dve.tensor_tensor(
                gub[:, b % 2].rearrange("p h (j c) -> p (h j) c", j=2),
                GU[:, b, :].rearrange("p (j c) -> p j c", j=PER),
                bguT[:, bass.ds(e, 1), PER * b:PER * b + PER].rearrange("p a j -> p (a j)").unsqueeze(2)
                .to_broadcast([P, PER, CAP]), ALU.add)

        def dve_glu(dve, b):
            return dve.tensor_scalar(gub[:, b % 2, 0], gub[:, b % 2, 0], LIMIT, None, ALU.min)

        def dve_lin(dve, b):
            return dve.tensor_scalar(gub[:, b % 2, 1], gub[:, b % 2, 1], LIMIT, -LIMIT, ALU.min, ALU.max)

        def dve_prod(dve, b):
            return dve.scalar_tensor_tensor(prod[:, b % 2], gub[:, b % 2, 1], 1.0, gub[:, b % 2, 0],
                                            ALU.add, ALU.mult)

        def dve_act(dve, b):
            return dve.tensor_tensor(actT[:, 2 * b:2 * b + 2, :].rearrange("p j c -> p (j c)"),
                                     prod[:, b % 2], sig[:, b % 2], ALU.mult)

        def act_sig(act, b):
            return act.activation(sig[:, b % 2], gub[:, b % 2, 0], ACT.Sigmoid, scale=ALPHA)

        def act_yT(act, half):
            return act.activation(yT[:, 4 * half:4 * half + 4, :].rearrange("p k c -> p (k c)"),
                                  YT[:, half, :], ACT.Copy)

        def act_row(act, half):
            return act.activation(y_row[0:CAP, half * 512:(half + 1) * 512], MISC[0:CAP, half, :], ACT.Copy)

        def store_rows(act, row):
            return act.dma_start(y_rows[bass.ds(row, CAP), :], y_row[0:CAP, :])

        def further_blocks(eng, load, block, skip_expert, skip_block, setup=None):
            most = eng.value_load(count_max_i[0:1, 0:1], min_val=0, max_val=S)
            with eng.If(most > CAP):
                if setup:
                    setup()
                with eng.Fori(0, E) as e:
                    c = eng.value_load(count_i[0:1, bass.ds(e, 1)], min_val=0, max_val=S)
                    with eng.If(c > CAP):
                        load(e)
                        eng.sem_inc(passed, 1)
                    with eng.Else():
                        skip_expert()
                    eng.nop()
                    with eng.Fori(1, BLOCKS) as b:
                        with eng.If(c > b * CAP):
                            block(e, b, e * (BLOCKS - 1) + b)
                            eng.sem_inc(passed, 1)
                        with eng.Else():
                            skip_block()
                        eng.nop()
                    eng.nop()
                eng.nop()
            with eng.Else():
                eng.nop()
            eng.nop()
            return most

        block = ctx.enter_context(nc.Block())

        @block.sync
        def _(sp):
            for t in range(NT):
                sp.dma_start(x_sb[:, t, :], xt_d[:, t, :]).then_inc(x_loaded[t], 16)
            for c in range(5):
                src = w_in[0, :, win_cols[c] * W:(win_cols[c] + 1) * W].rearrange("(k p) c -> p k c", p=P)
                sp.dma_start(win(c), src).then_inc(win_loaded[c], 16)

            def expert0(slots):
                for s in slots:
                    load_chunk(sp, s, 0).then_inc(slot_loaded[s], 16)

            sp.wait_ge(z_done, 4)
            expert0((0, 1))
            sp.wait_ge(z_done, 8)
            expert0((2, 3))
            sp.wait_ge(z_done, 12)
            sp.dma_start(ring[:, 4:6, :].rearrange("p s (a c) -> p (s a) c", a=2),
                         w_out[0, W:2 * W, :].rearrange("(k p) c -> p k c", p=P)).then_inc(wout_loaded[1], 16)
            sp.wait_ge(z_done, 16)
            sp.dma_start(ring[:, 6:8, :].rearrange("p s (a c) -> p (s a) c", a=2),
                         w_out[0, 0:W, :].rearrange("(k p) c -> p k c", p=P)).then_inc(wout_loaded[0], 16)
            sp.wait_ge(scores_done, 16)
            expert0((10, 11))
            sp.wait_ge(z_done, 20)
            expert0((8, 9))
            sp.wait_ge(out_done, 8)
            expert0((4, 5, 6, 7))
            with sp.Fori(1, E) as e:
                for s in range(CH):
                    if s < CH - 1:
                        sp.wait_ge(chunk_used, (CH - 1) * (e - 1) + s + 1)
                    else:
                        sp.wait_ge(y_done, e)
                    load_chunk(sp, s, e).then_inc(slot_loaded[s], 16)

            sp.wait_ge(counts_ready, 1)
            def load(e):
                sp.wait_ge(y_done, E)
                for s in range(CH):
                    load_chunk(sp, s, e).then_inc(more["weights"], 16)

            def one(e, b, n):
                sp.wait_ge(more["stored"], 16 * n)

            def clear():
                sp.wait_ge(zeros_ready, 1)
                sp.dma_start(y_rows[FIRST:BLOCKS * FIRST, :].rearrange("(n p) d -> p n d", p=P),
                             zeros.unsqueeze(1).to_broadcast([P, (BLOCKS - 1) * FIRST // P, D])).then_inc(cleared, 16)

            further_blocks(sp, load, one, lambda: sp.sem_inc(more["weights"], 16 * CH), lambda: sp.nop(), clear)

            for t in range(NT):
                sp.wait_ge(out_ready, t + 1)
                sp.dma_start(out_d[:, t, :], o_row[:, t, :]).then_inc(out_stored, 16)
            sp.wait_ge(out_stored, 16 * NT)

        @block.gpsimd
        def _(pool):
            pool.memset(ones[:, :], 1.0).then_inc(consts_made, 1)
            pool.memset(pT[:, :, 0:PADS], 0.0).then_inc(pad_ready, 1)
            pool.wait_ge(rw_loaded, 16)
            for t in range(NT):
                pool.wait_ge(silu_ready, t + 1)
                pool.tensor_tensor(gate_sb[:, t, :], gate_sb[:, t, :], rw_sb[:, :], ALU.mult).then_inc(gate_ready, 1)
            step = 0
            pool.wait_ge(pad_ready, 1)
            for n, g in enumerate(reversed(range(H))):
                emptied(pool, ("z", 16 + n))
                src = pT[:, g, :]
                if n:
                    pool.wait_ge(pooled_ready, n)
                w = 1
                while w < WINDOWS[g]:
                    dst = psum_a if src is not psum_a else psum_b
                    pool.tensor_tensor(dst[:, w:PADS + S], src[:, w:PADS + S], src[:, 0:PADS + S - w], ALU.add)\
                        .then_inc(pool_step, 1)
                    pool.memset(dst[:, 0:w], 0.0).then_inc(pool_step, 1)
                    step += 2
                    pool.wait_ge(pool_step, step)
                    src = dst
                    w *= 2
                pool.tensor_tensor(src[:, PADS:2 * PADS], src[:, PADS:2 * PADS], corr[:, g, :], ALU.mult)\
                    .then_inc(window_ready, 1)

            pool.wait_ge(counts_ready, 1)
            def make_zeros():
                pool.wait_ge(parts_ready, NT)
                pool.memset(zeros, 0.0).then_inc(zeros_ready, 1)

            most = further_blocks(pool, lambda e: pool.nop(), lambda e, b, n: pool.wait_ge(more["stored"], 16 * n),
                                  lambda: pool.nop(), lambda: pool.nop(), make_zeros)
            pool.wait_ge(routed, 1)
            pool.wait_ge(rows_stored, 16 * E)
            pool.wait_ge(y_done, E)

            def fetch(rows):
                for t in range(NT):
                    for k in range(TOP_K):
                        n = t * TOP_K + k
                        pool.indirect_dma_start(
                            out=got[:, n, :], out_offset=None, in_=rows,
                            in_offset=bass.IndirectOffsetOnAxis(ap=row_u[:, n:n + 1], axis=0))\
                            .then_inc(got_rows[t], 16)

            with pool.If(most > CAP):
                fetch(y_rows)
            with pool.Else():
                fetch(y_rows[0:FIRST, :])
            pool.nop()

        @block.scalar
        def _(act):
            act.dma_start(sm[:, :], small).then_inc(small_loaded, 16)
            with nc.allow_non_contiguous_dma(reason="1024 weights, one on each partition and tile"):
                act.dma_start(nm_w[:, :], norm_mix_w[0].rearrange("(k p) -> p k", p=P)).then_inc(norms_loaded, 16)
                act.dma_start(nf_w[:, :], norm_ffn_w[0].rearrange("(k p) -> p k", p=P)).then_inc(norms_loaded, 16)
                act.dma_start(ps_w[:, :], pool_scale[0].rearrange("(g p) -> p g", p=P)).then_inc(norms_loaded, 16)
            act.dma_start(bgu_raw[:, :], b_gu[0].rearrange("e (q c) -> (e q) c", q=4)).then_inc(bgu_loaded, 16)
            act.dma_start(reg_r[:, 0:1024], rope).then_inc(rope_loaded, 16)
            act.dma_start(reg_d, decay).then_inc(dec_loaded, 16)
            act.dma_start(rw_sb[:, :], ret_norm_w[0:1, :].to_broadcast([P, W])).then_inc(rw_loaded, 16)
            act.dma_start(wp_sb[:, :, :], w_pool[0].rearrange("g c d -> c g d")).then_inc(wpool_loaded, 16)
            act.dma_start(wr_sb[:, :, :], w_router[0].rearrange("(k p) e -> p k e", p=P)).then_inc(router_loaded, 16)
            act.dma_start(br_sb[:, :], b_router[0:1, :].to_broadcast([P, E])).then_inc(router_loaded, 16)

            norms = [0]

            def root(width, n):
                r = norms[0]
                norms[0] += 1
                act.wait_ge(ss_ready, r + 1)
                act.activation(std[:, r, 0:width], ss[:, r, 0:width], ACT.Sqrt, bias=eps_t[:, :], scale=1.0 / n)\
                    .then_inc(std_ready, 1)

            act.wait_ge(consts_made, 3)
            for t in range(NT):
                act.wait_ge(x_loaded[t], 16)
                if t >= 2:
                    act.wait_ge(x_turned, t - 1)
                act.activation(xn1[:, t % 2], x_sb[:, t, :], ACT.Square, accum_out=ss[:, t, 0:1]).then_inc(ss_ready, 1)
                root(1, D)

            def qk(n):
                act.wait_ge(qk_turned, n + 1)
                dst = (qT if n < 4 else kT)[:, :, (n % 4) * P:(n % 4 + 1) * P]
                ins = act.activation(dst, bank(("qk", n)).rearrange("p (h c) -> p h c", h=H), ACT.Copy)
                free(ins, ("qk", n))

            def gate_sig(t):
                act.wait_ge(z_done, 8 + t + 1)
                act.activation(gate_sb[:, t, :], bank(("z", 8 + t)), ACT.Sigmoid).then_inc(sig_gate, 1)

            for n in range(6):
                qk(n)
            gate_sig(0)
            qk(6)
            gate_sig(1)
            qk(7)
            gate_sig(2)
            gate_sig(3)
            for t in range(NT):
                act.wait_ge(z_done, 12 + t + 1)
                ins = act.activation(v_sb[:, t, :], bank(("z", 12 + t)), ACT.Copy)
                free(ins, ("z", 12 + t))
            for h in range(H):
                act.wait_ge(pv_done, h + 1)
                for j in range(NT):
                    ins = act.activation(mixtok[:, h, j * P:(j + 1) * P], bank(("pv", h))[:, j * P:(j + 1) * P],
                                         ACT.Square, accum_out=ss[:, 4 + h, j:j + 1])
                ins.then_inc(ss_ready, 1)
                root(NT, P)
                act.wait_ge(z_done, 16 + h + 1)
                act.wait_ge(pad_ready, 1)
                ins = act.activation(pT[:, H - 1 - h, PADS:PADS + S], bank(("z", 16 + h)), ACT.Copy)
                free(ins, ("z", 16 + h))
            for h in range(H):
                act.wait_ge(mix_turned, h + 1)
                act.wait_ge(z_done, 20)
                ins = act.activation(mixT[:, h, :], bank(("mix", h)), ACT.Copy)
                free(ins, ("mix", h))
            act.wait_ge(norms_loaded, 48)
            for n, g in enumerate(reversed(range(H))):
                act.wait_ge(pool_done, n + 1)
                ins = act.activation(mixT[:, H + g, :], bank(("pool", n)), ACT.Copy, scale=ps_w[:, g:g + 1])
                free(ins, ("pool", n))

            def norm2(t):
                act.wait_ge(x2_ready, t + 1)
                if t >= 2:
                    act.wait_ge(h2_turned, t - 1)
                    act.wait_ge(rest_ready, t - 1)
                act.activation(xn2[:, t % 2], x_sb[:, t, :], ACT.Square, accum_out=ss[:, 8 + t, 0:1])\
                    .then_inc(ss_ready, 1)
                root(1, D)

            def high_parts(t):
                act.wait_ge(xn2_ready, t + 1)
                act.activation(parts[:, 0, t, :], xn2[:, t % 2], ACT.Copy).then_inc(hi_ready, 1)
                act.wait_ge(rest_ready, t + 1)
                act.activation(parts[:, 1, t, :], rest, ACT.Copy).then_inc(mid_ready, 1)

            def exps(t):
                act.wait_ge(top_ready, t + 1)
                act.activation(expo[:, t, :], top8[:, t, 0:TOP_K], ACT.Exp, bias=negmax[:, t:t + 1],
                               accum_out=esum[:, t:t + 1]).then_inc(exp_ready, 1)

            for t in range(NT):
                norm2(t)
                high_parts(t)
            for t in range(NT):
                exps(t)

            def finish_rows(e_before):
                act.wait_ge(y_done, e_before + 1)
                for half in range(2):
                    act_yT(act, half).then_inc(yT_ready, 1)
                act.wait_ge(row_turned, e_before + 1)
                for half in range(2):
                    act_row(act, half).then_inc(row_ready, 1)
                act.wait_ge(row_ready, 2 * e_before + 2)
                store_rows(act, e_before * CAP).then_inc(rows_stored, 16)

            def sigs(e, first=False):
                for b in range(GB):
                    act.wait_ge(glu_ready, GB * e + b + 1)
                    if b >= 2 or not first:
                        act.wait_ge(act_ready, GB * e + b - 1)
                    act_sig(act, b).then_inc(sig_ready, 1)

            sigs(0, first=True)
            finish_rows(0)
            with act.Fori(1, E) as e:
                sigs(e)
                act.wait_ge(rows_stored, 16 * e)
                finish_rows(e)

            act.wait_ge(counts_ready, 1)
            act.wait_ge(rows_stored, 16 * E)

            def one(e, b, n):
                for i in range(GB):
                    act.wait_ge(more["glu"], GB * n - GB + i + 1)
                    act_sig(act, i).then_inc(more["sig"], 1)
                act.wait_ge(more["y"], n)
                for half in range(2):
                    act_yT(act, half).then_inc(more["yT"], 1)
                act.wait_ge(more["turned"], n)
                for half in range(2):
                    act_row(act, half).then_inc(more["row"], 1)
                act.wait_ge(more["row"], 2 * n)
                act.wait_ge(cleared, 16)
                store_rows(act, b * FIRST + e * CAP).then_inc(more["stored"], 16)
                act.wait_ge(more["stored"], 16 * n)

            def skip():
                act.sem_inc(more["sig"], GB)
                act.sem_inc(more["yT"], 2)
                act.sem_inc(more["row"], 2)
                act.sem_inc(more["stored"], 16)

            further_blocks(act, lambda e: act.nop(), one, lambda: act.nop(), skip)

            act.wait_ge(act_ready, GB * E)
            act.wait_ge(y_done, E)
            act.wait_ge(row_turned, E)
            act.dma_start(fin_w, norm_final_w.rearrange("(a d) -> a d", a=1).to_broadcast([P, D])).then_inc(tail_loaded, 16)
            act.dma_start(bd_sb, b_down[0]).then_inc(tail_loaded, 16)
            act.wait_ge(gd_turned, 1)
            ins = act.activation(gdT, ps[0:E, 4, :], ACT.Copy).then_inc(gdT_ready, 1)
            for t in range(NT):
                act.wait_ge(acc_ready, t + 1)
                act.activation(o_row[:, t, :], x_sb[:, t, :], ACT.Square, accum_out=ss[:, 12 + t, 0:1])\
                    .then_inc(ss_ready, 1)
                root(1, D)

        @block.tensor
        def _(pe):
            pe.wait_ge(small_loaded, 16)
            pe.wait_ge(bgu_loaded, 16)
            for j in range(4):
                take(pe, ("bgu", j))
                pe.transpose(bank(("bgu", j))[:, 0:P], bgu_raw[:, j * P:(j + 1) * P], ident).then_inc(bgu_turned, 1)
            for t in range(NT):
                pe.wait_ge(xn_ready, t + 1)
                for k in range(KD):
                    if k % 4 == 0:
                        take(pe, ("x", t, k // 4))
                    mm = pe.transpose(bank(("x", t, k // 4))[:, (k % 4) * P:(k % 4 + 1) * P],
                                      xn1[:, t % 2, k * P:(k + 1) * P], ident)
                mm.then_inc(x_turned, 1)

            def z(n):
                c = min(n // 4, 4)
                pe.wait_ge(win_loaded[c], 16)
                if n < 4:
                    pe.wait_ge(hT_ready, n + 1)
                take(pe, ("z", n))
                for k in range(KD):
                    if c < 4:
                        lhsT, rhs = hT[:, k, (n % 4) * P:(n % 4 + 1) * P], win(c)[:, k, :]
                    else:
                        g = H - 1 - (n - 16)
                        lhsT, rhs = win(4)[:, k, g * P:(g + 1) * P], hT[:, k, :]
                    mm = pe.matmul(bank(("z", n)), lhsT, rhs, start=(k == 0), stop=(k == KD - 1))
                mm.then_inc(z_done, 1)

            def turn_qk(n):
                pe.wait_ge(rot_ready, n + 1)
                take(pe, ("qk", n))
                for h in range(H):
                    mm = pe.transpose(bank(("qk", n))[:, h * P:(h + 1) * P], rot[:, n % 2, h * P:(h + 1) * P], ident)
                mm.then_inc(qk_turned, 1)

            def scores(h):
                for i in range(NT):
                    take(pe, ("s", h, i))
                    emptied(pe, ("qk", 7))
                    emptied(pe, ("qk", 6))
                    pe.matmul(bank(("s", h, i))[:, 0:S - i * P], kT[:, h, i * P:(i + 1) * P], qT[:, h, i * P:S],
                              start=True, stop=True).then_inc(scores_done, 1)

            def pv(h):
                pe.wait_ge(sT_ready, NT * (h + 1))
                for t in range(NT):
                    emptied(pe, ("z", 12 + t))
                take(pe, ("pv", h))
                for j in range(NT):
                    for i in range(j + 1):
                        off = 4 * i - i * (i - 1) // 2
                        mm = pe.matmul(bank(("pv", h))[:, j * P:(j + 1) * P],
                                       sT[:, h % 2, (off + j - i) * P:(off + j - i + 1) * P],
                                       v_sb[:, i, h * P:(h + 1) * P], start=(i == 0), stop=(i == j))
                mm.then_inc(pv_done, 1)

            for n in range(8):
                z(n)
                if n >= 2:
                    turn_qk(n - 2)
            z(8)
            turn_qk(6)
            z(9)
            turn_qk(7)
            z(10)
            pe.wait_ge(dec_loaded, 16)
            scores(0)
            z(11)
            scores(1)
            for n in range(12, 16):
                z(n)
            for h in range(H):
                pv(h)
                if h < 2:
                    scores(h + 2)
                z(16 + h)
            for h in range(H):
                pe.wait_ge(mixtok_ready, h + 1)
                take(pe, ("mix", h))
                for j in range(NT):
                    mm = pe.transpose(bank(("mix", h))[:, j * P:(j + 1) * P], mixtok[:, h, j * P:(j + 1) * P], ident)
                mm.then_inc(mix_turned, 1)
            pe.wait_ge(wpool_loaded, 16)
            for n, g in enumerate(reversed(range(H))):
                pe.wait_ge(pooled_ready, n + 1)
                take(pe, ("pool", n))
                pe.matmul(bank(("pool", n)), wp_sb[:, g, :], pT[:, g, PADS:PADS + S], start=True, stop=True)\
                    .then_inc(pool_done, 1)

            for h in range(H):
                emptied(pe, ("mix", h))
            for c in range(2):
                pe.wait_ge(wout_loaded[c], 16)

            def project(m):
                t, half = m // 2, m % 2
                take(pe, ("out", m))
                for k in range(KD):
                    if m == 0 and k == H:
                        for n in range(H):
                            emptied(pe, ("pool", n))
                    mm = pe.matmul(bank(("out", m)), mixT[:, k, t * P:(t + 1) * P],
                                   wout(k)[:, half * 512:(half + 1) * 512], start=(k == 0), stop=(k == KD - 1))
                mm.then_inc(out_done, 1)

            def turn_h2(t):
                pe.wait_ge(xn2_ready, t + 1)
                for k in range(KD):
                    if k % 4 == 0:
                        take(pe, ("h2", t, k // 4))
                    mm = pe.transpose(bank(("h2", t, k // 4))[:, (k % 4) * P:(k % 4 + 1) * P],
                                      xn2[:, t % 2, k * P:(k + 1) * P], ident)
                mm.then_inc(h2_turned, 1)

            def route(t):
                pe.wait_ge(h2T_ready, t + 1)
                pe.wait_ge(router_loaded, 32)
                take(pe, ("log", t, 0))
                for k in range(KD):
                    mm = pe.matmul(bank(("log", t, 0))[:, 0:E], h2T[:, t % 2, k, :], wr_sb[:, k, :],
                                   start=(k == 0), stop=(k == KD - 1))
                mm.then_inc(logits_done, 1)

            for t in range(NT):
                project(2 * t)
                project(2 * t + 1)
                if t >= 1:
                    turn_h2(t - 1)
                    route(t - 1)
            turn_h2(3)
            route(3)
            take(pe, ("pos", 0))
            pe.wait_ge(consts_made, 3)
            pe.wait_ge(chosen_ready, NT)
            pos = bank(("pos", 0))
            for t in range(NT + 1):
                for i in range(min(t + 1, NT)):
                    mm = pe.matmul(pos[:, t * E:(t + 1) * E], (tri if i == t else ones)[:, :], chosen_b[:, i, :],
                                   start=(i == 0), stop=(i == min(t, NT - 1)))
            mm.then_inc(pos_done, 1)

            def gather(e):
                pe.wait_ge(onehot_ready, e + 1)
                pe_gather(pe).then_inc(gathered, 1)

            for b in range(8):
                pe.wait_ge(bank_free[b], uses[b])
            pe.wait_ge(parts_ready, NT)
            gather(0)

            def turn_rows(e):
                pe.wait_ge(yT_ready, 2 * e + 2)
                pe_turn_rows(pe).then_inc(row_turned, 1)

            def expert(e, first=False, last=False):
                pe.wait_ge(xT_ready, e + 1)
                if not first:
                    pe.wait_ge(gu_taken, GB * e)
                for k in range(KD):
                    pe.wait_ge(slot_loaded[k], 16 * e + 16)
                    for b in range(GB):
                        mm = pe_gu(pe, k, b)
                        if k == KD - 1:
                            mm.then_inc(gu_done, 1)
                    if k < KD - 1:
                        mm.then_inc(chunk_used, 1)
                    if k == 1 and not first:
                        turn_rows(e - 1)
                if not last:
                    if not first:
                        pe.wait_ge(row_ready, 2 * e)
                    gather(e + 1)
                for f in range(KD):
                    if f % 2 == 0:
                        pe.wait_ge(act_ready, GB * e + f // 2 + 1)
                        pe.wait_ge(slot_loaded[GU_CH + f // 2], 16 * e + 16)
                        if f == 0 and not first:
                            pe.wait_ge(yT_ready, 2 * e)
                    mm = pe_down(pe, f)
                    if f == 0 or (f % 2 == 1 and f < KD - 1):
                        mm.then_inc(chunk_used, 1)
                    elif f == KD - 1:
                        mm.then_inc(y_done, 1)

            expert(0, first=True)
            with pe.Fori(1, E - 1) as e:
                expert(e)
            expert(E - 1, last=True)
            turn_rows(E - 1)

            pe.wait_ge(counts_ready, 1)
            pe.wait_ge(rows_stored, 16 * E)

            def load(e):
                pe.wait_ge(more["weights"], 16 * CH * (e + 1))

            def one(e, b, n):
                pe.wait_ge(more["onehot"], n)
                pe_gather(pe).then_inc(more["gathered"], 1)
                pe.wait_ge(more["xT"], n)
                for k in range(KD):
                    for i in range(GB):
                        mm = pe_gu(pe, k, i)
                mm.then_inc(more["gu"], 1)
                pe.wait_ge(more["act"], GB * n)
                for f in range(KD):
                    mm = pe_down(pe, f)
                mm.then_inc(more["y"], 1)
                pe.wait_ge(more["yT"], 2 * n)
                pe_turn_rows(pe).then_inc(more["turned"], 1)
                pe.wait_ge(more["stored"], 16 * n)

            def skip():
                for k in ("gathered", "gu", "y", "turned"):
                    pe.sem_inc(more[k], 1)

            further_blocks(pe, load, one, lambda: pe.nop(), skip)

            pe.wait_ge(routed, 1)
            pe.wait_ge(row_ready, 2 * E)
            for t in range(NT):
                mm = pe.transpose(ps[0:E, 4, t * P:(t + 1) * P], gdense[:, t, :], ident)
            mm.then_inc(gd_turned, 1)
            pe.wait_ge(gdT_ready, 1)
            pe.wait_ge(tail_loaded, 32)
            order = [0, 1, 2, 3, 5, 6, 7, 4]
            for m in range(2 * NT):
                t, half = m // 2, m % 2
                pe.matmul(ps[:, order[m], :], gdT[:, t * P:(t + 1) * P], bd_sb[:, half * 512:(half + 1) * 512],
                          start=True, stop=True).then_inc(bias_done, 1)

        @block.vector
        def _(dve):
            steps = [0]

            def step(ins):
                ins.then_inc(dve_step, 1)
                steps[0] += 1
                dve.wait_ge(dve_step, steps[0])

            def inverse_root(r, width, n):
                dve.wait_ge(ss_ready, r + 1)
                v, y, w = var[:, r, 0:width], rstd[:, r, 0:width], nwt[:, 0:width]
                step(dve.tensor_scalar(v, ss[:, r, 0:width], 1.0 / n, EPS, ALU.mult, ALU.add))
                dve.wait_ge(std_ready, r + 1)
                step(dve.reciprocal(y, std[:, r, 0:width]))
                step(dve.tensor_tensor(w, y, y, ALU.mult))
                step(dve.scalar_tensor_tensor(w, w, -0.5, v, ALU.mult, ALU.mult))
                step(dve.scalar_tensor_tensor(y, w, 1.5, y, ALU.add, ALU.mult))

            dve.memset(eps_t[:, :], EPS).then_inc(consts_made, 1)
            dve.wait_ge(small_loaded, 16)
            dve.tensor_copy(tri[:, :], tri_f).then_inc(consts_made, 1)
            dve.wait_ge(norms_loaded, 48)

            def hT_tile(t):
                dve.wait_ge(x_turned, t + 1)
                for i in range(2):
                    ins = dve.tensor_tensor(
                        hT[:, 4 * i:4 * i + 4, t * P:(t + 1) * P], bank(("x", t, i)).rearrange("p (k c) -> p k c", k=4),
                        nm_w[:, 4 * i:4 * i + 4].unsqueeze(2).to_broadcast([P, 4, P]), ALU.mult)
                    free(ins, ("x", t, i))
                emptied(dve, ("x", t, 0))
                emptied(dve, ("x", t, 1))
                dve.sem_inc(hT_ready, 1)

            for t in range(NT):
                inverse_root(t, 1, D)
                dve.tensor_scalar(xn1[:, t % 2], x_sb[:, t, :], rstd[:, t, 0:1], None, ALU.mult).then_inc(xn_ready, 1)
                if t == 0:
                    for j in range(4):
                        dve.wait_ge(bgu_turned, j + 1)
                        dst = bguT[:, :, :].rearrange("p e (ql b qh r) -> p e qh ql b r", ql=2, b=2, qh=2)[
                            :, :, :, :, j // 2, j % 2]
                        ins = dve.tensor_copy(dst, bank(("bgu", j))[:, 0:P].rearrange(
                            "p (e qh ql) -> p e qh ql", e=E, qh=2))
                        free(ins, ("bgu", j))
                if t >= 1:
                    hT_tile(t - 1)
            hT_tile(NT - 1)

            def rotate(n):
                t = n % 4
                dve.wait_ge(z_done, n + 1)
                if n >= 2:
                    dve.wait_ge(qk_turned, n - 1)
                    dve.wait_ge(rot_ready, n - 1)
                zz = bank(("z", n)).rearrange("p (h c) -> p h c", h=H)
                dst = rot[:, n % 2].rearrange("p (h c) -> p h c", h=H)
                tmp = sT[:, n % 2, 0:512].rearrange("p (h c) -> p h c", h=H)
                cb = rope_c[:, t, :].unsqueeze(1).to_broadcast([P, H, P])
                sb_ = rope_s[:, t, :].unsqueeze(1).to_broadcast([P, H, P])
                dve.tensor_tensor(dst, zz, cb, ALU.mult)
                dve.tensor_tensor(tmp[:, :, 0:64], zz[:, :, 64:128], sb_[:, :, 0:64], ALU.mult)
                ins = dve.tensor_tensor(tmp[:, :, 64:128], zz[:, :, 0:64], sb_[:, :, 64:128], ALU.mult)
                free(ins, ("z", n))
                emptied(dve, ("z", n))
                dve.tensor_tensor(dst, dst, tmp, ALU.add).then_inc(rot_ready, 1)

            def silu(t):
                dve.wait_ge(sig_gate, t + 1)
                ins = dve.tensor_tensor(gate_sb[:, t, :], bank(("z", 8 + t)), gate_sb[:, t, :], ALU.mult)
                free(ins, ("z", 8 + t))
                emptied(dve, ("z", 8 + t))
                dve.sem_inc(silu_ready, 1)

            def decayed(h):
                if h >= 2:
                    dve.wait_ge(pv_done, h - 1)
                off = 0
                for i in range(NT):
                    n = S - i * P
                    dve.wait_ge(scores_done, NT * h + i + 1)
                    ins = dve.tensor_tensor(sT[:, h % 2, off:off + n], bank(("s", h, i))[:, 0:n], dec[:, h, 0:n], ALU.mult)
                    free(ins, ("s", h, i))
                    off += n
                emptied(dve, ("s", h, 3))
                dve.sem_inc(sT_ready, NT)

            def head_norm(h):
                inverse_root(4 + h, NT, P)
                dve.wait_ge(gate_ready, NT)
                for j in range(NT):
                    ins = dve.scalar_tensor_tensor(
                        mixtok[:, h, j * P:(j + 1) * P], bank(("pv", h))[:, j * P:(j + 1) * P], rstd[:, 4 + h, j:j + 1],
                        gate_sb[:, j, h * P:(h + 1) * P], ALU.mult, ALU.mult)
                free(ins, ("pv", h))
                emptied(dve, ("pv", h))
                dve.sem_inc(mixtok_ready, 1)

            dve.wait_ge(rope_loaded, 16)
            for n in range(8):
                rotate(n)
            dve.wait_ge(dec_loaded, 16)
            dve.wait_ge(rot_ready, 8)
            silu(0)
            silu(1)
            silu(2)
            decayed(0)
            silu(3)
            decayed(1)
            head_norm(0)
            decayed(2)
            head_norm(1)
            decayed(3)
            head_norm(2)
            head_norm(3)
            for n, g in enumerate(reversed(range(H))):
                dve.wait_ge(window_ready, n + 1)
                s = psum_a if g % 2 == 0 else psum_b
                dve.scalar_tensor_tensor(pT[:, g, PADS:PADS + S], s[:, PADS:PADS + S], 1.0 / WINDOWS[g],
                                         pT[:, g, PADS:PADS + S], ALU.mult, ALU.subtract).then_inc(pooled_ready, 1)

            def residual(t):
                for half in range(2):
                    m = 2 * t + half
                    dve.wait_ge(out_done, m + 1)
                    xs = x_sb[:, t, half * 512:(half + 1) * 512]
                    ins = dve.tensor_tensor(xs, bank(("out", m)), xs, ALU.add)
                    free(ins, ("out", m))
                for half in range(2):
                    emptied(dve, ("out", 2 * t + half))
                dve.sem_inc(x2_ready, 1)

            def normed(t):
                inverse_root(8 + t, 1, D)
                dve.tensor_scalar(xn2[:, t % 2], x_sb[:, t, :], rstd[:, 8 + t, 0:1], None, ALU.mult)\
                    .then_inc(xn2_ready, 1)

            def low_parts(t):
                dve.wait_ge(hi_ready, t + 1)
                dve.tensor_tensor(rest, xn2[:, t % 2], parts[:, 0, t, :], ALU.subtract).then_inc(rest_ready, 1)
                dve.wait_ge(mid_ready, t + 1)
                dve.tensor_tensor(parts[:, 2, t, :], rest, parts[:, 1, t, :], ALU.subtract).then_inc(parts_ready, 1)
                dve.wait_ge(parts_ready, t + 1)

            def turned_h2(t):
                dve.wait_ge(h2_turned, t + 1)
                if t >= 2:
                    dve.wait_ge(logits_done, t - 1)
                for i in range(2):
                    ins = dve.tensor_tensor(
                        h2T[:, t % 2, 4 * i:4 * i + 4, :], bank(("h2", t, i)).rearrange("p (k c) -> p k c", k=4),
                        nf_w[:, 4 * i:4 * i + 4].unsqueeze(2).to_broadcast([P, 4, P]), ALU.mult)
                    free(ins, ("h2", t, i))
                for i in range(2):
                    emptied(dve, ("h2", t, i))
                dve.sem_inc(h2T_ready, 1)

            def choose(t):
                dve.wait_ge(logits_done, t + 1)
                if t == 0:
                    dve.wait_ge(router_loaded, 32)
                ins = dve.tensor_tensor(logit[:, t, :], bank(("log", t, 0))[:, 0:E], br_sb[:, :], ALU.add)
                free(ins, ("log", t, 0))
                emptied(dve, ("log", t, 0))
                step(dve.max(top8[:, t, :], logit[:, t, :]))
                step(dve.max_index(idx8[:, t, :], top8[:, t, :], logit[:, t, :]))
                step(dve.tensor_copy(idxf[:, t, :], idx8[:, t, :]))
                step(dve.tensor_scalar(chosen[:, t, :], iota32, idxf[:, t, 0:1], None, ALU.is_equal))
                for k in range(1, TOP_K):
                    step(dve.scalar_tensor_tensor(chosen[:, t, :], iota32, idxf[:, t, k:k + 1], chosen[:, t, :],
                                                  ALU.is_equal, ALU.add))
                dve.tensor_copy(chosen_b[:, t, :], chosen[:, t, :]).then_inc(chosen_ready, 1)
                dve.tensor_scalar(negmax[:, t:t + 1], top8[:, t, 0:1], -1.0, None, ALU.mult).then_inc(top_ready, 1)

            for t in range(NT):
                residual(t)
                normed(t)
                low_parts(t)
                if t >= 1:
                    turned_h2(t - 1)
                    choose(t - 1)
            turned_h2(3)
            choose(3)

            dve.wait_ge(pos_done, 1)
            pos = bank(("pos", 0))
            step(dve.scalar_tensor_tensor(rank1[:, :, :].rearrange("p e t -> p t e"),
                                          pos[:, 0:NT * E].rearrange("p (t e) -> p t e", t=NT), 1.0,
                                          chosen[:, :, :], ALU.add, ALU.mult))
            dve_onehot(dve, 0, 0).then_inc(onehot_ready, 1)
            step(dve.tensor_copy(count_i[:, :], pos[:, NT * E:(NT + 1) * E]))
            step(dve.tensor_reduce(count_max[:, :], pos[:, NT * E:(NT + 1) * E], AX_X, ALU.max))
            ins = dve.tensor_copy(count_max_i[:, :], count_max[:, :])
            step(ins)
            ins = dve.tensor_tensor(rank_row[:, :, :], rank1[:, :, :].rearrange("p e t -> p t e"),
                                    e_base.unsqueeze(1).to_broadcast([P, NT, E]), ALU.add)
            free(ins, ("pos", 0))
            emptied(dve, ("pos", 0))
            dve.sem_inc(counts_ready, 1)

            def xT_next(e):
                dve.wait_ge(gathered, e + 1)
                dve_xT(dve).then_inc(xT_ready, 1)

            xT_next(0)

            def rows_and_gates():
                for b in range(1, BLOCKS):
                    step(dve.tensor_scalar(passed_b[:, :, :], rank1[:, :, :].rearrange("p e t -> p t e"),
                                           float(b * CAP), float(FIRST - CAP), ALU.is_gt, ALU.mult))
                    step(dve.tensor_tensor(rank_row[:, :, :], rank_row[:, :, :], passed_b[:, :, :], ALU.add))
                for t in range(NT):
                    for k in range(TOP_K):
                        n = t * TOP_K + k
                        step(dve.scalar_tensor_tensor(pick[:, :], iota32, idxf[:, t, k:k + 1], rank_row[:, t, :],
                                                      ALU.is_equal, ALU.mult, accum_out=row_f[:, n:n + 1]))
                step(dve.tensor_copy(row_u[:, :], row_f[:, :]))
                dve.wait_ge(exp_ready, NT)
                step(dve.reciprocal(einv[:, :], esum[:, :]))
                for t in range(NT):
                    step(dve.tensor_scalar(gates[:, t, :], expo[:, t, :], einv[:, t:t + 1], None, ALU.mult))
                    step(dve.tensor_scalar(gdense[:, t, :], iota32, idxf[:, t, 0:1], gates[:, t, 0:1],
                                           ALU.is_equal, ALU.mult))
                    for k in range(1, TOP_K):
                        step(dve.tensor_scalar(gtmp[:, :], iota32, idxf[:, t, k:k + 1], gates[:, t, k:k + 1],
                                               ALU.is_equal, ALU.mult))
                        step(dve.tensor_tensor(gdense[:, t, :], gdense[:, t, :], gtmp[:, :], ALU.add))
                dve.sem_inc(routed, 1)

            def expert(e, first=False, last=False):
                if not last:
                    dve_onehot(dve, e + 1, 0).then_inc(onehot_ready, 1)
                for b in range(GB + 1):
                    if b < GB:
                        dve.wait_ge(gu_done, GB * e + b + 1)
                        if b >= 2 or not first:
                            dve.wait_ge(sig_ready, GB * e + b - 1)
                            dve.wait_ge(prod_ready, GB * e + b - 1)
                        dve_bias(dve, e, b).then_inc(gu_taken, 1)
                        dve.wait_ge(gu_taken, GB * e + b + 1)
                        dve_glu(dve, b).then_inc(glu_ready, 1)
                        dve_lin(dve, b).then_inc(lin_ready, 1)
                        dve.wait_ge(glu_ready, GB * e + b + 1)
                        dve.wait_ge(lin_ready, GB * e + b + 1)
                        if b >= 2 or not first:
                            dve.wait_ge(act_ready, GB * e + b - 1)
                        dve_prod(dve, b).then_inc(prod_ready, 1)
                    if b >= 1:
                        dve.wait_ge(prod_ready, GB * e + b)
                        dve.wait_ge(sig_ready, GB * e + b)
                        dve_act(dve, b - 1).then_inc(act_ready, 1)
                if not last:
                    xT_next(e + 1)

            rows_and_gates()
            expert(0, first=True)
            with dve.Fori(1, E - 1) as e:
                expert(e)
            expert(E - 1, last=True)

            dve.wait_ge(rows_stored, 16 * E)

            def one(e, b, n):
                dve_onehot(dve, e, b * CAP).then_inc(more["onehot"], 1)
                dve.wait_ge(more["gathered"], n)
                dve_xT(dve).then_inc(more["xT"], 1)
                dve.wait_ge(more["gu"], n)
                for i in range(GB):
                    base = GB * n - GB + i + 1
                    dve_bias(dve, e, i).then_inc(more["biased"], 1)
                    dve.wait_ge(more["biased"], base)
                    dve_lin(dve, i).then_inc(more["prod"], 1)
                    dve_glu(dve, i).then_inc(more["glu"], 1)
                    dve.wait_ge(more["prod"], 2 * base - 1)
                    dve.wait_ge(more["glu"], base)
                    dve_prod(dve, i).then_inc(more["prod"], 1)
                    dve.wait_ge(more["prod"], 2 * base)
                    dve.wait_ge(more["sig"], base)
                    dve_act(dve, i).then_inc(more["act"], 1)
                dve.wait_ge(more["stored"], 16 * n)

            def skip():
                dve.sem_inc(more["onehot"], 1)
                dve.sem_inc(more["xT"], 1)
                dve.sem_inc(more["prod"], 2 * GB)
                for k in ("biased", "glu", "act"):
                    dve.sem_inc(more[k], GB)

            further_blocks(dve, lambda e: dve.nop(), one, lambda: dve.nop(), skip)

            order = [0, 1, 2, 3, 5, 6, 7, 4]
            for m in range(2 * NT):
                t, half = m // 2, m % 2
                dve.wait_ge(bias_done, m + 1)
                xs = x_sb[:, t, half * 512:(half + 1) * 512]
                ins = dve.tensor_tensor(xs, ps[:, order[m], :], xs, ALU.add)
            step(ins)
            dve.wait_ge(tail_loaded, 32)
            for t in range(NT):
                dve.wait_ge(got_rows[t], 16 * TOP_K)
                for k in range(TOP_K):
                    ins = dve.scalar_tensor_tensor(x_sb[:, t, :], got[:, t * TOP_K + k, :], gates[:, t, k:k + 1],
                                                   x_sb[:, t, :], ALU.mult, ALU.add)
                    if k < TOP_K - 1:
                        step(ins)
                    else:
                        ins.then_inc(acc_ready, 1)
                inverse_root(12 + t, 1, D)
                dve.scalar_tensor_tensor(o_row[:, t, :], x_sb[:, t, :], rstd[:, 12 + t, 0:1], fin_w,
                                         ALU.mult, ALU.mult).then_inc(out_ready, 1)


_INS = ['x', 'norm_mix_w', 'w_in', 'ret_norm_w', 'w_pool', 'pool_scale', 'w_out', 'norm_ffn_w', 'w_router',
        'b_router', 'w_gu', 'b_gu', 'w_down', 'b_down', 'norm_final_w']


def shape_constants(seq):
    import numpy as np
    half = P // 2
    inv = np.power(np.float32(10000.0), -np.arange(half, dtype=np.float32) / np.float32(half), dtype=np.float32)
    ang = np.arange(seq, dtype=np.float32)[:, None] * inv[None, :]
    c, s = np.cos(ang.astype(np.float64)), np.sin(ang.astype(np.float64))
    nt = seq // P
    cc = np.concatenate([c, c], 1).reshape(nt, P, P).transpose(1, 0, 2).reshape(P, -1)
    sn = np.concatenate([-s, s], 1).reshape(nt, P, P).transpose(1, 0, 2).reshape(P, -1)
    rope = np.concatenate([cc, sn], 1).astype(np.float32)

    m, n = np.arange(P)[:, None], np.arange(seq)[None, :]
    seen = (n // CHUNK) >= (m // CHUNK)
    heads = []
    for h in range(4):
        log_g = np.log1p(-np.exp2(-5.0 - h))
        heads.append(np.where(seen, np.exp(log_g * np.abs(n - m)), 0.0) * P ** -0.5)
    decay = np.concatenate(heads, 1).astype(np.float32)

    blocks = -(-seq // CAP)
    small = np.zeros((P, 384 + blocks * CAP), np.float32)
    small[:, 0:128] = np.eye(P)
    small[:, 128:256] = np.triu(np.ones((P, P)), 1)
    small[:, 256:288] = np.arange(32)
    small[:, 288:320] = CAP * np.arange(32) - 1
    for g, w in enumerate(WINDOWS):
        small[:, 320 + 16 * g:336 + 16 * g] = w / np.minimum(np.arange(16) + 1, w)
    small[:, 384:] = np.arange(blocks * CAP) + 1
    return {"rope": rope, "decay": decay, "small": small}


def kernel(**inputs):
    import numpy as _np
    import concourse.bacc as _bacc
    from concourse import mybir as _mybir
    from concourse.bass_utils import run_bass_kernel_spmd as _run

    nc = _bacc.Bacc("TRN2", target_bir_lowering=False, num_devices=1)
    arrays, args = {}, []
    for name in _INS:
        a = _np.ascontiguousarray(inputs[name])
        arrays[f"in_{name}_dram"] = a
        args.append(nc.dram_tensor(f"in_{name}_dram", a.shape, _mybir.dt.from_np(a.dtype), kind="ExternalInput").ap())
    for name, a in shape_constants(inputs["x"].shape[1]).items():
        arrays[f"const_{name}_dram"] = a
        args.append(nc.dram_tensor(f"const_{name}_dram", a.shape, _mybir.dt.from_np(a.dtype), kind="ExternalInput").ap())
    shape = inputs["x"].shape
    args.append(nc.dram_tensor("out_0_dram", shape, _mybir.dt.float32, kind="ExternalOutput").ap())
    build_program(nc, *args)
    r = _run(nc, [arrays], core_ids=[0])
    return r.results[0]["out_0_dram"]
```

```python
from contextlib import ExitStack

import concourse.bass as bass
from concourse import mybir

ALU = mybir.AluOpType
ACT = mybir.ActivationFunctionType
AX_X = mybir.AxisListType.X
F32 = mybir.dt.float32
BF16 = mybir.dt.bfloat16
F16 = mybir.dt.float16
I32 = mybir.dt.int32
U32 = mybir.dt.uint32

P = 128
CAP = 88
EPS = 1e-6
TOP_K = 4
WINDOWS = (2, 4, 8, 16)
LIMIT = 7.0
ALPHA = 1.702
CHUNK = 64
SCALE_X = 16.0
SCALE_W = 32.0
SCALE_A = 64.0


def build_program(nc, x, norm_mix_w, w_in, ret_norm_w, w_pool, pool_scale, w_out, norm_ffn_w, w_router,
                  b_router, w_gu, b_gu, w_down, b_down, norm_final_w, rope, decay, small, out):
    _, S, D = x.shape
    E = w_router.shape[2]
    F = w_down.shape[2]
    NT = S // P
    KD = D // P
    W = w_in.shape[2] // 5
    H = W // P
    NF = 2 * F // P
    BLOCKS = -(-S // CAP)
    RANKS = BLOCKS * CAP
    FIRST = E * CAP
    GU_CH = KD
    DN_CH = F // P // 2
    CH = GU_CH + DN_CH
    RAW = CH // 2
    BY_POOL = (3, 9)
    BY_DVE = tuple(c for c in range(CH) if c not in BY_POOL)
    SLOT = 2 * F
    GB = 4
    PER = NF // GB
    assert D == F and W == 512 and H == 4 and NT == 4 and GU_CH == 8 and S == 512 and PER * CAP <= 512

    y_rows = nc.dram_tensor("y_rows", [BLOCKS * FIRST, D], F32, kind="Internal").ap()

    with ExitStack() as ctx:
        def sb(name, shape, dt=F32):
            return ctx.enter_context(nc.sbuf_tensor(name, shape, dt))

        def sem(name):
            return ctx.enter_context(nc.semaphore(name))

        ring = sb("ring", [P, CH, SLOT])
        arena = sb("arena", [P, 24160])
        at = [0]

        def region(cols):
            at[0] += cols
            return arena[:, at[0] - cols:at[0]]

        x_sb = region(NT * D).rearrange("p (t d) -> p t d", t=NT)
        reg_h = region(KD * S)
        reg_vg = region(2048 + 2048 + 2560)
        reg_d = region(2048)
        reg_r = region(2048)
        reg_p = region(2112 + 1056 + 2048)

        hT = reg_h.rearrange("p (k s) -> p k s", k=KD)
        mixT = hT
        v_sb = reg_vg[:, 0:2048].rearrange("p (t c) -> p t c", t=NT)
        gate_sb = reg_vg[:, 2048:4096].rearrange("p (t c) -> p t c", t=NT)
        sT = reg_vg[:, 4096:6656].rearrange("p (b c) -> p b c", b=2)
        xn1 = reg_vg[:, 0:2048].rearrange("p (b c) -> p b c", b=2)
        dec = reg_d.rearrange("p (h c) -> p h c", h=H)
        rope_c = reg_r[:, 0:512].rearrange("p (t c) -> p t c", t=NT)
        rope_s = reg_r[:, 512:1024].rearrange("p (t c) -> p t c", t=NT)
        rot = reg_r[:, 1024:2048].rearrange("p (b c) -> p b c", b=2)
        PADS = 16
        pT = reg_p[:, 0:2112].rearrange("p (g c) -> p g c", g=H)
        psum_a = reg_p[:, 2112:2112 + 528]
        psum_b = reg_p[:, 2640:2640 + 528]
        mixtok = reg_p[:, 3168:5216].rearrange("p (h c) -> p h c", h=H)
        qT = ring[:, 10, :].rearrange("p (h s) -> p h s", h=H)
        kT = ring[:, 11, :].rearrange("p (h s) -> p h s", h=H)
        bgu_raw = mixtok[:, 0, :]
        parts = reg_vg[:, 0:4096].bitcast(F16).rearrange("p (i t d) -> p i t d", i=2, t=NT)
        nf_row = reg_vg[:, 4096:5120]
        h2T = reg_d.rearrange("p (b k c) -> p b k c", b=2, k=KD)
        xn2 = reg_r.rearrange("p (b c) -> p b c", b=2)
        xT = reg_h[:, 0:KD * CAP].bitcast(F16).rearrange("p (i k c) -> p i k c", i=2, k=KD)
        actT = reg_h[:, 768:768 + KD * CAP].bitcast(F16).rearrange("p (i k c) -> p i k c", i=2, k=KD)
        act32 = reg_d[:, 0:PER * CAP].rearrange("p (b c) -> p b c", b=2)
        yT = reg_h[:, 1536:1536 + KD * CAP].rearrange("p (k c) -> p k c", k=KD)
        gub = reg_h[:, 2304:2304 + 2 * PER * CAP].rearrange("p (b h c) -> p b h c", b=2, h=2)
        prod = reg_h[:, 3072:3072 + PER * CAP].rearrange("p (b c) -> p b c", b=2)
        sig = reg_h[:, 3456:3456 + PER * CAP].rearrange("p (b c) -> p b c", b=2)
        zeros = reg_p[:, 0:1024]
        y_row = reg_p[:, 1024:2048]
        onehot = reg_p[:, 2048:2048 + NT * CAP // 2].bitcast(F16).rearrange("p (t c) -> p t c", t=NT)
        is_kth = reg_p[:, 2304:2816].rearrange("p (t k e) -> p t k e", t=NT, k=TOP_K)
        of_kth = reg_p[:, 2816:3328].rearrange("p (t k e) -> p t k e", t=NT, k=TOP_K)
        got = ring[:, :, :].rearrange("p s (a d) -> p (s a) d", a=2)
        o_row = reg_vg[:, 0:4096].rearrange("p (t d) -> p t d", t=NT)
        fin_w = reg_h[:, 0:1024]
        bd_sb = reg_h[0:E, 1024:2048]
        gdT = reg_h[0:E, 2048:2048 + S]

        sm = sb("sm", [P, small.shape[1]])
        ident = sm[:, 0:128]
        tri_f = sm[:, 128:256]
        iota32 = sm[:, 256:288]
        e_base = sm[:, 288:320]
        corr = sm[:, 320:384].rearrange("p (g c) -> p g c", g=H)
        ranks = sm[:, 384:384 + RANKS]
        tri = sb("tri", [P, P], BF16)
        ones = sb("ones", [P, P], BF16)
        wp_sb = sb("wp_sb", [P, H, P])
        wr_sb = sb("wr_sb", [P, KD, E])
        br_sb = sb("br_sb", [P, E])
        rw_sb = sb("rw_sb", [P, W])
        bguT = sb("bguT", [P, E, NF])
        nm_w = sb("nm_w", [P, KD])
        ps_w = sb("ps_w", [P, H])
        eps_t = sb("eps_t", [P, 1])
        ss = sb("ss", [P, 16, 4])
        var = sb("var", [P, 16, 4])
        std = sb("std", [P, 16, 4])
        rstd = sb("rstd", [P, 16, 4])
        nwt = sb("nwt", [P, 4])
        logit = sb("logit", [P, NT, E])
        top8 = sb("top8", [P, NT, 8])
        idx8 = sb("idx8", [P, NT, 8], U32)
        idxf = sb("idxf", [P, NT, 8])
        negmax = sb("negmax", [P, NT])
        expo = sb("expo", [P, NT, TOP_K])
        esum = sb("esum", [P, NT])
        einv = sb("einv", [P, NT])
        gates = sb("gates", [P, NT, TOP_K])
        chosen = sb("chosen", [P, NT, E])
        chosen_b = sb("chosen_b", [P, NT, E], BF16)
        rank1 = sb("rank1", [P, E, NT])
        rank_row = sb("rank_row", [P, NT, E])
        passed_b = sb("passed_b", [P, NT, E])
        row_f = sb("row_f", [P, NT * TOP_K])
        row_u = sb("row_u", [P, NT * TOP_K], U32)
        gdense = sb("gdense", [P, NT, E])
        count_i = sb("count_i", [P, E], I32)
        count_max = sb("count_max", [P, 1])
        count_max_i = sb("count_max_i", [P, 1], I32)

        ps = ctx.enter_context(nc.psum_tensor("ps", [P, 8, 512], F32))

        wide = [("z", n) for n in range(16)]
        for h in range(H):
            wide += [("pv", h), ("z", 16 + h)]
        wide += [("pool", g) for g in range(H)] + [("out", m) for m in range(2 * NT)]
        turned = [("bgu", j) for j in range(4)] + [("x", t, i) for t in range(NT) for i in range(2)]
        turned += [("qk", n) for n in range(8)]
        turned += [("s", h, i) for h in range(H) for i in range(NT)]
        turned += [("mix", h) for h in range(H)]
        for t in range(NT - 1):
            turned += [("h2", t, 0), ("h2", t, 1), ("log", t, 0), ("log", t, 1)]
        turned += [("h2", 3, 0), ("h2", 3, 1), ("log", 3, 0), ("pos", 0)]
        bank_of, turn_of = {}, {}
        for first, order in ((0, wide), (4, turned)):
            for n, key in enumerate(order):
                bank_of[key], turn_of[key] = first + n % 4, n // 4
        empty = {key for key in turned if key[0] == "log" and key[2] == 1}
        uses = [0] * 8
        for key in wide + turned:
            if key not in empty:
                turn_of[key] = uses[bank_of[key]]
                uses[bank_of[key]] += 1
        bank_free = [sem(f"bank_free{b}") for b in range(8)]

        def bank(key):
            return ps[:, bank_of[key], :]

        def take(pe, key):
            if turn_of[key]:
                pe.wait_ge(bank_free[bank_of[key]], turn_of[key])

        def emptied(eng, key):
            eng.wait_ge(bank_free[bank_of[key]], turn_of[key] + 1)

        def free(ins, key):
            ins.then_inc(bank_free[bank_of[key]], 1)

        x_loaded = [sem(f"x_loaded{t}") for t in range(NT)]
        win_loaded = [sem(f"win_loaded{c}") for c in range(5)]
        wout_loaded = [sem(f"wout_loaded{c}") for c in range(2)]
        small_loaded = sem("small_loaded")
        rope_loaded = sem("rope_loaded")
        dec_loaded = sem("dec_loaded")
        norms_loaded = sem("norms_loaded")
        wpool_loaded = sem("wpool_loaded")
        router_loaded = sem("router_loaded")
        bgu_loaded = sem("bgu_loaded")
        rw_loaded = sem("rw_loaded")
        consts_made = sem("consts_made")
        bgu_turned = sem("bgu_turned")
        ss_ready = sem("ss_ready")
        std_ready = sem("std_ready")
        xn_ready = sem("xn_ready")
        x_turned = sem("x_turned")
        hT_ready = sem("hT_ready")
        z_done = sem("z_done")
        rot_ready = sem("rot_ready")
        qk_turned = sem("qk_turned")
        sig_gate = sem("sig_gate")
        silu_ready = sem("silu_ready")
        gate_ready = sem("gate_ready")
        pad_ready = sem("pad_ready")
        scores_done = sem("scores_done")
        sT_ready = sem("sT_ready")
        pv_done = sem("pv_done")
        mixtok_ready = sem("mixtok_ready")
        mix_turned = sem("mix_turned")
        pool_step = sem("pool_step")
        window_ready = sem("window_ready")
        pooled_ready = sem("pooled_ready")
        pool_done = sem("pool_done")
        out_done = sem("out_done")
        x2_ready = sem("x2_ready")
        xn2_ready = sem("xn2_ready")
        hi_ready = sem("hi_ready")
        parts_ready = sem("parts_ready")
        h2_turned = sem("h2_turned")
        logits_done = sem("logits_done")
        top_ready = sem("top_ready")
        exp_ready = sem("exp_ready")
        chosen_ready = sem("chosen_ready")
        pos_done = sem("pos_done")
        dve_step = sem("dve_step")
        routed = sem("routed")
        nf_loaded = sem("nf_loaded")
        counts_ready = sem("counts_ready")
        slot_loaded = [sem(f"slot_loaded{s}") for s in range(RAW)]
        high_ready = sem("high_ready")
        low_ready = sem("low_ready")
        scaled_ready = sem("scaled_ready")
        pool_low_ready = sem("pool_low_ready")
        act32_ready = sem("act32_ready")
        ah_ready = sem("ah_ready")
        chunk_used = sem("chunk_used")
        onehot_ready = sem("onehot_ready")
        gathered = sem("gathered")
        xT_ready = sem("xT_ready")
        gu_done = sem("gu_done")
        gu_taken = sem("gu_taken")
        glu_ready = sem("glu_ready")
        lin_ready = sem("lin_ready")
        prod_ready = sem("prod_ready")
        sig_ready = sem("sig_ready")
        act_ready = sem("act_ready")
        y_done = sem("y_done")
        yT_ready = sem("yT_ready")
        row_turned = sem("row_turned")
        row_ready = sem("row_ready")
        rows_stored = sem("rows_stored")
        more = {k: sem(f"more_{k}") for k in ("high", "low", "used", "onehot", "gathered", "xT", "biased",
                                              "glu", "prod", "sig", "act32", "ah", "act", "yT", "turned",
                                              "row", "stored")}
        more_loaded = [sem(f"more_loaded{s}") for s in range(RAW)]
        passed = sem("passed")
        zeros_ready = sem("zeros_ready")
        cleared = sem("cleared")
        tail_loaded = sem("tail_loaded")
        gd_turned = sem("gd_turned")
        gdT_ready = sem("gdT_ready")
        bias_done = sem("bias_done")
        got_rows = [sem(f"got_rows{t}") for t in range(NT)]
        acc_ready = sem("acc_ready")
        out_ready = sem("out_ready")
        out_stored = sem("out_stored")

        xt_d = x[0].rearrange("(t p) d -> p t d", p=P)
        out_d = out[0].rearrange("(t p) d -> p t d", p=P)
        win_cols = [0, 1, 3, 2, 4]

        def win(c):
            return ring[:, 2 * c:2 * c + 2, :].rearrange("p s c -> p (s c)").rearrange("p (k c) -> p k c", k=KD)

        def wout(k):
            j = (k + 4) % 8
            return ring[:, 4 + j // 2, (j % 2) * D:(j % 2 + 1) * D]

        def load_chunk(sp, c, e):
            dst = ring[:, c % RAW, :]
            if c < GU_CH:
                return sp.dma_start(dst, w_gu[0, bass.ds(e, 1), c * P:(c + 1) * P, :].rearrange("a p c -> (a p) c"))
            r = (c - GU_CH) * 2 * P
            src = w_down[0, bass.ds(e, 1), r:r + 2 * P, :].rearrange("a (j p) c -> p (a j) c", p=P)
            return sp.dma_start(dst.rearrange("p (j c) -> p j c", j=2), src)

        def split_of(c):
            return ring[:, RAW + (c + 2) % RAW, :].bitcast(F16).rearrange("p (i c) -> p i c", i=2)

        def act_high(act, c):
            return act.activation(split_of(c)[:, 0, :], ring[:, c % RAW, :], ACT.Copy, scale=SCALE_W)

        def dve_low(dve, c):
            return dve.scalar_tensor_tensor(split_of(c)[:, 1, :], ring[:, c % RAW, :], SCALE_W,
                                            split_of(c)[:, 0, :], ALU.mult, ALU.subtract)

        def act_scale(act, c):
            return act.activation(ring[:, c % RAW, :], ring[:, c % RAW, :], ACT.Copy, scale=SCALE_W)

        def act_scaled_high(act, c):
            return act.activation(split_of(c)[:, 0, :], ring[:, c % RAW, :], ACT.Copy)

        def pool_low(pool, c):
            return pool.tensor_tensor(split_of(c)[:, 1, :], ring[:, c % RAW, :], split_of(c)[:, 0, :], ALU.subtract)

        def split_done(eng, e, c):
            if c in BY_POOL:
                eng.wait_ge(pool_low_ready, len(BY_POOL) * e + BY_POOL.index(c) + 1)
            else:
                eng.wait_ge(low_ready, len(BY_DVE) * e + BY_DVE.index(c) + 1)

        def chunk_gone(eng, e, c):
            if c < GU_CH - 1:
                eng.wait_ge(chunk_used, (CH - 2) * e + c + 1)
            elif c == GU_CH - 1:
                eng.wait_ge(gu_done, GB * e + GB)
            elif c < CH - 1:
                eng.wait_ge(chunk_used, (CH - 2) * e + c)
            else:
                eng.wait_ge(y_done, e + 1)

        MISC = ps[:, 6:8, :]
        GU = ps[:, 0:4, 0:PER * CAP]
        YT = ps[:, 4:6, 0:4 * CAP]

        def pe_gather(pe, i):
            for d in range(KD):
                o = (MISC if i == 0 else YT)[:, d // 4, (d % 4) * CAP:(d % 4 + 1) * CAP]
                for t in range(NT):
                    mm = pe.matmul(o, parts[:, i, t, d * P:(d + 1) * P], onehot[:, t, :],
                                   start=(t == 0), stop=(t == NT - 1), skip_group_check=True)
            return mm

        def product(pe, o, w, col, src, k, start, stop):
            for n, (i, j) in enumerate(((0, 0), (0, 1), (1, 0))):
                mm = pe.matmul(o, w[:, i, col:col + P], src[:, j, k, :], start=start and n == 0,
                               stop=stop and n == 2, skip_group_check=True)
            return mm

        def gu_tile(b, j):
            return 2 * b + j if j < 2 else NF // 2 + 2 * b + j - 2

        def pe_gu(pe, k, b):
            for j in range(PER):
                f = gu_tile(b, j)
                mm = product(pe, GU[:, b, j * CAP:(j + 1) * CAP], split_of(k), f * P, xT, k,
                             k == 0 and j == 0, k == KD - 1)
            return mm

        def pe_down(pe, f):
            for d in range(KD):
                mm = product(pe, YT[:, d // 4, (d % 4) * CAP:(d % 4 + 1) * CAP], split_of(GU_CH + f // 2),
                             (f % 2) * D + d * P, actT, f, f == 0 and d % 4 == 0, f == KD - 1)
            return mm

        def pe_turn_rows(pe):
            for d in range(KD):
                mm = pe.transpose(MISC[0:CAP, d // 4, (d % 4) * P:(d % 4 + 1) * P], yT[:, d, :], ident)
            return mm

        def dve_onehot(dve, e, first_rank):
            return dve.tensor_tensor(
                onehot, ranks[:, bass.ds(first_rank, CAP)].unsqueeze(1).to_broadcast([P, NT, CAP]),
                rank1[:, bass.ds(e, 1), :].rearrange("p a t -> p (a t)").unsqueeze(2).to_broadcast([P, NT, CAP]),
                ALU.is_equal)

        def act_xT(act, i):
            src = (MISC if i == 0 else YT)[:, :, 0:4 * CAP]
            return act.activation(xT[:, i].rearrange("p (a k) c -> p a (k c)", a=2), src, ACT.Copy)

        def dve_bias(dve, e, b):
            return dve.scalar_tensor_tensor(
                gub[:, b % 2].rearrange("p h (j c) -> p (h j) c", j=2),
                GU[:, b, :].rearrange("p (j c) -> p j c", j=PER), 1.0 / (SCALE_X * SCALE_W),
                bguT[:, bass.ds(e, 1), PER * b:PER * b + PER].rearrange("p a j -> p (a j)").unsqueeze(2)
                .to_broadcast([P, PER, CAP]), ALU.mult, ALU.add)

        def dve_glu(dve, b):
            return dve.tensor_scalar(gub[:, b % 2, 0], gub[:, b % 2, 0], LIMIT, None, ALU.min)

        def dve_lin(dve, b):
            return dve.tensor_scalar(gub[:, b % 2, 1], gub[:, b % 2, 1], LIMIT, -LIMIT, ALU.min, ALU.max)

        def dve_prod(dve, b):
            return dve.scalar_tensor_tensor(prod[:, b % 2], gub[:, b % 2, 1], 1.0, gub[:, b % 2, 0],
                                            ALU.add, ALU.mult)

        def dve_act32(dve, b):
            return dve.scalar_tensor_tensor(act32[:, b % 2], prod[:, b % 2], SCALE_A, sig[:, b % 2],
                                            ALU.mult, ALU.mult)

        def act_ah(act, b):
            return act.activation(actT[:, 0, 2 * b:2 * b + 2, :].rearrange("p j c -> p (j c)"), act32[:, b % 2], ACT.Copy)

        def dve_al(dve, b):
            return dve.tensor_tensor(actT[:, 1, 2 * b:2 * b + 2, :].rearrange("p j c -> p (j c)"), act32[:, b % 2],
                                     actT[:, 0, 2 * b:2 * b + 2, :].rearrange("p j c -> p (j c)"), ALU.subtract)

        def act_sig(act, b):
            return act.activation(sig[:, b % 2], gub[:, b % 2, 0], ACT.Sigmoid, scale=ALPHA)

        def act_yT(act, half):
            return act.activation(yT[:, 4 * half:4 * half + 4, :].rearrange("p k c -> p (k c)"),
                                  YT[:, half, :], ACT.Copy, scale=1.0 / (SCALE_A * SCALE_W))

        def act_row(act, half):
            return act.activation(y_row[0:CAP, half * 512:(half + 1) * 512], MISC[0:CAP, half, :], ACT.Copy)

        def store_rows(act, row):
            return act.dma_start(y_rows[bass.ds(row, CAP), :], y_row[0:CAP, :])

        def further_blocks(eng, block, skip_block, setup=None):
            most = eng.value_load(count_max_i[0:1, 0:1], min_val=0, max_val=S)
            with eng.If(most > CAP):
                if setup:
                    setup()
                with eng.Fori(0, E) as e:
                    c = eng.value_load(count_i[0:1, bass.ds(e, 1)], min_val=0, max_val=S)
                    with eng.Fori(1, BLOCKS) as b:
                        with eng.If(c > b * CAP):
                            block(e, b, e * (BLOCKS - 1) + b)
                            eng.sem_inc(passed, 1)
                        with eng.Else():
                            skip_block()
                        eng.nop()
                    eng.nop()
                eng.nop()
            with eng.Else():
                eng.nop()
            eng.nop()
            return most

        block = ctx.enter_context(nc.Block())

        @block.sync
        def _(sp):
            for t in range(NT):
                sp.dma_start(x_sb[:, t, :], xt_d[:, t, :]).then_inc(x_loaded[t], 16)
            for c in range(5):
                src = w_in[0, :, win_cols[c] * W:(win_cols[c] + 1) * W].rearrange("(k p) c -> p k c", p=P)
                sp.dma_start(win(c), src).then_inc(win_loaded[c], 16)

            def expert0(chunks):
                for c in chunks:
                    load_chunk(sp, c, 0).then_inc(slot_loaded[c % RAW], 16)

            sp.wait_ge(z_done, 4)
            expert0((0, 1))
            sp.wait_ge(z_done, 8)
            expert0((2, 3))
            sp.wait_ge(z_done, 12)
            sp.dma_start(ring[:, 4:6, :].rearrange("p s (a c) -> p (s a) c", a=2),
                         w_out[0, W:2 * W, :].rearrange("(k p) c -> p k c", p=P)).then_inc(wout_loaded[1], 16)
            sp.wait_ge(z_done, 16)
            sp.dma_start(ring[:, 6:8, :].rearrange("p s (a c) -> p (s a) c", a=2),
                         w_out[0, 0:W, :].rearrange("(k p) c -> p k c", p=P)).then_inc(wout_loaded[0], 16)
            for c in (6, 7, 8, 9):
                split_done(sp, 0, c - RAW)
                expert0((c,))
            sp.wait_ge(out_done, 8)
            expert0((4, 5))
            for c in (10, 11):
                split_done(sp, 0, c - RAW)
                expert0((c,))
            with sp.Fori(1, E) as e:
                for c in range(CH):
                    split_done(sp, e if c >= RAW else e - 1, (c - RAW) % CH)
                    load_chunk(sp, c, e).then_inc(slot_loaded[c % RAW], 16)

            sp.wait_ge(counts_ready, 1)
            split_done(sp, E - 1, CH - 1)
            split_done(sp, E - 1, BY_POOL[-1])

            def one(e, b, n):
                for c in range(CH):
                    if c >= RAW:
                        sp.wait_ge(more["low"], CH * (n - 1) + c - RAW + 1)
                    load_chunk(sp, c, e).then_inc(more_loaded[c % RAW], 16)
                sp.wait_ge(more["stored"], 16 * n)

            def skip():
                for s in range(RAW):
                    sp.sem_inc(more_loaded[s], 32)

            def clear():
                sp.wait_ge(zeros_ready, 1)
                sp.dma_start(y_rows[FIRST:BLOCKS * FIRST, :].rearrange("(n p) d -> p n d", p=P),
                             zeros.unsqueeze(1).to_broadcast([P, (BLOCKS - 1) * FIRST // P, D])).then_inc(cleared, 16)

            further_blocks(sp, one, skip, clear)

            for t in range(NT):
                sp.wait_ge(out_ready, t + 1)
                sp.dma_start(out_d[:, t, :], o_row[:, t, :]).then_inc(out_stored, 16)
            sp.wait_ge(out_stored, 16 * NT)

        @block.gpsimd
        def _(pool):
            pool.memset(ones[:, :], 1.0).then_inc(consts_made, 1)
            pool.memset(pT[:, :, 0:PADS], 0.0).then_inc(pad_ready, 1)
            pool.wait_ge(rw_loaded, 16)
            for t in range(NT):
                pool.wait_ge(silu_ready, t + 1)
                pool.tensor_tensor(gate_sb[:, t, :], gate_sb[:, t, :], rw_sb[:, :], ALU.mult).then_inc(gate_ready, 1)
            step = 0
            pool.wait_ge(pad_ready, 1)
            for n, g in enumerate(reversed(range(H))):
                emptied(pool, ("z", 16 + n))
                src = pT[:, g, :]
                if n:
                    pool.wait_ge(pooled_ready, n)
                w = 1
                while w < WINDOWS[g]:
                    dst = psum_a if src is not psum_a else psum_b
                    pool.tensor_tensor(dst[:, w:PADS + S], src[:, w:PADS + S], src[:, 0:PADS + S - w], ALU.add)\
                        .then_inc(pool_step, 1)
                    pool.memset(dst[:, 0:w], 0.0).then_inc(pool_step, 1)
                    step += 2
                    pool.wait_ge(pool_step, step)
                    src = dst
                    w *= 2
                pool.tensor_tensor(src[:, PADS:2 * PADS], src[:, PADS:2 * PADS], corr[:, g, :], ALU.mult)\
                    .then_inc(window_ready, 1)

            def low(e, c):
                pool.wait_ge(high_ready, CH * e + c + 1)
                pool_low(pool, c).then_inc(pool_low_ready, 1)

            with pool.Fori(0, E) as e:
                for c in BY_POOL:
                    low(e, c)

            pool.wait_ge(counts_ready, 1)

            def make_zeros():
                pool.wait_ge(parts_ready, NT)
                pool.memset(zeros, 0.0).then_inc(zeros_ready, 1)

            most = further_blocks(pool, lambda e, b, n: pool.wait_ge(more["stored"], 16 * n), lambda: pool.nop(),
                                  make_zeros)
            pool.wait_ge(routed, 1)
            pool.wait_ge(rows_stored, 16 * E)
            pool.wait_ge(y_done, E)

            def fetch(rows):
                for t in range(NT):
                    for k in range(TOP_K):
                        n = t * TOP_K + k
                        pool.indirect_dma_start(
                            out=got[:, n, :], out_offset=None, in_=rows,
                            in_offset=bass.IndirectOffsetOnAxis(ap=row_u[:, n:n + 1], axis=0))\
                            .then_inc(got_rows[t], 16)

            with pool.If(most > CAP):
                fetch(y_rows)
            with pool.Else():
                fetch(y_rows[0:FIRST, :])
            pool.nop()

        @block.scalar
        def _(act):
            act.dma_start(sm[:, :], small).then_inc(small_loaded, 16)
            with nc.allow_non_contiguous_dma(reason="1024 weights, one on each partition and tile"):
                act.dma_start(nm_w[:, :], norm_mix_w[0].rearrange("(k p) -> p k", p=P)).then_inc(norms_loaded, 16)
                act.dma_start(ps_w[:, :], pool_scale[0].rearrange("(g p) -> p g", p=P)).then_inc(norms_loaded, 16)
            act.dma_start(bgu_raw[:, :], b_gu[0].rearrange("e (q c) -> (e q) c", q=4)).then_inc(bgu_loaded, 16)
            act.dma_start(reg_r[:, 0:1024], rope).then_inc(rope_loaded, 16)
            act.dma_start(reg_d, decay).then_inc(dec_loaded, 16)
            act.dma_start(rw_sb[:, :], ret_norm_w[0:1, :].to_broadcast([P, W])).then_inc(rw_loaded, 16)
            act.dma_start(wp_sb[:, :, :], w_pool[0].rearrange("g c d -> c g d")).then_inc(wpool_loaded, 16)
            act.dma_start(wr_sb[:, :, :], w_router[0].rearrange("(k p) e -> p k e", p=P)).then_inc(router_loaded, 16)
            act.dma_start(br_sb[:, :], b_router[0:1, :].to_broadcast([P, E])).then_inc(router_loaded, 16)

            norms = [0]

            def root(width, n):
                r = norms[0]
                norms[0] += 1
                act.wait_ge(ss_ready, r + 1)
                act.activation(std[:, r, 0:width], ss[:, r, 0:width], ACT.Sqrt, bias=eps_t[:, :], scale=1.0 / n)\
                    .then_inc(std_ready, 1)

            act.wait_ge(consts_made, 3)
            for t in range(NT):
                act.wait_ge(x_loaded[t], 16)
                if t >= 2:
                    act.wait_ge(x_turned, t - 1)
                act.activation(xn1[:, t % 2], x_sb[:, t, :], ACT.Square, accum_out=ss[:, t, 0:1]).then_inc(ss_ready, 1)
                root(1, D)

            def qk(n):
                act.wait_ge(qk_turned, n + 1)
                dst = (qT if n < 4 else kT)[:, :, (n % 4) * P:(n % 4 + 1) * P]
                ins = act.activation(dst, bank(("qk", n)).rearrange("p (h c) -> p h c", h=H), ACT.Copy)
                free(ins, ("qk", n))

            def gate_sig(t):
                act.wait_ge(z_done, 8 + t + 1)
                act.activation(gate_sb[:, t, :], bank(("z", 8 + t)), ACT.Sigmoid).then_inc(sig_gate, 1)

            for n in range(6):
                qk(n)
            gate_sig(0)
            qk(6)
            gate_sig(1)
            qk(7)
            gate_sig(2)
            gate_sig(3)
            for t in range(NT):
                act.wait_ge(z_done, 12 + t + 1)
                ins = act.activation(v_sb[:, t, :], bank(("z", 12 + t)), ACT.Copy)
                free(ins, ("z", 12 + t))
            for h in range(H):
                act.wait_ge(pv_done, h + 1)
                for j in range(NT):
                    ins = act.activation(mixtok[:, h, j * P:(j + 1) * P], bank(("pv", h))[:, j * P:(j + 1) * P],
                                         ACT.Square, accum_out=ss[:, 4 + h, j:j + 1])
                ins.then_inc(ss_ready, 1)
                root(NT, P)
                if h == H - 1:
                    act.dma_start(nf_row, norm_ffn_w[0:1, :].to_broadcast([P, D])).then_inc(nf_loaded, 16)
                act.wait_ge(z_done, 16 + h + 1)
                act.wait_ge(pad_ready, 1)
                ins = act.activation(pT[:, H - 1 - h, PADS:PADS + S], bank(("z", 16 + h)), ACT.Copy)
                free(ins, ("z", 16 + h))
            for h in range(H):
                act.wait_ge(mix_turned, h + 1)
                act.wait_ge(z_done, 20)
                ins = act.activation(mixT[:, h, :], bank(("mix", h)), ACT.Copy)
                free(ins, ("mix", h))
            act.wait_ge(norms_loaded, 32)
            for n, g in enumerate(reversed(range(H))):
                act.wait_ge(pool_done, n + 1)
                ins = act.activation(mixT[:, H + g, :], bank(("pool", n)), ACT.Copy, scale=ps_w[:, g:g + 1])
                free(ins, ("pool", n))

            def norm2(t):
                act.wait_ge(x2_ready, t + 1)
                if t >= 2:
                    act.wait_ge(h2_turned, t - 1)
                    act.wait_ge(parts_ready, t - 1)
                act.activation(xn2[:, t % 2], x_sb[:, t, :], ACT.Square, accum_out=ss[:, 8 + t, 0:1])\
                    .then_inc(ss_ready, 1)
                root(1, D)

            def high_part(t):
                act.wait_ge(xn2_ready, t + 1)
                act.activation(parts[:, 0, t, :], xn2[:, t % 2], ACT.Copy, scale=SCALE_X).then_inc(hi_ready, 1)

            def turned_h2(t):
                act.wait_ge(h2_turned, t + 1)
                if t >= 2:
                    act.wait_ge(logits_done, t - 1)
                for i in range(2):
                    ins = act.activation(h2T[:, t % 2, 4 * i:4 * i + 4, :].rearrange("p k c -> p (k c)"),
                                         bank(("h2", t, i)), ACT.Copy)
                    free(ins, ("h2", t, i))

            def high(e, c):
                act.wait_ge(slot_loaded[c % RAW], 32 * e + 16 * (c // RAW) + 16)
                if c in BY_POOL:
                    act_scale(act, c).then_inc(scaled_ready, 1)
                    act.wait_ge(scaled_ready, len(BY_POOL) * e + BY_POOL.index(c) + 1)
                if c >= RAW:
                    chunk_gone(act, e, c - RAW)
                else:
                    chunk_gone(act, e - 1, c + RAW)
                (act_scaled_high if c in BY_POOL else act_high)(act, c).then_inc(high_ready, 1)

            def first_high(c):
                act.wait_ge(slot_loaded[c], 16)
                act.wait_ge(*((z_done, 20), (scores_done, 16), (out_done, 8))[c // 2])
                if c in BY_POOL:
                    act_scale(act, c).then_inc(scaled_ready, 1)
                    act.wait_ge(scaled_ready, 1)
                (act_scaled_high if c in BY_POOL else act_high)(act, c).then_inc(high_ready, 1)

            for c in range(4):
                first_high(c)
            for t in range(NT):
                norm2(t)
                high_part(t)
                if t == NT - 1:
                    first_high(4)
                turned_h2(t)
            first_high(5)
            for t in range(NT):
                act.wait_ge(top_ready, t + 1)
                act.activation(expo[:, t, :], top8[:, t, 0:TOP_K], ACT.Exp, bias=negmax[:, t:t + 1],
                               accum_out=esum[:, t:t + 1]).then_inc(exp_ready, 1)

            def columns(e, i):
                act.wait_ge(gathered, 2 * e + 2 - i)
                act_xT(act, i).then_inc(xT_ready, 1)

            columns(0, 1)
            columns(0, 0)

            def turned_y(e):
                act.wait_ge(y_done, e + 1)
                for half in range(2):
                    act_yT(act, half).then_inc(yT_ready, 1)

            def finish_rows(e, first=False):
                act.wait_ge(row_turned, e + 1)
                if not first:
                    act.wait_ge(rows_stored, 16 * e)
                for half in range(2):
                    act_row(act, half).then_inc(row_ready, 1)
                act.wait_ge(row_ready, 2 * e + 2)
                store_rows(act, e * CAP).then_inc(rows_stored, 16)

            def sigmoid(e, b, first):
                act.wait_ge(glu_ready, GB * e + b + 1)
                if b >= 2 or not first:
                    act.wait_ge(act32_ready, GB * e + b - 1)
                act_sig(act, b).then_inc(sig_ready, 1)

            def act_high_part(e, b):
                act.wait_ge(act32_ready, GB * e + b + 1)
                act_ah(act, b).then_inc(ah_ready, 1)

            def expert(e, first=False, last=False, second=False):
                for c in range(0 if not first else RAW, 10):
                    high(e, c)
                    if c == 2 and not first:
                        turned_y(e - 1)
                    if c == 4 and not first:
                        finish_rows(e - 1, second)
                sigmoid(e, 0, first)
                if not last:
                    columns(e + 1, 1)
                sigmoid(e, 1, first)
                act_high_part(e, 0)
                if not last:
                    columns(e + 1, 0)
                sigmoid(e, 2, first)
                act_high_part(e, 1)
                high(e, 10)
                sigmoid(e, 3, first)
                act_high_part(e, 2)
                act_high_part(e, 3)
                high(e, 11)

            expert(0, first=True)
            expert(1, second=True)
            with act.Fori(2, E - 1) as e:
                expert(e)
            expert(E - 1, last=True)
            turned_y(E - 1)
            finish_rows(E - 1)

            act.wait_ge(counts_ready, 1)
            act.wait_ge(rows_stored, 16 * E)

            def one(e, b, n):
                def more_high(c):
                    act.wait_ge(more_loaded[c % RAW], 32 * n - 32 + 16 * (c // RAW) + 16)
                    if c >= RAW:
                        act.wait_ge(more["used"], CH * (n - 1) + c - RAW + 1)
                    act_high(act, c).then_inc(more["high"], 1)

                for i in (1, 0):
                    act.wait_ge(more["gathered"], 2 * n - i)
                    act_xT(act, i).then_inc(more["xT"], 1)
                for c in range(GU_CH):
                    more_high(c)
                for i in range(GB):
                    act.wait_ge(more["glu"], GB * n - GB + i + 1)
                    act_sig(act, i).then_inc(more["sig"], 1)
                    act.wait_ge(more["act32"], GB * n - GB + i + 1)
                    act_ah(act, i).then_inc(more["ah"], 1)
                for c in range(GU_CH, CH):
                    more_high(c)
                act.wait_ge(more["used"], CH * n)
                for half in range(2):
                    act_yT(act, half).then_inc(more["yT"], 1)
                act.wait_ge(more["turned"], n)
                for half in range(2):
                    act_row(act, half).then_inc(more["row"], 1)
                act.wait_ge(more["row"], 2 * n)
                act.wait_ge(cleared, 16)
                store_rows(act, b * FIRST + e * CAP).then_inc(more["stored"], 16)
                act.wait_ge(more["stored"], 16 * n)

            def skip():
                act.sem_inc(more["high"], CH)
                act.sem_inc(more["sig"], GB)
                act.sem_inc(more["ah"], GB)
                for k in ("xT", "yT", "row"):
                    act.sem_inc(more[k], 2)
                act.sem_inc(more["stored"], 16)

            further_blocks(act, one, skip)

            act.wait_ge(act_ready, GB * E)
            act.wait_ge(y_done, E)
            act.wait_ge(row_turned, E)
            act.dma_start(fin_w, norm_final_w.rearrange("(a d) -> a d", a=1).to_broadcast([P, D])).then_inc(tail_loaded, 16)
            act.dma_start(bd_sb, b_down[0]).then_inc(tail_loaded, 16)
            act.wait_ge(gd_turned, 1)
            ins = act.activation(gdT, ps[0:E, 4, :], ACT.Copy).then_inc(gdT_ready, 1)
            for t in range(NT):
                act.wait_ge(acc_ready, t + 1)
                act.activation(o_row[:, t, :], x_sb[:, t, :], ACT.Square, accum_out=ss[:, 12 + t, 0:1])\
                    .then_inc(ss_ready, 1)
                root(1, D)

        @block.tensor
        def _(pe):
            pe.wait_ge(small_loaded, 16)
            pe.wait_ge(bgu_loaded, 16)
            for j in range(4):
                take(pe, ("bgu", j))
                pe.transpose(bank(("bgu", j))[:, 0:P], bgu_raw[:, j * P:(j + 1) * P], ident).then_inc(bgu_turned, 1)
            for t in range(NT):
                pe.wait_ge(xn_ready, t + 1)
                for k in range(KD):
                    if k % 4 == 0:
                        take(pe, ("x", t, k // 4))
                    mm = pe.transpose(bank(("x", t, k // 4))[:, (k % 4) * P:(k % 4 + 1) * P],
                                      xn1[:, t % 2, k * P:(k + 1) * P], ident)
                mm.then_inc(x_turned, 1)

            def z(n):
                c = min(n // 4, 4)
                pe.wait_ge(win_loaded[c], 16)
                if n < 4:
                    pe.wait_ge(hT_ready, n + 1)
                take(pe, ("z", n))
                for k in range(KD):
                    if c < 4:
                        lhsT, rhs = hT[:, k, (n % 4) * P:(n % 4 + 1) * P], win(c)[:, k, :]
                    else:
                        g = H - 1 - (n - 16)
                        lhsT, rhs = win(4)[:, k, g * P:(g + 1) * P], hT[:, k, :]
                    mm = pe.matmul(bank(("z", n)), lhsT, rhs, start=(k == 0), stop=(k == KD - 1))
                mm.then_inc(z_done, 1)

            def turn_qk(n):
                pe.wait_ge(rot_ready, n + 1)
                take(pe, ("qk", n))
                for h in range(H):
                    mm = pe.transpose(bank(("qk", n))[:, h * P:(h + 1) * P], rot[:, n % 2, h * P:(h + 1) * P], ident)
                mm.then_inc(qk_turned, 1)

            def scores(h):
                for i in range(NT):
                    take(pe, ("s", h, i))
                    emptied(pe, ("qk", 7))
                    emptied(pe, ("qk", 6))
                    pe.matmul(bank(("s", h, i))[:, 0:S - i * P], kT[:, h, i * P:(i + 1) * P], qT[:, h, i * P:S],
                              start=True, stop=True).then_inc(scores_done, 1)

            def pv(h):
                pe.wait_ge(sT_ready, NT * (h + 1))
                for t in range(NT):
                    emptied(pe, ("z", 12 + t))
                take(pe, ("pv", h))
                for j in range(NT):
                    for i in range(j + 1):
                        off = 4 * i - i * (i - 1) // 2
                        mm = pe.matmul(bank(("pv", h))[:, j * P:(j + 1) * P],
                                       sT[:, h % 2, (off + j - i) * P:(off + j - i + 1) * P],
                                       v_sb[:, i, h * P:(h + 1) * P], start=(i == 0), stop=(i == j))
                mm.then_inc(pv_done, 1)

            for n in range(8):
                z(n)
                if n >= 2:
                    turn_qk(n - 2)
            z(8)
            turn_qk(6)
            z(9)
            turn_qk(7)
            z(10)
            pe.wait_ge(dec_loaded, 16)
            scores(0)
            z(11)
            scores(1)
            for n in range(12, 16):
                z(n)
            for h in range(H):
                pv(h)
                if h < 2:
                    scores(h + 2)
                z(16 + h)
            for h in range(H):
                pe.wait_ge(mixtok_ready, h + 1)
                take(pe, ("mix", h))
                for j in range(NT):
                    mm = pe.transpose(bank(("mix", h))[:, j * P:(j + 1) * P], mixtok[:, h, j * P:(j + 1) * P], ident)
                mm.then_inc(mix_turned, 1)
            pe.wait_ge(wpool_loaded, 16)
            for n, g in enumerate(reversed(range(H))):
                pe.wait_ge(pooled_ready, n + 1)
                take(pe, ("pool", n))
                pe.matmul(bank(("pool", n)), wp_sb[:, g, :], pT[:, g, PADS:PADS + S], start=True, stop=True)\
                    .then_inc(pool_done, 1)

            for h in range(H):
                emptied(pe, ("mix", h))
            for c in range(2):
                pe.wait_ge(wout_loaded[c], 16)

            def project(m):
                t, half = m // 2, m % 2
                take(pe, ("out", m))
                for k in range(KD):
                    if m == 0 and k == H:
                        for n in range(H):
                            emptied(pe, ("pool", n))
                    mm = pe.matmul(bank(("out", m)), mixT[:, k, t * P:(t + 1) * P],
                                   wout(k)[:, half * 512:(half + 1) * 512], start=(k == 0), stop=(k == KD - 1))
                mm.then_inc(out_done, 1)

            def turn_h2(t):
                pe.wait_ge(xn2_ready, t + 1)
                for k in range(KD):
                    if k % 4 == 0:
                        take(pe, ("h2", t, k // 4))
                    mm = pe.transpose(bank(("h2", t, k // 4))[:, (k % 4) * P:(k % 4 + 1) * P],
                                      xn2[:, t % 2, k * P:(k + 1) * P], ident)
                mm.then_inc(h2_turned, 1)

            def route(t):
                emptied(pe, ("h2", t, 0))
                emptied(pe, ("h2", t, 1))
                pe.wait_ge(router_loaded, 32)
                take(pe, ("log", t, 0))
                for k in range(KD):
                    mm = pe.matmul(bank(("log", t, 0))[:, 0:E], h2T[:, t % 2, k, :], wr_sb[:, k, :],
                                   start=(k == 0), stop=(k == KD - 1))
                mm.then_inc(logits_done, 1)

            for t in range(NT):
                project(2 * t)
                if t >= 1:
                    turn_h2(t - 1)
                project(2 * t + 1)
                if t >= 1:
                    route(t - 1)
            turn_h2(3)
            route(3)
            take(pe, ("pos", 0))
            pe.wait_ge(consts_made, 3)
            pe.wait_ge(chosen_ready, NT)
            pos = bank(("pos", 0))
            for t in range(NT + 1):
                for i in range(min(t + 1, NT)):
                    mm = pe.matmul(pos[:, t * E:(t + 1) * E], (tri if i == t else ones)[:, :], chosen_b[:, i, :],
                                   start=(i == 0), stop=(i == min(t, NT - 1)))
            mm.then_inc(pos_done, 1)

            def gather(e, i):
                pe.wait_ge(onehot_ready, e + 1)
                pe_gather(pe, i).then_inc(gathered, 1)

            for b in range(8):
                pe.wait_ge(bank_free[b], uses[b])
            pe.wait_ge(parts_ready, NT)
            gather(0, 1)
            gather(0, 0)

            def turn_rows(e):
                pe.wait_ge(yT_ready, 2 * e + 2)
                pe_turn_rows(pe).then_inc(row_turned, 1)

            def expert(e, first=False, last=False):
                pe.wait_ge(xT_ready, 2 * e + 2)
                if not first:
                    pe.wait_ge(gu_taken, GB * e)
                for k in range(KD):
                    split_done(pe, e, k)
                    for b in range(GB):
                        mm = pe_gu(pe, k, b)
                        if k == KD - 1:
                            mm.then_inc(gu_done, 1)
                    if k < KD - 1:
                        mm.then_inc(chunk_used, 1)
                    if k == 2 and not first:
                        turn_rows(e - 1)
                if not last:
                    gather(e + 1, 1)
                    if not first:
                        pe.wait_ge(row_ready, 2 * e)
                    gather(e + 1, 0)
                for f in range(KD):
                    if f % 2 == 0:
                        pe.wait_ge(act_ready, GB * e + f // 2 + 1)
                        split_done(pe, e, GU_CH + f // 2)
                    if f == 0 and not last:
                        pe.wait_ge(xT_ready, 2 * e + 3)
                    mm = pe_down(pe, f)
                    if f % 2 == 1 and f < KD - 1:
                        mm.then_inc(chunk_used, 1)
                    elif f == KD - 1:
                        mm.then_inc(y_done, 1)

            expert(0, first=True)
            with pe.Fori(1, E - 1) as e:
                expert(e)
            expert(E - 1, last=True)
            turn_rows(E - 1)

            pe.wait_ge(counts_ready, 1)
            pe.wait_ge(rows_stored, 16 * E)

            def one(e, b, n):
                pe.wait_ge(more["onehot"], n)
                for i in (1, 0):
                    pe_gather(pe, i).then_inc(more["gathered"], 1)
                pe.wait_ge(more["xT"], 2 * n)
                for k in range(KD):
                    pe.wait_ge(more["low"], CH * (n - 1) + k + 1)
                    for i in range(GB):
                        mm = pe_gu(pe, k, i)
                    mm.then_inc(more["used"], 1)
                for f in range(KD):
                    if f % 2 == 0:
                        pe.wait_ge(more["act"], GB * n - GB + f // 2 + 1)
                        pe.wait_ge(more["low"], CH * (n - 1) + GU_CH + f // 2 + 1)
                    mm = pe_down(pe, f)
                    if f % 2 == 1:
                        mm.then_inc(more["used"], 1)
                pe.wait_ge(more["yT"], 2 * n)
                pe_turn_rows(pe).then_inc(more["turned"], 1)
                pe.wait_ge(more["stored"], 16 * n)

            def skip():
                pe.sem_inc(more["gathered"], 2)
                pe.sem_inc(more["used"], CH)
                pe.sem_inc(more["turned"], 1)

            further_blocks(pe, one, skip)

            pe.wait_ge(routed, 1)
            pe.wait_ge(row_ready, 2 * E)
            for t in range(NT):
                mm = pe.transpose(ps[0:E, 4, t * P:(t + 1) * P], gdense[:, t, :], ident)
            mm.then_inc(gd_turned, 1)
            pe.wait_ge(gdT_ready, 1)
            pe.wait_ge(tail_loaded, 32)
            order = [0, 1, 2, 3, 5, 6, 7, 4]
            for m in range(2 * NT):
                t, half = m // 2, m % 2
                pe.matmul(ps[:, order[m], :], gdT[:, t * P:(t + 1) * P], bd_sb[:, half * 512:(half + 1) * 512],
                          start=True, stop=True).then_inc(bias_done, 1)

        @block.vector
        def _(dve):
            steps = [0]

            def step(ins):
                ins.then_inc(dve_step, 1)
                steps[0] += 1
                dve.wait_ge(dve_step, steps[0])

            def inverse_root(r, width, n):
                dve.wait_ge(ss_ready, r + 1)
                v, y, w = var[:, r, 0:width], rstd[:, r, 0:width], nwt[:, 0:width]
                step(dve.tensor_scalar(v, ss[:, r, 0:width], 1.0 / n, EPS, ALU.mult, ALU.add))
                dve.wait_ge(std_ready, r + 1)
                step(dve.reciprocal(y, std[:, r, 0:width]))
                step(dve.tensor_tensor(w, y, y, ALU.mult))
                step(dve.scalar_tensor_tensor(w, w, -0.5, v, ALU.mult, ALU.mult))
                step(dve.scalar_tensor_tensor(y, w, 1.5, y, ALU.add, ALU.mult))

            dve.memset(eps_t[:, :], EPS).then_inc(consts_made, 1)
            dve.wait_ge(small_loaded, 16)
            dve.tensor_copy(tri[:, :], tri_f).then_inc(consts_made, 1)
            dve.wait_ge(norms_loaded, 32)

            def hT_tile(t):
                dve.wait_ge(x_turned, t + 1)
                for i in range(2):
                    ins = dve.tensor_tensor(
                        hT[:, 4 * i:4 * i + 4, t * P:(t + 1) * P], bank(("x", t, i)).rearrange("p (k c) -> p k c", k=4),
                        nm_w[:, 4 * i:4 * i + 4].unsqueeze(2).to_broadcast([P, 4, P]), ALU.mult)
                    free(ins, ("x", t, i))
                emptied(dve, ("x", t, 0))
                emptied(dve, ("x", t, 1))
                dve.sem_inc(hT_ready, 1)

            for t in range(NT):
                inverse_root(t, 1, D)
                dve.tensor_scalar(xn1[:, t % 2], x_sb[:, t, :], rstd[:, t, 0:1], None, ALU.mult).then_inc(xn_ready, 1)
                if t == 0:
                    for j in range(4):
                        dve.wait_ge(bgu_turned, j + 1)
                        dst = bguT[:, :, :].rearrange("p e (ql b qh r) -> p e qh ql b r", ql=2, b=2, qh=2)[
                            :, :, :, :, j // 2, j % 2]
                        ins = dve.tensor_copy(dst, bank(("bgu", j))[:, 0:P].rearrange(
                            "p (e qh ql) -> p e qh ql", e=E, qh=2))
                        free(ins, ("bgu", j))
                if t >= 1:
                    hT_tile(t - 1)
            hT_tile(NT - 1)

            def rotate(n):
                t = n % 4
                dve.wait_ge(z_done, n + 1)
                if n >= 2:
                    dve.wait_ge(qk_turned, n - 1)
                    dve.wait_ge(rot_ready, n - 1)
                zz = bank(("z", n)).rearrange("p (h c) -> p h c", h=H)
                dst = rot[:, n % 2].rearrange("p (h c) -> p h c", h=H)
                tmp = sT[:, n % 2, 0:512].rearrange("p (h c) -> p h c", h=H)
                cb = rope_c[:, t, :].unsqueeze(1).to_broadcast([P, H, P])
                sb_ = rope_s[:, t, :].unsqueeze(1).to_broadcast([P, H, P])
                dve.tensor_tensor(dst, zz, cb, ALU.mult)
                dve.tensor_tensor(tmp[:, :, 0:64], zz[:, :, 64:128], sb_[:, :, 0:64], ALU.mult)
                ins = dve.tensor_tensor(tmp[:, :, 64:128], zz[:, :, 0:64], sb_[:, :, 64:128], ALU.mult)
                free(ins, ("z", n))
                emptied(dve, ("z", n))
                dve.tensor_tensor(dst, dst, tmp, ALU.add).then_inc(rot_ready, 1)

            def silu(t):
                dve.wait_ge(sig_gate, t + 1)
                ins = dve.tensor_tensor(gate_sb[:, t, :], bank(("z", 8 + t)), gate_sb[:, t, :], ALU.mult)
                free(ins, ("z", 8 + t))
                emptied(dve, ("z", 8 + t))
                dve.sem_inc(silu_ready, 1)

            def decayed(h):
                if h >= 2:
                    dve.wait_ge(pv_done, h - 1)
                off = 0
                for i in range(NT):
                    n = S - i * P
                    dve.wait_ge(scores_done, NT * h + i + 1)
                    ins = dve.tensor_tensor(sT[:, h % 2, off:off + n], bank(("s", h, i))[:, 0:n], dec[:, h, 0:n], ALU.mult)
                    free(ins, ("s", h, i))
                    off += n
                emptied(dve, ("s", h, 3))
                dve.sem_inc(sT_ready, NT)

            def head_norm(h):
                inverse_root(4 + h, NT, P)
                dve.wait_ge(gate_ready, NT)
                for j in range(NT):
                    ins = dve.scalar_tensor_tensor(
                        mixtok[:, h, j * P:(j + 1) * P], bank(("pv", h))[:, j * P:(j + 1) * P], rstd[:, 4 + h, j:j + 1],
                        gate_sb[:, j, h * P:(h + 1) * P], ALU.mult, ALU.mult)
                free(ins, ("pv", h))
                emptied(dve, ("pv", h))
                dve.sem_inc(mixtok_ready, 1)

            dve.wait_ge(rope_loaded, 16)
            for n in range(8):
                rotate(n)
            dve.wait_ge(dec_loaded, 16)
            dve.wait_ge(rot_ready, 8)
            silu(0)
            silu(1)
            silu(2)
            decayed(0)
            silu(3)
            decayed(1)
            head_norm(0)
            decayed(2)
            head_norm(1)
            decayed(3)
            head_norm(2)
            head_norm(3)
            for n, g in enumerate(reversed(range(H))):
                dve.wait_ge(window_ready, n + 1)
                s = psum_a if g % 2 == 0 else psum_b
                dve.scalar_tensor_tensor(pT[:, g, PADS:PADS + S], s[:, PADS:PADS + S], 1.0 / WINDOWS[g],
                                         pT[:, g, PADS:PADS + S], ALU.mult, ALU.subtract).then_inc(pooled_ready, 1)

            def residual(t):
                for half in range(2):
                    m = 2 * t + half
                    dve.wait_ge(out_done, m + 1)
                    xs = x_sb[:, t, half * 512:(half + 1) * 512]
                    ins = dve.tensor_tensor(xs, bank(("out", m)), xs, ALU.add)
                    free(ins, ("out", m))
                for half in range(2):
                    emptied(dve, ("out", 2 * t + half))
                dve.sem_inc(x2_ready, 1)

            def normed(t):
                inverse_root(8 + t, 1, D)
                if t == 0:
                    dve.wait_ge(nf_loaded, 16)
                dve.scalar_tensor_tensor(xn2[:, t % 2], x_sb[:, t, :], rstd[:, 8 + t, 0:1], nf_row,
                                         ALU.mult, ALU.mult).then_inc(xn2_ready, 1)

            def low_part(t):
                dve.wait_ge(hi_ready, t + 1)
                dve.scalar_tensor_tensor(parts[:, 1, t, :], xn2[:, t % 2], SCALE_X, parts[:, 0, t, :],
                                         ALU.mult, ALU.subtract).then_inc(parts_ready, 1)
                dve.wait_ge(parts_ready, t + 1)

            def low(e, c):
                dve.wait_ge(high_ready, CH * e + c + 1)
                dve_low(dve, c).then_inc(low_ready, 1)

            def choose(t):
                dve.wait_ge(logits_done, t + 1)
                if t == 0:
                    dve.wait_ge(router_loaded, 32)
                ins = dve.tensor_tensor(logit[:, t, :], bank(("log", t, 0))[:, 0:E], br_sb[:, :], ALU.add)
                free(ins, ("log", t, 0))
                emptied(dve, ("log", t, 0))
                step(dve.max(top8[:, t, :], logit[:, t, :]))
                step(dve.max_index(idx8[:, t, :], top8[:, t, :], logit[:, t, :]))
                step(dve.tensor_copy(idxf[:, t, :], idx8[:, t, :]))
                step(dve.tensor_tensor(is_kth[:, t], iota32.unsqueeze(1).to_broadcast([P, TOP_K, E]),
                                       idxf[:, t, 0:TOP_K].unsqueeze(2).to_broadcast([P, TOP_K, E]), ALU.is_equal))
                step(dve.tensor_reduce(chosen[:, t, :], is_kth[:, t].rearrange("p k e -> p e k"), AX_X, ALU.add))
                dve.tensor_copy(chosen_b[:, t, :], chosen[:, t, :]).then_inc(chosen_ready, 1)
                dve.tensor_scalar(negmax[:, t:t + 1], top8[:, t, 0:1], -1.0, None, ALU.mult).then_inc(top_ready, 1)

            for c in range(3):
                low(0, c)
            for t in range(NT):
                residual(t)
                normed(t)
                low_part(t)
                if t >= 1:
                    choose(t - 1)
            low(0, 4)
            choose(3)
            low(0, 5)

            dve.wait_ge(pos_done, 1)
            pos = bank(("pos", 0))
            step(dve.scalar_tensor_tensor(rank1[:, :, :].rearrange("p e t -> p t e"),
                                          pos[:, 0:NT * E].rearrange("p (t e) -> p t e", t=NT), 1.0,
                                          chosen[:, :, :], ALU.add, ALU.mult))
            dve_onehot(dve, 0, 0).then_inc(onehot_ready, 1)
            step(dve.tensor_copy(count_i[:, :], pos[:, NT * E:(NT + 1) * E]))
            step(dve.tensor_reduce(count_max[:, :], pos[:, NT * E:(NT + 1) * E], AX_X, ALU.max))
            ins = dve.tensor_copy(count_max_i[:, :], count_max[:, :])
            step(ins)
            ins = dve.tensor_tensor(rank_row[:, :, :], rank1[:, :, :].rearrange("p e t -> p t e"),
                                    e_base.unsqueeze(1).to_broadcast([P, NT, E]), ALU.add)
            free(ins, ("pos", 0))
            emptied(dve, ("pos", 0))
            dve.sem_inc(counts_ready, 1)

            def rows_and_gates():
                for b in range(1, BLOCKS):
                    step(dve.tensor_scalar(passed_b[:, :, :], rank1[:, :, :].rearrange("p e t -> p t e"),
                                           float(b * CAP), float(FIRST - CAP), ALU.is_gt, ALU.mult))
                    step(dve.tensor_tensor(rank_row[:, :, :], rank_row[:, :, :], passed_b[:, :, :], ALU.add))
                every = [P, NT, TOP_K, E]
                step(dve.tensor_tensor(of_kth, is_kth, rank_row[:, :, :].unsqueeze(2).to_broadcast(every), ALU.mult))
                step(dve.tensor_reduce(row_f[:, :], of_kth.rearrange("p t k e -> p (t k) e"), AX_X, ALU.add))
                step(dve.tensor_copy(row_u[:, :], row_f[:, :]))
                dve.wait_ge(exp_ready, NT)
                step(dve.reciprocal(einv[:, :], esum[:, :]))
                step(dve.tensor_tensor(gates[:, :, :], expo[:, :, :], einv[:, :].unsqueeze(2).to_broadcast([P, NT, TOP_K]),
                                       ALU.mult))
                step(dve.tensor_tensor(of_kth, is_kth, gates[:, :, :].unsqueeze(3).to_broadcast(every), ALU.mult))
                step(dve.tensor_reduce(gdense[:, :, :], of_kth.rearrange("p t k e -> p t e k"), AX_X, ALU.add))
                dve.sem_inc(routed, 1)

            def bias_and_clamp(e, b, first):
                dve.wait_ge(gu_done, GB * e + b + 1)
                if b >= 2 or not first:
                    dve.wait_ge(sig_ready, GB * e + b - 1)
                    dve.wait_ge(prod_ready, GB * e + b - 1)
                dve_bias(dve, e, b).then_inc(gu_taken, 1)
                dve.wait_ge(gu_taken, GB * e + b + 1)
                dve_glu(dve, b).then_inc(glu_ready, 1)
                dve_lin(dve, b).then_inc(lin_ready, 1)
                dve.wait_ge(glu_ready, GB * e + b + 1)
                dve.wait_ge(lin_ready, GB * e + b + 1)
                if b >= 2 or not first:
                    dve.wait_ge(act32_ready, GB * e + b - 1)
                dve_prod(dve, b).then_inc(prod_ready, 1)

            def activate(e, b, first):
                dve.wait_ge(prod_ready, GB * e + b + 1)
                dve.wait_ge(sig_ready, GB * e + b + 1)
                if b >= 2 or not first:
                    dve.wait_ge(ah_ready, GB * e + b - 1)
                    dve.wait_ge(act_ready, GB * e + b - 1)
                dve_act32(dve, b).then_inc(act32_ready, 1)

            def act_low_part(e, b):
                dve.wait_ge(ah_ready, GB * e + b + 1)
                dve_al(dve, b).then_inc(act_ready, 1)

            def expert(e, first=False, last=False):
                if not last:
                    dve.wait_ge(gathered, 2 * e + 2)
                    dve_onehot(dve, e + 1, 0).then_inc(onehot_ready, 1)
                for c in range(RAW if first else 0, GU_CH + 1):
                    if c in BY_DVE:
                        low(e, c)
                bias_and_clamp(e, 0, first)
                bias_and_clamp(e, 1, first)
                activate(e, 0, first)
                bias_and_clamp(e, 2, first)
                activate(e, 1, first)
                act_low_part(e, 0)
                bias_and_clamp(e, 3, first)
                activate(e, 2, first)
                act_low_part(e, 1)
                activate(e, 3, first)
                act_low_part(e, 2)
                act_low_part(e, 3)
                for c in range(GU_CH + 1, CH):
                    if c in BY_DVE:
                        low(e, c)
                if last:
                    rows_and_gates()

            expert(0, first=True)
            with dve.Fori(1, E - 1) as e:
                expert(e)
            expert(E - 1, last=True)

            dve.wait_ge(rows_stored, 16 * E)

            def one(e, b, n):
                dve_onehot(dve, e, b * CAP).then_inc(more["onehot"], 1)
                for c in range(GU_CH):
                    dve.wait_ge(more["high"], CH * (n - 1) + c + 1)
                    dve_low(dve, c).then_inc(more["low"], 1)
                dve.wait_ge(more["used"], CH * (n - 1) + GU_CH)
                for i in range(GB):
                    base = GB * n - GB + i + 1
                    dve_bias(dve, e, i).then_inc(more["biased"], 1)
                    dve.wait_ge(more["biased"], base)
                    dve_lin(dve, i).then_inc(more["prod"], 1)
                    dve_glu(dve, i).then_inc(more["glu"], 1)
                    dve.wait_ge(more["prod"], 2 * base - 1)
                    dve.wait_ge(more["glu"], base)
                    dve_prod(dve, i).then_inc(more["prod"], 1)
                    dve.wait_ge(more["prod"], 2 * base)
                    dve.wait_ge(more["sig"], base)
                    dve_act32(dve, i).then_inc(more["act32"], 1)
                    dve.wait_ge(more["ah"], base)
                    dve_al(dve, i).then_inc(more["act"], 1)
                    dve.wait_ge(more["act"], base)
                for c in range(GU_CH, CH):
                    dve.wait_ge(more["high"], CH * (n - 1) + c + 1)
                    dve_low(dve, c).then_inc(more["low"], 1)
                dve.wait_ge(more["stored"], 16 * n)

            def skip():
                dve.sem_inc(more["onehot"], 1)
                dve.sem_inc(more["low"], CH)
                dve.sem_inc(more["prod"], 2 * GB)
                for k in ("biased", "glu", "act32", "act"):
                    dve.sem_inc(more[k], GB)

            further_blocks(dve, one, skip)

            order = [0, 1, 2, 3, 5, 6, 7, 4]
            for m in range(2 * NT):
                t, half = m // 2, m % 2
                dve.wait_ge(bias_done, m + 1)
                xs = x_sb[:, t, half * 512:(half + 1) * 512]
                ins = dve.tensor_tensor(xs, ps[:, order[m], :], xs, ALU.add)
            step(ins)
            dve.wait_ge(tail_loaded, 32)
            for t in range(NT):
                dve.wait_ge(got_rows[t], 16 * TOP_K)
                for k in range(TOP_K):
                    ins = dve.scalar_tensor_tensor(x_sb[:, t, :], got[:, t * TOP_K + k, :], gates[:, t, k:k + 1],
                                                   x_sb[:, t, :], ALU.mult, ALU.add)
                    if k < TOP_K - 1:
                        step(ins)
                    else:
                        ins.then_inc(acc_ready, 1)
                inverse_root(12 + t, 1, D)
                dve.scalar_tensor_tensor(o_row[:, t, :], x_sb[:, t, :], rstd[:, 12 + t, 0:1], fin_w,
                                         ALU.mult, ALU.mult).then_inc(out_ready, 1)


_INS = ['x', 'norm_mix_w', 'w_in', 'ret_norm_w', 'w_pool', 'pool_scale', 'w_out', 'norm_ffn_w', 'w_router',
        'b_router', 'w_gu', 'b_gu', 'w_down', 'b_down', 'norm_final_w']


def shape_constants(seq):
    import numpy as np
    half = P // 2
    inv = np.power(np.float32(10000.0), -np.arange(half, dtype=np.float32) / np.float32(half), dtype=np.float32)
    ang = np.arange(seq, dtype=np.float32)[:, None] * inv[None, :]
    c, s = np.cos(ang.astype(np.float64)), np.sin(ang.astype(np.float64))
    nt = seq // P
    cc = np.concatenate([c, c], 1).reshape(nt, P, P).transpose(1, 0, 2).reshape(P, -1)
    sn = np.concatenate([-s, s], 1).reshape(nt, P, P).transpose(1, 0, 2).reshape(P, -1)
    rope = np.concatenate([cc, sn], 1).astype(np.float32)

    m, n = np.arange(P)[:, None], np.arange(seq)[None, :]
    seen = (n // CHUNK) >= (m // CHUNK)
    heads = []
    for h in range(4):
        log_g = np.log1p(-np.exp2(-5.0 - h))
        heads.append(np.where(seen, np.exp(log_g * np.abs(n - m)), 0.0) * P ** -0.5)
    decay = np.concatenate(heads, 1).astype(np.float32)

    blocks = -(-seq // CAP)
    small = np.zeros((P, 384 + blocks * CAP), np.float32)
    small[:, 0:128] = np.eye(P)
    small[:, 128:256] = np.triu(np.ones((P, P)), 1)
    small[:, 256:288] = np.arange(32)
    small[:, 288:320] = CAP * np.arange(32) - 1
    for g, w in enumerate(WINDOWS):
        small[:, 320 + 16 * g:336 + 16 * g] = w / np.minimum(np.arange(16) + 1, w)
    small[:, 384:] = np.arange(blocks * CAP) + 1
    return {"rope": rope, "decay": decay, "small": small}


def kernel(**inputs):
    import numpy as _np
    import concourse.bacc as _bacc
    from concourse import mybir as _mybir
    from concourse.bass_utils import run_bass_kernel_spmd as _run

    nc = _bacc.Bacc("TRN2", target_bir_lowering=False, num_devices=1)
    arrays, args = {}, []
    for name in _INS:
        a = _np.ascontiguousarray(inputs[name])
        arrays[f"in_{name}_dram"] = a
        args.append(nc.dram_tensor(f"in_{name}_dram", a.shape, _mybir.dt.from_np(a.dtype), kind="ExternalInput").ap())
    for name, a in shape_constants(inputs["x"].shape[1]).items():
        arrays[f"const_{name}_dram"] = a
        args.append(nc.dram_tensor(f"const_{name}_dram", a.shape, _mybir.dt.from_np(a.dtype), kind="ExternalInput").ap())
    shape = inputs["x"].shape
    args.append(nc.dram_tensor("out_0_dram", shape, _mybir.dt.float32, kind="ExternalOutput").ap())
    build_program(nc, *args)
    r = _run(nc, [arrays], core_ids=[0])
    return r.results[0]["out_0_dram"]
```

```python
from contextlib import ExitStack

import concourse.bass as bass
from concourse import mybir

ALU = mybir.AluOpType
ACT = mybir.ActivationFunctionType
AX_X = mybir.AxisListType.X
F32 = mybir.dt.float32
BF16 = mybir.dt.bfloat16
F16 = mybir.dt.float16
I32 = mybir.dt.int32
U32 = mybir.dt.uint32

P = 128
CAP = 88
EPS = 1e-6
TOP_K = 4
WINDOWS = (2, 4, 8, 16)
LIMIT = 7.0
ALPHA = 1.702
CHUNK = 64
SCALE_X = 16.0
SCALE_W = 32.0
SCALE_A = 64.0
UNSCALE = 1.0 / (SCALE_X * SCALE_W)


def build_program(nc, x, norm_mix_w, w_in, ret_norm_w, w_pool, pool_scale, w_out, norm_ffn_w, w_router,
                  b_router, w_gu, b_gu, w_down, b_down, norm_final_w, rope, decay, small, out):
    _, S, D = x.shape
    E = w_router.shape[2]
    F = w_down.shape[2]
    NT = S // P
    KD = D // P
    W = w_in.shape[2] // 5
    H = W // P
    NF = 2 * F // P
    BLOCKS = -(-S // CAP)
    RANKS = BLOCKS * CAP
    FIRST = E * CAP
    GU_CH = KD
    DN_CH = F // P // 2
    CH = GU_CH + DN_CH
    RAW = CH // 2
    BY_POOL = (3, 9)
    BY_DVE = tuple(c for c in range(CH) if c not in BY_POOL)
    SLOT = 2 * F
    GB = 4
    PER = NF // GB
    assert D == F and W == 512 and H == 4 and NT == 4 and GU_CH == 8 and S == 512 and PER * CAP <= 512 and CAP <= P - E

    y_rows = nc.dram_tensor("y_rows", [BLOCKS * FIRST, D], F32, kind="Internal").ap()

    with ExitStack() as ctx:
        def sb(name, shape, dt=F32):
            return ctx.enter_context(nc.sbuf_tensor(name, shape, dt))

        def sem(name):
            return ctx.enter_context(nc.semaphore(name))

        ring = sb("ring", [P, CH, SLOT])
        arena = sb("arena", [P, 24160])
        at = [0]

        def region(cols):
            at[0] += cols
            return arena[:, at[0] - cols:at[0]]

        x_sb = region(NT * D).rearrange("p (t d) -> p t d", t=NT)
        reg_h = region(KD * S)
        reg_vg = region(2048 + 2048 + 2560)
        reg_d = region(2048)
        reg_r = region(2048)
        reg_p = region(2112 + 1056 + 2048)

        hT = reg_h.bitcast(F16).rearrange("p (i k s) -> p i k s", i=2, k=KD)
        mixT = reg_h.rearrange("p (k s) -> p k s", k=KD)
        v_sb = reg_vg[:, 0:2048].rearrange("p (t c) -> p t c", t=NT)
        gate_sb = reg_vg[:, 2048:4096].rearrange("p (t c) -> p t c", t=NT)
        sT = reg_vg[:, 4096:6656].rearrange("p (b c) -> p b c", b=2)
        xn1 = reg_vg[:, 0:2048].rearrange("p (b c) -> p b c", b=2)
        h32 = reg_vg[:, 2048:4096].rearrange("p (b k c) -> p b k c", b=2, k=KD)
        dec = reg_d.rearrange("p (h c) -> p h c", h=H)
        rope_c = reg_r[:, 0:512].rearrange("p (t c) -> p t c", t=NT)
        rope_s = reg_r[:, 512:1024].rearrange("p (t c) -> p t c", t=NT)
        rot = reg_r[:, 1024:2048].rearrange("p (b c) -> p b c", b=2)
        PADS = 16
        pT = reg_p[:, 0:2112].rearrange("p (g c) -> p g c", g=H)
        psum_a = reg_p[:, 2112:2112 + 528]
        psum_b = reg_p[:, 2640:2640 + 528]
        mixtok = reg_p[:, 3168:5216].rearrange("p (h c) -> p h c", h=H)
        qT = ring[:, 10, :].rearrange("p (h s) -> p h s", h=H)
        kT = ring[:, 11, :].rearrange("p (h s) -> p h s", h=H)
        bgu_raw = mixtok[:, 0, :]
        parts = reg_vg[:, 0:4096].bitcast(F16).rearrange("p (i t d) -> p i t d", i=2, t=NT)
        nf_row = reg_vg[:, 4096:5120]
        h2T = reg_d.rearrange("p (b k c) -> p b k c", b=2, k=KD)
        xn2 = reg_r.rearrange("p (b c) -> p b c", b=2)
        xT = reg_h[:, 0:KD * CAP].bitcast(F16).rearrange("p (i k c) -> p i k c", i=2, k=KD)
        actT = reg_h[:, 768:768 + KD * CAP].bitcast(F16).rearrange("p (i k c) -> p i k c", i=2, k=KD)
        act32 = reg_d[:, 0:PER * CAP].rearrange("p (b c) -> p b c", b=2)
        yT = reg_h[:, 1536:1536 + KD * CAP].rearrange("p (k c) -> p k c", k=KD)
        gub = reg_h[:, 2304:2304 + 2 * PER * CAP].rearrange("p (b h c) -> p b h c", b=2, h=2)
        prod = reg_h[:, 3072:3072 + PER * CAP].rearrange("p (b c) -> p b c", b=2)
        sig = reg_h[:, 3456:3456 + PER * CAP].rearrange("p (b c) -> p b c", b=2)
        zeros = reg_p[:, 0:1024]
        y_row = reg_p[:, 1024:2048]
        onehot = reg_p[:, 2048:2048 + NT * CAP // 2].bitcast(F16).rearrange("p (t c) -> p t c", t=NT)
        is_kth = reg_p[:, 2304:2816].rearrange("p (t k e) -> p t k e", t=NT, k=TOP_K)
        of_kth = reg_p[:, 2816:3328].rearrange("p (t k e) -> p t k e", t=NT, k=TOP_K)
        def got(t):
            if t == 0:
                return reg_vg[:, 0:4096].rearrange("p (k d) -> p k d", k=TOP_K)
            s = (0, 2, 8)[t - 1]
            return ring[:, s:s + 2, :].rearrange("p s (a d) -> p (s a) d", a=2)

        o_row = ring[:, 4:6, :].rearrange("p s (a d) -> p (s a) d", a=2)
        BD = P - E
        y_last = reg_p[:, 3328:4352]
        wg = reg_p[:, 4352:4352 + NT * P].rearrange("p (t c) -> p t c", t=NT)
        gdense = wg[:, :, BD:P]
        wgT = reg_d[:, 512:512 + S]
        fin_w = reg_r[:, 0:1024]

        sm = sb("sm", [P, small.shape[1]])
        ident = sm[:, 0:128]
        tri_f = sm[:, 128:256]
        iota32 = sm[:, 256:288]
        e_base = sm[:, 288:320]
        corr = sm[:, 320:384].rearrange("p (g c) -> p g c", g=H)
        ranks = sm[:, 384:384 + RANKS]
        tri = sb("tri", [P, P], BF16)
        ones = sb("ones", [P, P], BF16)
        wp_sb = sb("wp_sb", [P, H, P])
        wr_sb = sb("wr_sb", [P, KD, E])
        br_sb = sb("br_sb", [P, E])
        rw_sb = sb("rw_sb", [P, W])
        bguT = sb("bguT", [P, E, NF])
        nm_w = sb("nm_w", [P, KD])
        ps_w = sb("ps_w", [P, H])
        eps_t = sb("eps_t", [P, 1])
        ss = sb("ss", [P, 16, 4])
        var = sb("var", [P, 16, 4])
        std = sb("std", [P, 16, 4])
        rstd = sb("rstd", [P, 16, 4])
        nwt = sb("nwt", [P, 4])
        logit = sb("logit", [P, NT, E])
        top8 = sb("top8", [P, NT, 8])
        idx8 = sb("idx8", [P, NT, 8], U32)
        idxf = sb("idxf", [P, NT, 8])
        negmax = sb("negmax", [P, NT])
        expo = sb("expo", [P, NT, TOP_K])
        esum = sb("esum", [P, NT])
        einv = sb("einv", [P, NT])
        gates = sb("gates", [P, NT, TOP_K])
        chosen = sb("chosen", [P, NT, E])
        chosen_b = sb("chosen_b", [P, NT, E], BF16)
        rank1 = sb("rank1", [P, E, NT])
        rank_row = sb("rank_row", [P, NT, E])
        passed_b = sb("passed_b", [P, NT, E])
        row_f = sb("row_f", [P, NT * TOP_K])
        row_u = sb("row_u", [P, NT * TOP_K], U32)
        fetch_gates = sb("fetch_gates", [P, NT, TOP_K])
        past_first = sb("past_first", [P, NT])
        count_i = sb("count_i", [P, E], I32)
        count_max = sb("count_max", [P, 1])
        count_max_i = sb("count_max_i", [P, 1], I32)

        ps = ctx.enter_context(nc.psum_tensor("ps", [P, 8, 512], F32))

        wide = [("z", n) for n in range(16)]
        for h in range(H):
            wide += [("pv", h), ("z", 16 + h)]
        wide += [("pool", g) for g in range(H)] + [("out", m) for m in range(2 * NT)]
        turned = [("bgu", j) for j in range(4)] + [("x", t, i) for t in range(NT) for i in range(2)]
        turned += [("qk", n) for n in range(8)]
        turned += [("s", h, i) for h in range(H) for i in range(NT)]
        turned += [("mix", h) for h in range(H)]
        for t in range(NT - 1):
            turned += [("h2", t, 0), ("h2", t, 1), ("log", t, 0), ("log", t, 1)]
        turned += [("h2", 3, 0), ("h2", 3, 1), ("log", 3, 0), ("pos", 0)]
        bank_of, turn_of = {}, {}
        for first, order in ((0, wide), (4, turned)):
            for n, key in enumerate(order):
                bank_of[key], turn_of[key] = first + n % 4, n // 4
        empty = {key for key in turned if key[0] == "log" and key[2] == 1}
        uses = [0] * 8
        for key in wide + turned:
            if key not in empty:
                turn_of[key] = uses[bank_of[key]]
                uses[bank_of[key]] += 1
        bank_free = [sem(f"bank_free{b}") for b in range(8)]

        def bank(key):
            return ps[:, bank_of[key], :]

        def take(pe, key):
            if turn_of[key]:
                pe.wait_ge(bank_free[bank_of[key]], turn_of[key])

        def emptied(eng, key):
            eng.wait_ge(bank_free[bank_of[key]], turn_of[key] + 1)

        def free(ins, key):
            ins.then_inc(bank_free[bank_of[key]], 1)

        x_loaded = [sem(f"x_loaded{t}") for t in range(NT)]
        win_loaded = [sem(f"win_loaded{c}") for c in range(5)]
        wout_loaded = [sem(f"wout_loaded{c}") for c in range(2)]
        small_loaded = sem("small_loaded")
        rope_loaded = sem("rope_loaded")
        dec_loaded = sem("dec_loaded")
        norms_loaded = sem("norms_loaded")
        wpool_loaded = sem("wpool_loaded")
        router_loaded = sem("router_loaded")
        bgu_loaded = sem("bgu_loaded")
        rw_loaded = sem("rw_loaded")
        consts_made = sem("consts_made")
        bgu_turned = sem("bgu_turned")
        ss_ready = sem("ss_ready")
        std_ready = sem("std_ready")
        xn_ready = sem("xn_ready")
        x_turned = sem("x_turned")
        hT_ready = sem("hT_ready")
        z_done = sem("z_done")
        win_high = sem("win_high")
        win_low = sem("win_low")
        win_scaled = sem("win_scaled")
        win_pool_low = sem("win_pool_low")
        h32_ready = sem("h32_ready")
        h_high = sem("h_high")
        rot_ready = sem("rot_ready")
        qk_turned = sem("qk_turned")
        sig_gate = sem("sig_gate")
        silu_ready = sem("silu_ready")
        gate_ready = sem("gate_ready")
        pad_ready = sem("pad_ready")
        scores_done = sem("scores_done")
        sT_ready = sem("sT_ready")
        pv_done = sem("pv_done")
        mixtok_ready = sem("mixtok_ready")
        mix_turned = sem("mix_turned")
        pool_step = sem("pool_step")
        window_ready = sem("window_ready")
        pooled_ready = sem("pooled_ready")
        pool_done = sem("pool_done")
        out_done = sem("out_done")
        x2_ready = sem("x2_ready")
        xn2_ready = sem("xn2_ready")
        hi_ready = sem("hi_ready")
        parts_ready = sem("parts_ready")
        h2_turned = sem("h2_turned")
        logits_done = sem("logits_done")
        top_ready = sem("top_ready")
        exp_ready = sem("exp_ready")
        chosen_ready = sem("chosen_ready")
        pos_done = sem("pos_done")
        dve_step = sem("dve_step")
        routed = sem("routed")
        nf_loaded = sem("nf_loaded")
        counts_ready = sem("counts_ready")
        slot_loaded = [sem(f"slot_loaded{s}") for s in range(RAW)]
        high_ready = sem("high_ready")
        low_ready = sem("low_ready")
        scaled_ready = sem("scaled_ready")
        pool_low_ready = sem("pool_low_ready")
        act32_ready = sem("act32_ready")
        ah_ready = sem("ah_ready")
        chunk_used = sem("chunk_used")
        onehot_ready = sem("onehot_ready")
        gathered = sem("gathered")
        xT_ready = sem("xT_ready")
        gu_done = sem("gu_done")
        gu_taken = sem("gu_taken")
        glu_ready = sem("glu_ready")
        lin_ready = sem("lin_ready")
        prod_ready = sem("prod_ready")
        sig_ready = sem("sig_ready")
        act_ready = sem("act_ready")
        y_done = sem("y_done")
        yT_ready = sem("yT_ready")
        row_turned = sem("row_turned")
        row_ready = sem("row_ready")
        rows_stored = sem("rows_stored")
        more = {k: sem(f"more_{k}") for k in ("high", "low", "used", "onehot", "gathered", "xT", "biased",
                                              "glu", "prod", "sig", "act32", "ah", "act", "yT", "turned",
                                              "row", "stored")}
        more_loaded = [sem(f"more_loaded{s}") for s in range(RAW)]
        passed = sem("passed")
        zeros_ready = sem("zeros_ready")
        cleared = sem("cleared")
        tail_loaded = sem("tail_loaded")
        wg_turned = sem("wg_turned")
        wgT_ready = sem("wgT_ready")
        pad_cleared = sem("pad_cleared")
        bias_done = sem("bias_done")
        got_rows = [sem(f"got_rows{n}") for n in range(NT * TOP_K)]
        acc_ready = sem("acc_ready")
        out_ready = sem("out_ready")
        out_stored = sem("out_stored")

        xt_d = x[0].rearrange("(t p) d -> p t d", p=P)
        out_d = out[0].rearrange("(t p) d -> p t d", p=P)
        win_cols = [0, 1, 3, 2, 4]

        WIN_RAW = (0, 2, 4, 0, 2)
        WIN_SPLIT = (6, 8, 6, 8, 0)

        def win(c):
            return ring[:, WIN_RAW[c]:WIN_RAW[c] + 2, :].rearrange("p s c -> p (s c)")

        def win_split(c):
            return ring[:, WIN_SPLIT[c]:WIN_SPLIT[c] + 2, :].bitcast(F16)

        def win_half(a, half):
            return a[..., half * KD * W // 2:(half + 1) * KD * W // 2]

        def wout(k):
            j = (k + 4) % 8
            return ring[:, 4 + j // 2, (j % 2) * D:(j % 2 + 1) * D]

        def load_chunk(sp, c, e):
            dst = ring[:, c % RAW, :]
            if c < GU_CH:
                return sp.dma_start(dst, w_gu[0, bass.ds(e, 1), c * P:(c + 1) * P, :].rearrange("a p c -> (a p) c"))
            r = (c - GU_CH) * 2 * P
            src = w_down[0, bass.ds(e, 1), r:r + 2 * P, :].rearrange("a (j p) c -> p (a j) c", p=P)
            return sp.dma_start(dst.rearrange("p (j c) -> p j c", j=2), src)

        def split_of(c):
            return ring[:, RAW + (c + 2) % RAW, :].bitcast(F16).rearrange("p (i c) -> p i c", i=2)

        def act_high(act, c):
            return act.activation(split_of(c)[:, 0, :], ring[:, c % RAW, :], ACT.Copy, scale=SCALE_W)

        def dve_low(dve, c):
            return dve.scalar_tensor_tensor(split_of(c)[:, 1, :], ring[:, c % RAW, :], SCALE_W,
                                            split_of(c)[:, 0, :], ALU.mult, ALU.subtract)

        def act_scale(act, c):
            return act.activation(ring[:, c % RAW, :], ring[:, c % RAW, :], ACT.Copy, scale=SCALE_W)

        def act_scaled_high(act, c):
            return act.activation(split_of(c)[:, 0, :], ring[:, c % RAW, :], ACT.Copy)

        def pool_low(pool, c):
            return pool.tensor_tensor(split_of(c)[:, 1, :], ring[:, c % RAW, :], split_of(c)[:, 0, :], ALU.subtract)

        def split_done(eng, e, c):
            if c in BY_POOL:
                eng.wait_ge(pool_low_ready, len(BY_POOL) * e + BY_POOL.index(c) + 1)
            else:
                eng.wait_ge(low_ready, len(BY_DVE) * e + BY_DVE.index(c) + 1)

        def chunk_gone(eng, e, c):
            if c < GU_CH - 1:
                eng.wait_ge(chunk_used, (CH - 2) * e + c + 1)
            elif c == GU_CH - 1:
                eng.wait_ge(gu_done, GB * e + GB)
            elif c < CH - 1:
                eng.wait_ge(chunk_used, (CH - 2) * e + c)
            else:
                eng.wait_ge(y_done, e + 1)

        MISC = ps[:, 6:8, :]
        GU = ps[:, 0:4, 0:PER * CAP]
        YT = ps[:, 4:6, 0:4 * CAP]

        def pe_gather(pe, i):
            for d in range(KD):
                o = (MISC if i == 0 else YT)[:, d // 4, (d % 4) * CAP:(d % 4 + 1) * CAP]
                for t in range(NT):
                    mm = pe.matmul(o, parts[:, i, t, d * P:(d + 1) * P], onehot[:, t, :],
                                   start=(t == 0), stop=(t == NT - 1), skip_group_check=True)
            return mm

        def product(pe, o, w, col, src, k, start, stop):
            for n, (i, j) in enumerate(((0, 0), (0, 1), (1, 0))):
                mm = pe.matmul(o, w[:, i, col:col + P], src[:, j, k, :], start=start and n == 0,
                               stop=stop and n == 2, skip_group_check=True)
            return mm

        def gu_tile(b, j):
            return 2 * b + j if j < 2 else NF // 2 + 2 * b + j - 2

        def pe_gu(pe, k, b):
            for j in range(PER):
                f = gu_tile(b, j)
                mm = product(pe, GU[:, b, j * CAP:(j + 1) * CAP], split_of(k), f * P, xT, k,
                             k == 0 and j == 0, k == KD - 1)
            return mm

        def pe_down(pe, f):
            for d in range(KD):
                mm = product(pe, YT[:, d // 4, (d % 4) * CAP:(d % 4 + 1) * CAP], split_of(GU_CH + f // 2),
                             (f % 2) * D + d * P, actT, f, f == 0 and d % 4 == 0, f == KD - 1)
            return mm

        def pe_turn_rows(pe):
            for d in range(KD):
                mm = pe.transpose(MISC[0:CAP, d // 4, (d % 4) * P:(d % 4 + 1) * P], yT[:, d, :], ident)
            return mm

        def dve_onehot(dve, e, first_rank):
            return dve.tensor_tensor(
                onehot, ranks[:, bass.ds(first_rank, CAP)].unsqueeze(1).to_broadcast([P, NT, CAP]),
                rank1[:, bass.ds(e, 1), :].rearrange("p a t -> p (a t)").unsqueeze(2).to_broadcast([P, NT, CAP]),
                ALU.is_equal)

        def act_xT(act, i):
            src = (MISC if i == 0 else YT)[:, :, 0:4 * CAP]
            return act.activation(xT[:, i].rearrange("p (a k) c -> p a (k c)", a=2), src, ACT.Copy)

        def dve_bias(dve, e, b):
            return dve.scalar_tensor_tensor(
                gub[:, b % 2].rearrange("p h (j c) -> p (h j) c", j=2),
                GU[:, b, :].rearrange("p (j c) -> p j c", j=PER), UNSCALE,
                bguT[:, bass.ds(e, 1), PER * b:PER * b + PER].rearrange("p a j -> p (a j)").unsqueeze(2)
                .to_broadcast([P, PER, CAP]), ALU.mult, ALU.add)

        def dve_glu(dve, b):
            return dve.tensor_scalar(gub[:, b % 2, 0], gub[:, b % 2, 0], LIMIT, None, ALU.min)

        def dve_lin(dve, b):
            return dve.tensor_scalar(gub[:, b % 2, 1], gub[:, b % 2, 1], LIMIT, -LIMIT, ALU.min, ALU.max)

        def dve_prod(dve, b):
            return dve.scalar_tensor_tensor(prod[:, b % 2], gub[:, b % 2, 1], 1.0, gub[:, b % 2, 0],
                                            ALU.add, ALU.mult)

        def dve_act32(dve, b):
            return dve.scalar_tensor_tensor(act32[:, b % 2], prod[:, b % 2], SCALE_A, sig[:, b % 2],
                                            ALU.mult, ALU.mult)

        def act_ah(act, b):
            return act.activation(actT[:, 0, 2 * b:2 * b + 2, :].rearrange("p j c -> p (j c)"), act32[:, b % 2], ACT.Copy)

        def dve_al(dve, b):
            return dve.tensor_tensor(actT[:, 1, 2 * b:2 * b + 2, :].rearrange("p j c -> p (j c)"), act32[:, b % 2],
                                     actT[:, 0, 2 * b:2 * b + 2, :].rearrange("p j c -> p (j c)"), ALU.subtract)

        def act_sig(act, b):
            return act.activation(sig[:, b % 2], gub[:, b % 2, 0], ACT.Sigmoid, scale=ALPHA)

        def act_yT(act, half):
            return act.activation(yT[:, 4 * half:4 * half + 4, :].rearrange("p k c -> p (k c)"),
                                  YT[:, half, :], ACT.Copy, scale=1.0 / (SCALE_A * SCALE_W))

        def act_row(act, half, rows=y_row):
            return act.activation(rows[0:CAP, half * 512:(half + 1) * 512], MISC[0:CAP, half, :], ACT.Copy)

        def store_rows(act, row):
            return act.dma_start(y_rows[bass.ds(row, CAP), :], y_row[0:CAP, :])

        def further_blocks(eng, block, skip_block, setup=None):
            most = eng.value_load(count_max_i[0:1, 0:1], min_val=0, max_val=S)
            with eng.If(most > CAP):
                if setup:
                    setup()
                with eng.Fori(0, E) as e:
                    c = eng.value_load(count_i[0:1, bass.ds(e, 1)], min_val=0, max_val=S)
                    with eng.Fori(1, BLOCKS) as b:
                        with eng.If(c > b * CAP):
                            block(e, b, e * (BLOCKS - 1) + b)
                            eng.sem_inc(passed, 1)
                        with eng.Else():
                            skip_block()
                        eng.nop()
                    eng.nop()
                eng.nop()
            with eng.Else():
                eng.nop()
            eng.nop()
            return most

        block = ctx.enter_context(nc.Block())

        @block.sync
        def _(sp):
            for t in range(NT):
                sp.dma_start(x_sb[:, t, :], xt_d[:, t, :]).then_inc(x_loaded[t], 16)
            for c in range(5):
                src = w_in[0, :, win_cols[c] * W:(win_cols[c] + 1) * W].rearrange("(k p) c -> p k c", p=P)
                if c == 3:
                    sp.wait_ge(win_low, 2)
                elif c == 4:
                    sp.wait_ge(win_low, 3)
                    sp.wait_ge(win_pool_low, 1)
                sp.dma_start(win(c).rearrange("p (k c) -> p k c", k=KD), src).then_inc(win_loaded[c], 16)
                if c == 1:
                    sp.dma_start(reg_r[:, 0:1024], rope).then_inc(rope_loaded, 16)
                    sp.dma_start(reg_d, decay).then_inc(dec_loaded, 16)
                    sp.dma_start(rw_sb[:, :], ret_norm_w[0:1, :].to_broadcast([P, W])).then_inc(rw_loaded, 16)
                    sp.dma_start(wp_sb[:, :, :], w_pool[0].rearrange("g c d -> c g d")).then_inc(wpool_loaded, 16)
                    sp.dma_start(wr_sb[:, :, :], w_router[0].rearrange("(k p) e -> p k e", p=P)).then_inc(router_loaded, 16)
                    sp.dma_start(br_sb[:, :], b_router[0:1, :].to_broadcast([P, E])).then_inc(router_loaded, 16)

            def expert0(chunks):
                for c in chunks:
                    load_chunk(sp, c, 0).then_inc(slot_loaded[c % RAW], 16)

            sp.wait_ge(win_low, 5)
            sp.dma_start(ring[:, 4:6, :].rearrange("p s (a c) -> p (s a) c", a=2),
                         w_out[0, W:2 * W, :].rearrange("(k p) c -> p k c", p=P)).then_inc(wout_loaded[1], 16)
            sp.wait_ge(z_done, 12)
            sp.dma_start(ring[:, 6:8, :].rearrange("p s (a c) -> p (s a) c", a=2),
                         w_out[0, 0:W, :].rearrange("(k p) c -> p k c", p=P)).then_inc(wout_loaded[0], 16)
            sp.wait_ge(win_low, 9)
            expert0((2, 3))
            sp.wait_ge(z_done, 20)
            expert0((0, 1))
            for c in (6, 7, 8, 9):
                split_done(sp, 0, c - RAW)
                expert0((c,))
            sp.wait_ge(out_done, 8)
            expert0((4, 5))
            for c in (10, 11):
                split_done(sp, 0, c - RAW)
                expert0((c,))
            with sp.Fori(1, E) as e:
                for c in range(CH):
                    split_done(sp, e if c >= RAW else e - 1, (c - RAW) % CH)
                    load_chunk(sp, c, e).then_inc(slot_loaded[c % RAW], 16)

            sp.wait_ge(counts_ready, 1)
            split_done(sp, E - 1, CH - 1)
            split_done(sp, E - 1, BY_POOL[-1])

            def one(e, b, n):
                for c in range(CH):
                    if c >= RAW:
                        sp.wait_ge(more["low"], CH * (n - 1) + c - RAW + 1)
                    load_chunk(sp, c, e).then_inc(more_loaded[c % RAW], 16)
                sp.wait_ge(more["stored"], 16 * n)

            def skip():
                for s in range(RAW):
                    sp.sem_inc(more_loaded[s], 32)

            def clear():
                sp.wait_ge(zeros_ready, 1)
                sp.dma_start(y_rows[FIRST:BLOCKS * FIRST, :].rearrange("(n p) d -> p n d", p=P),
                             zeros.unsqueeze(1).to_broadcast([P, (BLOCKS - 1) * FIRST // P, D])).then_inc(cleared, 16)
                sp.dma_start(y_rows[FIRST - CAP:FIRST, :], zeros[0:CAP, :]).then_inc(cleared, 16)

            further_blocks(sp, one, skip, clear)

            for t in range(NT):
                sp.wait_ge(out_ready, t + 1)
                sp.dma_start(out_d[:, t, :], o_row[:, t, :]).then_inc(out_stored, 16)
            sp.wait_ge(out_stored, 16 * NT)

        @block.gpsimd
        def _(pool):
            pool.memset(ones[:, :], 1.0).then_inc(consts_made, 1)
            pool.memset(pT[:, :, 0:PADS], 0.0).then_inc(pad_ready, 1)
            pool.wait_ge(win_high, 4)
            pool.tensor_tensor(win_half(win_split(1)[:, 1], 1), win_half(win(1), 1), win_half(win_split(1)[:, 0], 1),
                               ALU.subtract).then_inc(win_pool_low, 1)
            pool.wait_ge(rw_loaded, 16)
            for t in range(NT):
                pool.wait_ge(silu_ready, t + 1)
                pool.tensor_tensor(gate_sb[:, t, :], gate_sb[:, t, :], rw_sb[:, :], ALU.mult).then_inc(gate_ready, 1)
            step = 0
            pool.wait_ge(pad_ready, 1)
            for n, g in enumerate(reversed(range(H))):
                emptied(pool, ("z", 16 + n))
                src = pT[:, g, :]
                if n:
                    pool.wait_ge(pooled_ready, n)
                w = 1
                while w < WINDOWS[g]:
                    dst = psum_a if src is not psum_a else psum_b
                    pool.tensor_tensor(dst[:, w:PADS + S], src[:, w:PADS + S], src[:, 0:PADS + S - w], ALU.add)\
                        .then_inc(pool_step, 1)
                    pool.memset(dst[:, 0:w], 0.0).then_inc(pool_step, 1)
                    step += 2
                    pool.wait_ge(pool_step, step)
                    src = dst
                    w *= 2
                pool.tensor_tensor(src[:, PADS:2 * PADS], src[:, PADS:2 * PADS], corr[:, g, :], ALU.mult)\
                    .then_inc(window_ready, 1)

            def low(e, c):
                pool.wait_ge(high_ready, CH * e + c + 1)
                pool_low(pool, c).then_inc(pool_low_ready, 1)

            with pool.Fori(0, E) as e:
                for c in BY_POOL:
                    low(e, c)

            pool.wait_ge(counts_ready, 1)

            def make_zeros():
                pool.wait_ge(parts_ready, NT)
                pool.memset(zeros, 0.0).then_inc(zeros_ready, 1)

            most = further_blocks(pool, lambda e, b, n: pool.wait_ge(more["stored"], 16 * n), lambda: pool.nop(),
                                  make_zeros)
            pool.wait_ge(routed, 1)
            pool.wait_ge(rows_stored, 16 * (E - 1))
            pool.wait_ge(gathered, 2 * E)
            split_done(pool, E - 1, CH - 4)
            split_done(pool, E - 1, BY_POOL[-1])

            def fetch(rows):
                for t in range(NT):
                    if t == NT - 1:
                        pool.wait_ge(gu_done, GB * E)
                    for k in range(TOP_K):
                        n = t * TOP_K + k
                        pool.indirect_dma_start(
                            out=got(t)[:, k, :], out_offset=None, in_=rows,
                            in_offset=bass.IndirectOffsetOnAxis(ap=row_u[:, n:n + 1], axis=0))\
                            .then_inc(got_rows[n], 16)

            with pool.If(most > CAP):
                pool.wait_ge(cleared, 32)
                fetch(y_rows)
            with pool.Else():
                fetch(y_rows[0:FIRST - CAP, :])
            pool.nop()

        @block.scalar
        def _(act):
            act.dma_start(sm[:, :], small).then_inc(small_loaded, 16)
            with nc.allow_non_contiguous_dma(reason="1024 weights, one on each partition and tile"):
                act.dma_start(nm_w[:, :], norm_mix_w[0].rearrange("(k p) -> p k", p=P)).then_inc(norms_loaded, 16)
                act.dma_start(ps_w[:, :], pool_scale[0].rearrange("(g p) -> p g", p=P)).then_inc(norms_loaded, 16)
            act.dma_start(bgu_raw[:, :], b_gu[0].rearrange("e (q c) -> (e q) c", q=4)).then_inc(bgu_loaded, 16)

            norms = [0]

            def root(width, n):
                r = norms[0]
                norms[0] += 1
                act.wait_ge(ss_ready, r + 1)
                act.activation(std[:, r, 0:width], ss[:, r, 0:width], ACT.Sqrt, bias=eps_t[:, :], scale=1.0 / n)\
                    .then_inc(std_ready, 1)

            def first_norm(t):
                act.wait_ge(x_loaded[t], 16)
                if t >= 2:
                    act.wait_ge(x_turned, t - 1)
                act.activation(xn1[:, t % 2], x_sb[:, t, :], ACT.Square, accum_out=ss[:, t, 0:1]).then_inc(ss_ready, 1)
                root(1, D)

            def turned_h(t):
                act.wait_ge(h32_ready, t + 1)
                act.activation(hT[:, 0, :, t * P:(t + 1) * P], h32[:, t % 2], ACT.Copy, scale=SCALE_X)\
                    .then_inc(h_high, 1)

            def high_win(c):
                act.wait_ge(win_loaded[c], 16)
                if c == 2 or c == 3:
                    act.wait_ge(z_done, 4 * (c - 1))
                elif c == 4:
                    act.wait_ge(win_low, 7)
                for half in range(2):
                    if c == 1 and half == 1:
                        act.activation(win_half(win(c), half), win_half(win(c), half), ACT.Copy, scale=SCALE_W)\
                            .then_inc(win_scaled, 1)
                        act.wait_ge(win_scaled, 1)
                        act.activation(win_half(win_split(c)[:, 0], half), win_half(win(c), half), ACT.Copy)\
                            .then_inc(win_high, 1)
                        continue
                    act.activation(win_half(win_split(c)[:, 0], half), win_half(win(c), half), ACT.Copy,
                                   scale=SCALE_W).then_inc(win_high, 1)

            act.wait_ge(consts_made, 3)
            first_norm(0)
            first_norm(1)
            turned_h(0)
            high_win(0)
            first_norm(2)
            turned_h(1)
            first_norm(3)
            high_win(1)
            turned_h(2)
            turned_h(3)

            def qk(n):
                act.wait_ge(qk_turned, n + 1)
                dst = (qT if n < 4 else kT)[:, :, (n % 4) * P:(n % 4 + 1) * P]
                ins = act.activation(dst, bank(("qk", n)).rearrange("p (h c) -> p h c", h=H), ACT.Copy)
                free(ins, ("qk", n))

            def gate_sig(t):
                act.wait_ge(z_done, 8 + t + 1)
                act.activation(gate_sb[:, t, :], bank(("z", 8 + t)), ACT.Sigmoid, scale=UNSCALE).then_inc(sig_gate, 1)

            qk(0)
            qk(1)
            high_win(2)
            for n in range(2, 6):
                qk(n)
            high_win(3)
            gate_sig(0)
            qk(6)
            gate_sig(1)
            qk(7)
            gate_sig(2)
            gate_sig(3)
            high_win(4)
            for t in range(NT):
                act.wait_ge(z_done, 12 + t + 1)
                ins = act.activation(v_sb[:, t, :], bank(("z", 12 + t)), ACT.Copy, scale=UNSCALE)
                free(ins, ("z", 12 + t))
            for h in range(H):
                act.wait_ge(pv_done, h + 1)
                for j in range(NT):
                    ins = act.activation(mixtok[:, h, j * P:(j + 1) * P], bank(("pv", h))[:, j * P:(j + 1) * P],
                                         ACT.Square, accum_out=ss[:, 4 + h, j:j + 1])
                ins.then_inc(ss_ready, 1)
                root(NT, P)
                if h == H - 1:
                    act.dma_start(nf_row, norm_ffn_w[0:1, :].to_broadcast([P, D])).then_inc(nf_loaded, 16)
                act.wait_ge(z_done, 16 + h + 1)
                act.wait_ge(pad_ready, 1)
                ins = act.activation(pT[:, H - 1 - h, PADS:PADS + S], bank(("z", 16 + h)), ACT.Copy, scale=UNSCALE)
                free(ins, ("z", 16 + h))
            for h in range(H):
                act.wait_ge(mix_turned, h + 1)
                act.wait_ge(z_done, 20)
                ins = act.activation(mixT[:, h, :], bank(("mix", h)), ACT.Copy)
                free(ins, ("mix", h))
            act.wait_ge(norms_loaded, 32)
            for n, g in enumerate(reversed(range(H))):
                act.wait_ge(pool_done, n + 1)
                ins = act.activation(mixT[:, H + g, :], bank(("pool", n)), ACT.Copy, scale=ps_w[:, g:g + 1])
                free(ins, ("pool", n))

            def norm2(t):
                act.wait_ge(x2_ready, t + 1)
                if t >= 2:
                    act.wait_ge(h2_turned, t - 1)
                    act.wait_ge(parts_ready, t - 1)
                act.activation(xn2[:, t % 2], x_sb[:, t, :], ACT.Square, accum_out=ss[:, 8 + t, 0:1])\
                    .then_inc(ss_ready, 1)
                root(1, D)

            def high_part(t):
                act.wait_ge(xn2_ready, t + 1)
                act.activation(parts[:, 0, t, :], xn2[:, t % 2], ACT.Copy, scale=SCALE_X).then_inc(hi_ready, 1)

            def turned_h2(t):
                act.wait_ge(h2_turned, t + 1)
                if t >= 2:
                    act.wait_ge(logits_done, t - 1)
                for i in range(2):
                    ins = act.activation(h2T[:, t % 2, 4 * i:4 * i + 4, :].rearrange("p k c -> p (k c)"),
                                         bank(("h2", t, i)), ACT.Copy)
                    free(ins, ("h2", t, i))

            def high(e, c):
                act.wait_ge(slot_loaded[c % RAW], 32 * e + 16 * (c // RAW) + 16)
                if c in BY_POOL:
                    act_scale(act, c).then_inc(scaled_ready, 1)
                    act.wait_ge(scaled_ready, len(BY_POOL) * e + BY_POOL.index(c) + 1)
                if c >= RAW:
                    chunk_gone(act, e, c - RAW)
                else:
                    chunk_gone(act, e - 1, c + RAW)
                (act_scaled_high if c in BY_POOL else act_high)(act, c).then_inc(high_ready, 1)

            def first_high(c):
                act.wait_ge(slot_loaded[c], 16)
                act.wait_ge(*((z_done, 20), (scores_done, 16), (out_done, 8))[c // 2])
                if c in BY_POOL:
                    act_scale(act, c).then_inc(scaled_ready, 1)
                    act.wait_ge(scaled_ready, 1)
                (act_scaled_high if c in BY_POOL else act_high)(act, c).then_inc(high_ready, 1)

            for c in range(4):
                first_high(c)
            for t in range(NT):
                norm2(t)
                high_part(t)
                if t == NT - 1:
                    first_high(4)
                turned_h2(t)
            first_high(5)
            for t in range(NT):
                act.wait_ge(top_ready, t + 1)
                act.activation(expo[:, t, :], top8[:, t, 0:TOP_K], ACT.Exp, bias=negmax[:, t:t + 1],
                               accum_out=esum[:, t:t + 1]).then_inc(exp_ready, 1)

            def columns(e, i):
                act.wait_ge(gathered, 2 * e + 2 - i)
                act_xT(act, i).then_inc(xT_ready, 1)

            columns(0, 1)
            columns(0, 0)
            act.wait_ge(h2_turned, NT)
            act.wait_ge(parts_ready, NT)
            act.dma_start(fin_w, norm_final_w.rearrange("(a d) -> a d", a=1).to_broadcast([P, D])).then_inc(tail_loaded, 16)
            act.dma_start(y_last[BD:P, :], b_down[0]).then_inc(tail_loaded, 16)

            def turned_y(e):
                act.wait_ge(y_done, e + 1)
                for half in range(2):
                    act_yT(act, half).then_inc(yT_ready, 1)

            def finish_rows(e, first=False):
                act.wait_ge(row_turned, e + 1)
                if not first:
                    act.wait_ge(rows_stored, 16 * e)
                for half in range(2):
                    act_row(act, half).then_inc(row_ready, 1)
                act.wait_ge(row_ready, 2 * e + 2)
                store_rows(act, e * CAP).then_inc(rows_stored, 16)

            def sigmoid(e, b, first):
                act.wait_ge(glu_ready, GB * e + b + 1)
                if b >= 2 or not first:
                    act.wait_ge(act32_ready, GB * e + b - 1)
                act_sig(act, b).then_inc(sig_ready, 1)

            def act_high_part(e, b):
                act.wait_ge(act32_ready, GB * e + b + 1)
                act_ah(act, b).then_inc(ah_ready, 1)

            def expert(e, first=False, last=False, second=False):
                for c in range(RAW, CH) if first else range(10):
                    high(e, c)
                    if c == 2 and not first:
                        turned_y(e - 1)
                    if c == 4 and not first:
                        finish_rows(e - 1, second)
                sigmoid(e, 0, first)
                if not last:
                    columns(e + 1, 1)
                sigmoid(e, 1, first)
                act_high_part(e, 0)
                if not last:
                    columns(e + 1, 0)
                sigmoid(e, 2, first)
                act_high_part(e, 1)
                if not first:
                    high(e, 10)
                sigmoid(e, 3, first)
                act_high_part(e, 2)
                act_high_part(e, 3)
                if not first:
                    high(e, 11)

            expert(0, first=True)
            expert(1, second=True)
            with act.Fori(2, E - 1) as e:
                expert(e)
            expert(E - 1, last=True)
            act.wait_ge(wg_turned, 1)
            act.activation(wgT, ps[:, 0, :], ACT.Copy).then_inc(wgT_ready, 1)
            act.wait_ge(pad_cleared, 1)
            turned_y(E - 1)
            act.wait_ge(row_turned, E)
            for half in range(2):
                act_row(act, half, y_last).then_inc(row_ready, 1)

            act.wait_ge(counts_ready, 1)

            def last_stored():
                act.wait_ge(rows_stored, 16 * (E - 1))

            def one(e, b, n):
                def more_high(c):
                    act.wait_ge(more_loaded[c % RAW], 32 * n - 32 + 16 * (c // RAW) + 16)
                    if c >= RAW:
                        act.wait_ge(more["used"], CH * (n - 1) + c - RAW + 1)
                    act_high(act, c).then_inc(more["high"], 1)

                for i in (1, 0):
                    act.wait_ge(more["gathered"], 2 * n - i)
                    act_xT(act, i).then_inc(more["xT"], 1)
                for c in range(GU_CH):
                    more_high(c)
                for i in range(GB):
                    act.wait_ge(more["glu"], GB * n - GB + i + 1)
                    act_sig(act, i).then_inc(more["sig"], 1)
                    act.wait_ge(more["act32"], GB * n - GB + i + 1)
                    act_ah(act, i).then_inc(more["ah"], 1)
                for c in range(GU_CH, CH):
                    more_high(c)
                act.wait_ge(more["used"], CH * n)
                for half in range(2):
                    act_yT(act, half).then_inc(more["yT"], 1)
                act.wait_ge(more["turned"], n)
                for half in range(2):
                    act_row(act, half).then_inc(more["row"], 1)
                act.wait_ge(more["row"], 2 * n)
                act.wait_ge(cleared, 32)
                store_rows(act, b * FIRST + e * CAP).then_inc(more["stored"], 16)
                act.wait_ge(more["stored"], 16 * n)

            def skip():
                act.sem_inc(more["high"], CH)
                act.sem_inc(more["sig"], GB)
                act.sem_inc(more["ah"], GB)
                for k in ("xT", "yT", "row"):
                    act.sem_inc(more[k], 2)
                act.sem_inc(more["stored"], 16)

            further_blocks(act, one, skip, last_stored)

            for t in range(NT):
                act.wait_ge(acc_ready, 2 * t + 2)
                act.activation(o_row[:, t, :], x_sb[:, t, :], ACT.Square, accum_out=ss[:, 12 + t, 0:1])\
                    .then_inc(ss_ready, 1)
                root(1, D)

        @block.tensor
        def _(pe):
            pe.wait_ge(small_loaded, 16)
            pe.wait_ge(bgu_loaded, 16)
            for j in range(4):
                take(pe, ("bgu", j))
                pe.transpose(bank(("bgu", j))[:, 0:P], bgu_raw[:, j * P:(j + 1) * P], ident).then_inc(bgu_turned, 1)

            def turn_x(t):
                pe.wait_ge(xn_ready, t + 1)
                for k in range(KD):
                    if k % 4 == 0:
                        take(pe, ("x", t, k // 4))
                    mm = pe.transpose(bank(("x", t, k // 4))[:, (k % 4) * P:(k % 4 + 1) * P],
                                      xn1[:, t % 2, k * P:(k + 1) * P], ident)
                mm.then_inc(x_turned, 1)

            def z(n):
                c = min(n // 4, 4)
                pe.wait_ge(win_low, 2 * c + (2 if c == 0 else 1))
                if c == 1:
                    pe.wait_ge(win_pool_low, 1)
                if n < 4:
                    pe.wait_ge(hT_ready, n + 1)
                take(pe, ("z", n))
                for k in range(KD):
                    for step, (i, j) in enumerate(((0, 0), (0, 1), (1, 0))):
                        if c < 4:
                            lhsT, rhs = hT[:, i, k, (n % 4) * P:(n % 4 + 1) * P], win_split(c)[:, j, k * W:(k + 1) * W]
                        else:
                            col = k * W + (H - 1 - (n - 16)) * P
                            lhsT, rhs = win_split(c)[:, i, col:col + P], hT[:, j, k, :]
                        mm = pe.matmul(bank(("z", n)), lhsT, rhs, start=(k == 0 and step == 0),
                                       stop=(k == KD - 1 and step == 2))
                mm.then_inc(z_done, 1)

            def turn_qk(n):
                pe.wait_ge(rot_ready, n + 1)
                take(pe, ("qk", n))
                for h in range(H):
                    mm = pe.transpose(bank(("qk", n))[:, h * P:(h + 1) * P], rot[:, n % 2, h * P:(h + 1) * P], ident)
                mm.then_inc(qk_turned, 1)

            def scores(h):
                for i in range(NT):
                    take(pe, ("s", h, i))
                    emptied(pe, ("qk", 7))
                    emptied(pe, ("qk", 6))
                    pe.matmul(bank(("s", h, i))[:, 0:S - i * P], kT[:, h, i * P:(i + 1) * P], qT[:, h, i * P:S],
                              start=True, stop=True).then_inc(scores_done, 1)

            def pv(h):
                pe.wait_ge(sT_ready, NT * (h + 1))
                for t in range(NT):
                    emptied(pe, ("z", 12 + t))
                take(pe, ("pv", h))
                for j in range(NT):
                    for i in range(j + 1):
                        off = 4 * i - i * (i - 1) // 2
                        mm = pe.matmul(bank(("pv", h))[:, j * P:(j + 1) * P],
                                       sT[:, h % 2, (off + j - i) * P:(off + j - i + 1) * P],
                                       v_sb[:, i, h * P:(h + 1) * P], start=(i == 0), stop=(i == j))
                mm.then_inc(pv_done, 1)

            turn_x(0)
            turn_x(1)
            for n in range(8):
                z(n)
                if n < 2:
                    turn_x(n + 2)
                else:
                    turn_qk(n - 2)
            z(8)
            turn_qk(6)
            z(9)
            turn_qk(7)
            z(10)
            pe.wait_ge(dec_loaded, 16)
            scores(0)
            z(11)
            scores(1)
            for n in range(12, 16):
                z(n)
            for h in range(H):
                pv(h)
                if h < 2:
                    scores(h + 2)
                z(16 + h)
            for h in range(H):
                pe.wait_ge(mixtok_ready, h + 1)
                take(pe, ("mix", h))
                for j in range(NT):
                    mm = pe.transpose(bank(("mix", h))[:, j * P:(j + 1) * P], mixtok[:, h, j * P:(j + 1) * P], ident)
                mm.then_inc(mix_turned, 1)
            pe.wait_ge(wpool_loaded, 16)
            for n, g in enumerate(reversed(range(H))):
                pe.wait_ge(pooled_ready, n + 1)
                take(pe, ("pool", n))
                pe.matmul(bank(("pool", n)), wp_sb[:, g, :], pT[:, g, PADS:PADS + S], start=True, stop=True)\
                    .then_inc(pool_done, 1)

            for h in range(H):
                emptied(pe, ("mix", h))
            for c in range(2):
                pe.wait_ge(wout_loaded[c], 16)

            def project(m):
                t, half = m // 2, m % 2
                take(pe, ("out", m))
                for k in range(KD):
                    if m == 0 and k == H:
                        for n in range(H):
                            emptied(pe, ("pool", n))
                    mm = pe.matmul(bank(("out", m)), mixT[:, k, t * P:(t + 1) * P],
                                   wout(k)[:, half * 512:(half + 1) * 512], start=(k == 0), stop=(k == KD - 1))
                mm.then_inc(out_done, 1)

            def turn_h2(t):
                pe.wait_ge(xn2_ready, t + 1)
                for k in range(KD):
                    if k % 4 == 0:
                        take(pe, ("h2", t, k // 4))
                    mm = pe.transpose(bank(("h2", t, k // 4))[:, (k % 4) * P:(k % 4 + 1) * P],
                                      xn2[:, t % 2, k * P:(k + 1) * P], ident)
                mm.then_inc(h2_turned, 1)

            def route(t):
                emptied(pe, ("h2", t, 0))
                emptied(pe, ("h2", t, 1))
                pe.wait_ge(router_loaded, 32)
                take(pe, ("log", t, 0))
                for k in range(KD):
                    mm = pe.matmul(bank(("log", t, 0))[:, 0:E], h2T[:, t % 2, k, :], wr_sb[:, k, :],
                                   start=(k == 0), stop=(k == KD - 1))
                mm.then_inc(logits_done, 1)

            for t in range(NT):
                project(2 * t)
                if t >= 1:
                    turn_h2(t - 1)
                project(2 * t + 1)
                if t >= 1:
                    route(t - 1)
            turn_h2(3)
            route(3)
            take(pe, ("pos", 0))
            pe.wait_ge(consts_made, 3)
            pe.wait_ge(chosen_ready, NT)
            pos = bank(("pos", 0))
            for t in range(NT + 1):
                for i in range(min(t + 1, NT)):
                    mm = pe.matmul(pos[:, t * E:(t + 1) * E], (tri if i == t else ones)[:, :], chosen_b[:, i, :],
                                   start=(i == 0), stop=(i == min(t, NT - 1)))
            mm.then_inc(pos_done, 1)

            def gather(e, i):
                pe.wait_ge(onehot_ready, e + 1)
                pe_gather(pe, i).then_inc(gathered, 1)

            for b in range(8):
                pe.wait_ge(bank_free[b], uses[b])
            pe.wait_ge(parts_ready, NT)
            gather(0, 1)
            gather(0, 0)

            def turn_rows(e):
                pe.wait_ge(yT_ready, 2 * e + 2)
                pe_turn_rows(pe).then_inc(row_turned, 1)

            def expert(e, first=False, last=False):
                pe.wait_ge(xT_ready, 2 * e + 2)
                if not first:
                    pe.wait_ge(gu_taken, GB * e)
                for k in range(KD):
                    split_done(pe, e, k)
                    for b in range(GB):
                        mm = pe_gu(pe, k, b)
                        if k == KD - 1:
                            mm.then_inc(gu_done, 1)
                    if k < KD - 1:
                        mm.then_inc(chunk_used, 1)
                    if k == 2 and not first:
                        turn_rows(e - 1)
                if not last:
                    gather(e + 1, 1)
                    if not first:
                        pe.wait_ge(row_ready, 2 * e)
                    gather(e + 1, 0)
                for f in range(KD):
                    if f % 2 == 0:
                        pe.wait_ge(act_ready, GB * e + f // 2 + 1)
                        split_done(pe, e, GU_CH + f // 2)
                    if f == 0 and not last:
                        pe.wait_ge(xT_ready, 2 * e + 3)
                    mm = pe_down(pe, f)
                    if f % 2 == 1 and f < KD - 1:
                        mm.then_inc(chunk_used, 1)
                    elif f == KD - 1:
                        mm.then_inc(y_done, 1)

            expert(0, first=True)
            with pe.Fori(1, E - 1) as e:
                expert(e)
            expert(E - 1, last=True)
            pe.wait_ge(routed, 1)
            pe.wait_ge(gu_taken, GB * E)
            for t in range(NT):
                mm = pe.transpose(ps[:, 0, t * P:(t + 1) * P], wg[:, t, :], ident)
            mm.then_inc(wg_turned, 1)
            turn_rows(E - 1)

            pe.wait_ge(counts_ready, 1)

            def last_stored():
                pe.wait_ge(rows_stored, 16 * (E - 1))
                pe.wait_ge(wgT_ready, 1)
                pe.wait_ge(row_ready, 2 * E)

            def one(e, b, n):
                pe.wait_ge(more["onehot"], n)
                for i in (1, 0):
                    pe_gather(pe, i).then_inc(more["gathered"], 1)
                pe.wait_ge(more["xT"], 2 * n)
                for k in range(KD):
                    pe.wait_ge(more["low"], CH * (n - 1) + k + 1)
                    for i in range(GB):
                        mm = pe_gu(pe, k, i)
                    mm.then_inc(more["used"], 1)
                for f in range(KD):
                    if f % 2 == 0:
                        pe.wait_ge(more["act"], GB * n - GB + f // 2 + 1)
                        pe.wait_ge(more["low"], CH * (n - 1) + GU_CH + f // 2 + 1)
                    mm = pe_down(pe, f)
                    if f % 2 == 1:
                        mm.then_inc(more["used"], 1)
                pe.wait_ge(more["yT"], 2 * n)
                pe_turn_rows(pe).then_inc(more["turned"], 1)
                pe.wait_ge(more["stored"], 16 * n)

            def skip():
                pe.sem_inc(more["gathered"], 2)
                pe.sem_inc(more["used"], CH)
                pe.sem_inc(more["turned"], 1)

            further_blocks(pe, one, skip, last_stored)

            pe.wait_ge(wgT_ready, 1)
            pe.wait_ge(tail_loaded, 32)
            pe.wait_ge(row_ready, 2 * E)
            for m in range(2 * NT):
                t, half = m // 2, m % 2
                pe.matmul(ps[:, m, :], wgT[:, t * P:(t + 1) * P], y_last[:, half * 512:(half + 1) * 512],
                          start=True, stop=True).then_inc(bias_done, 1)

        @block.vector
        def _(dve):
            steps = [0]

            def step(ins):
                ins.then_inc(dve_step, 1)
                steps[0] += 1
                dve.wait_ge(dve_step, steps[0])

            def inverse_root(r, width, n):
                dve.wait_ge(ss_ready, r + 1)
                v, y, w = var[:, r, 0:width], rstd[:, r, 0:width], nwt[:, 0:width]
                step(dve.tensor_scalar(v, ss[:, r, 0:width], 1.0 / n, EPS, ALU.mult, ALU.add))
                dve.wait_ge(std_ready, r + 1)
                step(dve.reciprocal(y, std[:, r, 0:width]))
                step(dve.tensor_tensor(w, y, y, ALU.mult))
                step(dve.scalar_tensor_tensor(w, w, -0.5, v, ALU.mult, ALU.mult))
                step(dve.scalar_tensor_tensor(y, w, 1.5, y, ALU.add, ALU.mult))

            dve.memset(eps_t[:, :], EPS).then_inc(consts_made, 1)
            dve.wait_ge(small_loaded, 16)
            dve.tensor_copy(tri[:, :], tri_f).then_inc(consts_made, 1)
            dve.wait_ge(norms_loaded, 32)

            def turned_h(t):
                dve.wait_ge(x_turned, t + 1)
                for i in range(2):
                    ins = dve.tensor_tensor(
                        h32[:, t % 2, 4 * i:4 * i + 4, :], bank(("x", t, i)).rearrange("p (k c) -> p k c", k=4),
                        nm_w[:, 4 * i:4 * i + 4].unsqueeze(2).to_broadcast([P, 4, P]), ALU.mult)
                    free(ins, ("x", t, i))
                emptied(dve, ("x", t, 0))
                emptied(dve, ("x", t, 1))
                dve.sem_inc(h32_ready, 1)

            def low_h(t):
                dve.wait_ge(h_high, t + 1)
                dve.scalar_tensor_tensor(hT[:, 1, :, t * P:(t + 1) * P], h32[:, t % 2], SCALE_X,
                                         hT[:, 0, :, t * P:(t + 1) * P], ALU.mult, ALU.subtract).then_inc(hT_ready, 1)

            def low_win(c, half):
                dve.wait_ge(win_high, 2 * c + half + 1)
                dve.scalar_tensor_tensor(win_half(win_split(c)[:, 1], half), win_half(win(c), half), SCALE_W,
                                         win_half(win_split(c)[:, 0], half), ALU.mult, ALU.subtract).then_inc(win_low, 1)

            for t in range(NT):
                if t == 2:
                    low_h(0)
                    low_win(0, 0)
                    low_win(0, 1)
                inverse_root(t, 1, D)
                dve.tensor_scalar(xn1[:, t % 2], x_sb[:, t, :], rstd[:, t, 0:1], None, ALU.mult).then_inc(xn_ready, 1)
                if t == 0:
                    for j in range(4):
                        dve.wait_ge(bgu_turned, j + 1)
                        dst = bguT[:, :, :].rearrange("p e (ql b qh r) -> p e qh ql b r", ql=2, b=2, qh=2)[
                            :, :, :, :, j // 2, j % 2]
                        ins = dve.tensor_copy(dst, bank(("bgu", j))[:, 0:P].rearrange(
                            "p (e qh ql) -> p e qh ql", e=E, qh=2))
                        free(ins, ("bgu", j))
                if t >= 3:
                    low_h(t - 2)
                if t >= 1:
                    if t >= 3:
                        dve.wait_ge(hT_ready, t - 2)
                    turned_h(t - 1)
            low_h(NT - 2)
            low_win(1, 0)
            dve.wait_ge(hT_ready, NT - 2)
            turned_h(NT - 1)
            low_h(NT - 1)

            def rotate(n):
                t = n % 4
                dve.wait_ge(z_done, n + 1)
                if n >= 2:
                    dve.wait_ge(qk_turned, n - 1)
                    dve.wait_ge(rot_ready, n - 1)
                zz = bank(("z", n)).rearrange("p (h c) -> p h c", h=H)
                dst = rot[:, n % 2].rearrange("p (h c) -> p h c", h=H)
                tmp = sT[:, n % 2, 0:512].rearrange("p (h c) -> p h c", h=H)
                cb = rope_c[:, t, :].unsqueeze(1).to_broadcast([P, H, P])
                sb_ = rope_s[:, t, :].unsqueeze(1).to_broadcast([P, H, P])
                dve.tensor_tensor(dst, zz, cb, ALU.mult)
                dve.tensor_tensor(tmp[:, :, 0:64], zz[:, :, 64:128], sb_[:, :, 0:64], ALU.mult)
                ins = dve.tensor_tensor(tmp[:, :, 64:128], zz[:, :, 0:64], sb_[:, :, 64:128], ALU.mult)
                free(ins, ("z", n))
                emptied(dve, ("z", n))
                dve.tensor_tensor(dst, dst, tmp, ALU.add).then_inc(rot_ready, 1)

            def silu(t):
                dve.wait_ge(sig_gate, t + 1)
                ins = dve.scalar_tensor_tensor(gate_sb[:, t, :], bank(("z", 8 + t)), UNSCALE, gate_sb[:, t, :],
                                               ALU.mult, ALU.mult)
                free(ins, ("z", 8 + t))
                emptied(dve, ("z", 8 + t))
                dve.sem_inc(silu_ready, 1)

            def decayed(h):
                if h >= 2:
                    dve.wait_ge(pv_done, h - 1)
                off = 0
                for i in range(NT):
                    n = S - i * P
                    dve.wait_ge(scores_done, NT * h + i + 1)
                    ins = dve.tensor_tensor(sT[:, h % 2, off:off + n], bank(("s", h, i))[:, 0:n], dec[:, h, 0:n], ALU.mult)
                    free(ins, ("s", h, i))
                    off += n
                emptied(dve, ("s", h, 3))
                dve.sem_inc(sT_ready, NT)

            def head_norm(h):
                inverse_root(4 + h, NT, P)
                dve.wait_ge(gate_ready, NT)
                for j in range(NT):
                    ins = dve.scalar_tensor_tensor(
                        mixtok[:, h, j * P:(j + 1) * P], bank(("pv", h))[:, j * P:(j + 1) * P], rstd[:, 4 + h, j:j + 1],
                        gate_sb[:, j, h * P:(h + 1) * P], ALU.mult, ALU.mult)
                free(ins, ("pv", h))
                emptied(dve, ("pv", h))
                dve.sem_inc(mixtok_ready, 1)

            dve.wait_ge(rope_loaded, 16)
            for n in range(8):
                rotate(n)
                if n in (3, 4):
                    low_win(2, n - 3)
            dve.wait_ge(dec_loaded, 16)
            dve.wait_ge(rot_ready, 8)
            low_win(3, 0)
            silu(0)
            low_win(3, 1)
            silu(1)
            silu(2)
            decayed(0)
            silu(3)
            decayed(1)
            low_win(4, 0)
            low_win(4, 1)

            def pooled(n):
                g = H - 1 - n
                dve.wait_ge(window_ready, n + 1)
                s = psum_a if g % 2 == 0 else psum_b
                dve.scalar_tensor_tensor(pT[:, g, PADS:PADS + S], s[:, PADS:PADS + S], 1.0 / WINDOWS[g],
                                         pT[:, g, PADS:PADS + S], ALU.mult, ALU.subtract).then_inc(pooled_ready, 1)

            head_norm(0)
            decayed(2)
            head_norm(1)
            decayed(3)
            pooled(0)
            head_norm(2)
            pooled(1)
            head_norm(3)
            pooled(2)
            pooled(3)

            def residual(t):
                for half in range(2):
                    m = 2 * t + half
                    dve.wait_ge(out_done, m + 1)
                    xs = x_sb[:, t, half * 512:(half + 1) * 512]
                    ins = dve.tensor_tensor(xs, bank(("out", m)), xs, ALU.add)
                    free(ins, ("out", m))
                for half in range(2):
                    emptied(dve, ("out", 2 * t + half))
                dve.sem_inc(x2_ready, 1)

            def normed(t):
                inverse_root(8 + t, 1, D)
                if t == 0:
                    dve.wait_ge(nf_loaded, 16)
                dve.scalar_tensor_tensor(xn2[:, t % 2], x_sb[:, t, :], rstd[:, 8 + t, 0:1], nf_row,
                                         ALU.mult, ALU.mult).then_inc(xn2_ready, 1)

            def low_part(t):
                dve.wait_ge(hi_ready, t + 1)
                dve.scalar_tensor_tensor(parts[:, 1, t, :], xn2[:, t % 2], SCALE_X, parts[:, 0, t, :],
                                         ALU.mult, ALU.subtract).then_inc(parts_ready, 1)
                dve.wait_ge(parts_ready, t + 1)

            def low(e, c):
                dve.wait_ge(high_ready, CH * e + c + 1)
                dve_low(dve, c).then_inc(low_ready, 1)

            def choose(t):
                dve.wait_ge(logits_done, t + 1)
                if t == 0:
                    dve.wait_ge(router_loaded, 32)
                ins = dve.tensor_tensor(logit[:, t, :], bank(("log", t, 0))[:, 0:E], br_sb[:, :], ALU.add)
                free(ins, ("log", t, 0))
                emptied(dve, ("log", t, 0))
                step(dve.max(top8[:, t, :], logit[:, t, :]))
                step(dve.max_index(idx8[:, t, :], top8[:, t, :], logit[:, t, :]))
                step(dve.tensor_copy(idxf[:, t, :], idx8[:, t, :]))
                step(dve.tensor_tensor(is_kth[:, t], iota32.unsqueeze(1).to_broadcast([P, TOP_K, E]),
                                       idxf[:, t, 0:TOP_K].unsqueeze(2).to_broadcast([P, TOP_K, E]), ALU.is_equal))
                step(dve.tensor_reduce(chosen[:, t, :], is_kth[:, t].rearrange("p k e -> p e k"), AX_X, ALU.add))
                dve.tensor_copy(chosen_b[:, t, :], chosen[:, t, :]).then_inc(chosen_ready, 1)
                dve.tensor_scalar(negmax[:, t:t + 1], top8[:, t, 0:1], -1.0, None, ALU.mult).then_inc(top_ready, 1)

            for c in range(3):
                low(0, c)
            for t in range(NT):
                residual(t)
                normed(t)
                low_part(t)
                if t >= 1:
                    choose(t - 1)
            low(0, 4)
            choose(3)
            low(0, 5)

            dve.wait_ge(pos_done, 1)
            pos = bank(("pos", 0))
            step(dve.scalar_tensor_tensor(rank1[:, :, :].rearrange("p e t -> p t e"),
                                          pos[:, 0:NT * E].rearrange("p (t e) -> p t e", t=NT), 1.0,
                                          chosen[:, :, :], ALU.add, ALU.mult))
            dve_onehot(dve, 0, 0).then_inc(onehot_ready, 1)
            step(dve.tensor_copy(count_i[:, :], pos[:, NT * E:(NT + 1) * E]))
            step(dve.tensor_reduce(count_max[:, :], pos[:, NT * E:(NT + 1) * E], AX_X, ALU.max))
            ins = dve.tensor_copy(count_max_i[:, :], count_max[:, :])
            step(ins)
            ins = dve.tensor_tensor(rank_row[:, :, :], rank1[:, :, :].rearrange("p e t -> p t e"),
                                    e_base.unsqueeze(1).to_broadcast([P, NT, E]), ALU.add)
            free(ins, ("pos", 0))
            emptied(dve, ("pos", 0))
            dve.sem_inc(counts_ready, 1)

            def rows_and_gates():
                for b in range(1, BLOCKS):
                    step(dve.tensor_scalar(passed_b[:, :, :], rank1[:, :, :].rearrange("p e t -> p t e"),
                                           float(b * CAP), float(FIRST - CAP), ALU.is_gt, ALU.mult))
                    step(dve.tensor_tensor(rank_row[:, :, :], rank_row[:, :, :], passed_b[:, :, :], ALU.add))
                step(dve.tensor_scalar(past_first[:, :], rank1[:, E - 1, :], float(CAP), None, ALU.is_gt))
                step(dve.tensor_tensor(rank_row[:, :, E - 1], rank_row[:, :, E - 1], past_first[:, :], ALU.mult))
                every = [P, NT, TOP_K, E]
                step(dve.tensor_tensor(of_kth, is_kth, rank_row[:, :, :].unsqueeze(2).to_broadcast(every), ALU.mult))
                step(dve.tensor_reduce(row_f[:, :], of_kth.rearrange("p t k e -> p (t k) e"), AX_X, ALU.add))
                step(dve.tensor_copy(row_u[:, :], row_f[:, :]))
                dve.wait_ge(exp_ready, NT)
                step(dve.reciprocal(einv[:, :], esum[:, :]))
                step(dve.tensor_tensor(gates[:, :, :], expo[:, :, :], einv[:, :].unsqueeze(2).to_broadcast([P, NT, TOP_K]),
                                       ALU.mult))
                step(dve.tensor_tensor(of_kth, is_kth, gates[:, :, :].unsqueeze(3).to_broadcast(every), ALU.mult))
                step(dve.tensor_reduce(gdense, of_kth.rearrange("p t k e -> p t e k"), AX_X, ALU.add))
                step(dve.tensor_tensor(of_kth[:, :, :, E - 1], of_kth[:, :, :, E - 1],
                                       past_first[:, :].unsqueeze(2).to_broadcast([P, NT, TOP_K]), ALU.mult))
                step(dve.tensor_reduce(fetch_gates[:, :, :].rearrange("p t k -> p (t k)"),
                                       of_kth.rearrange("p t k e -> p (t k) e"), AX_X, ALU.add))
                step(dve.memset(wg[:, :, 0:BD], 0.0))
                step(dve.tensor_tensor(wg[:, :, 0:CAP], ranks[:, 0:CAP].unsqueeze(1).to_broadcast([P, NT, CAP]),
                                       rank1[:, E - 1, :].unsqueeze(2).to_broadcast([P, NT, CAP]), ALU.is_equal))
                step(dve.tensor_tensor(wg[:, :, 0:CAP], wg[:, :, 0:CAP], gdense[:, :, E - 1].unsqueeze(2).to_broadcast([P, NT, CAP]), ALU.mult))
                dve.sem_inc(routed, 1)

            def bias_and_clamp(e, b, first):
                dve.wait_ge(gu_done, GB * e + b + 1)
                if b >= 2 or not first:
                    dve.wait_ge(sig_ready, GB * e + b - 1)
                    dve.wait_ge(prod_ready, GB * e + b - 1)
                dve_bias(dve, e, b).then_inc(gu_taken, 1)
                dve.wait_ge(gu_taken, GB * e + b + 1)
                dve_glu(dve, b).then_inc(glu_ready, 1)
                dve_lin(dve, b).then_inc(lin_ready, 1)
                dve.wait_ge(glu_ready, GB * e + b + 1)
                dve.wait_ge(lin_ready, GB * e + b + 1)
                if b >= 2 or not first:
                    dve.wait_ge(act32_ready, GB * e + b - 1)
                dve_prod(dve, b).then_inc(prod_ready, 1)

            def activate(e, b, first):
                dve.wait_ge(prod_ready, GB * e + b + 1)
                dve.wait_ge(sig_ready, GB * e + b + 1)
                if b >= 2 or not first:
                    dve.wait_ge(ah_ready, GB * e + b - 1)
                    dve.wait_ge(act_ready, GB * e + b - 1)
                dve_act32(dve, b).then_inc(act32_ready, 1)

            def act_low_part(e, b):
                dve.wait_ge(ah_ready, GB * e + b + 1)
                dve_al(dve, b).then_inc(act_ready, 1)

            def expert(e, first=False, last=False):
                if not last:
                    dve.wait_ge(gathered, 2 * e + 2)
                    dve_onehot(dve, e + 1, 0).then_inc(onehot_ready, 1)
                for c in range(RAW, CH) if first else range(GU_CH + 1):
                    if c in BY_DVE:
                        low(e, c)
                bias_and_clamp(e, 0, first)
                bias_and_clamp(e, 1, first)
                activate(e, 0, first)
                bias_and_clamp(e, 2, first)
                activate(e, 1, first)
                act_low_part(e, 0)
                bias_and_clamp(e, 3, first)
                activate(e, 2, first)
                act_low_part(e, 1)
                activate(e, 3, first)
                act_low_part(e, 2)
                act_low_part(e, 3)
                if not first:
                    for c in range(GU_CH + 1, CH):
                        if c in BY_DVE:
                            low(e, c)

            dve.memset(y_last[64:BD, :], 0.0).then_inc(pad_cleared, 1)
            rows_and_gates()
            expert(0, first=True)
            with dve.Fori(1, E - 1) as e:
                expert(e)
            expert(E - 1, last=True)

            def last_stored():
                dve.wait_ge(rows_stored, 16 * (E - 1))

            def one(e, b, n):
                dve_onehot(dve, e, b * CAP).then_inc(more["onehot"], 1)
                for c in range(GU_CH):
                    dve.wait_ge(more["high"], CH * (n - 1) + c + 1)
                    dve_low(dve, c).then_inc(more["low"], 1)
                dve.wait_ge(more["used"], CH * (n - 1) + GU_CH)
                for i in range(GB):
                    base = GB * n - GB + i + 1
                    dve_bias(dve, e, i).then_inc(more["biased"], 1)
                    dve.wait_ge(more["biased"], base)
                    dve_lin(dve, i).then_inc(more["prod"], 1)
                    dve_glu(dve, i).then_inc(more["glu"], 1)
                    dve.wait_ge(more["prod"], 2 * base - 1)
                    dve.wait_ge(more["glu"], base)
                    dve_prod(dve, i).then_inc(more["prod"], 1)
                    dve.wait_ge(more["prod"], 2 * base)
                    dve.wait_ge(more["sig"], base)
                    dve_act32(dve, i).then_inc(more["act32"], 1)
                    dve.wait_ge(more["ah"], base)
                    dve_al(dve, i).then_inc(more["act"], 1)
                    dve.wait_ge(more["act"], base)
                for c in range(GU_CH, CH):
                    dve.wait_ge(more["high"], CH * (n - 1) + c + 1)
                    dve_low(dve, c).then_inc(more["low"], 1)
                dve.wait_ge(more["stored"], 16 * n)

            def skip():
                dve.sem_inc(more["onehot"], 1)
                dve.sem_inc(more["low"], CH)
                dve.sem_inc(more["prod"], 2 * GB)
                for k in ("biased", "glu", "act32", "act"):
                    dve.sem_inc(more[k], GB)

            further_blocks(dve, one, skip, last_stored)

            dve.wait_ge(tail_loaded, 32)

            def add_row(t, k):
                dve.wait_ge(got_rows[t * TOP_K + k], 16)
                ins = dve.scalar_tensor_tensor(x_sb[:, t, :], got(t)[:, k, :], fetch_gates[:, t, k:k + 1],
                                               x_sb[:, t, :], ALU.mult, ALU.add)
                step(ins)

            def add_last(t):
                for half in range(2):
                    dve.wait_ge(bias_done, 2 * t + half + 1)
                    xs = x_sb[:, t, half * 512:(half + 1) * 512]
                    dve.tensor_tensor(xs, ps[:, 2 * t + half, :], xs, ALU.add).then_inc(acc_ready, 1)

            def finish(t):
                inverse_root(12 + t, 1, D)
                dve.scalar_tensor_tensor(o_row[:, t, :], x_sb[:, t, :], rstd[:, 12 + t, 0:1], fin_w,
                                         ALU.mult, ALU.mult).then_inc(out_ready, 1)

            for t in range(NT):
                for k in range(TOP_K):
                    add_row(t, k)
                    if t >= 2 and k == 1:
                        finish(t - 2)
                if t >= 1:
                    add_last(t - 1)
                    if t == NT - 1:
                        add_last(NT - 1)
                        finish(NT - 2)
            finish(NT - 1)


_INS = ['x', 'norm_mix_w', 'w_in', 'ret_norm_w', 'w_pool', 'pool_scale', 'w_out', 'norm_ffn_w', 'w_router',
        'b_router', 'w_gu', 'b_gu', 'w_down', 'b_down', 'norm_final_w']


def shape_constants(seq):
    import numpy as np
    half = P // 2
    inv = np.power(np.float32(10000.0), -np.arange(half, dtype=np.float32) / np.float32(half), dtype=np.float32)
    ang = np.arange(seq, dtype=np.float32)[:, None] * inv[None, :]
    c, s = np.cos(ang.astype(np.float64)), np.sin(ang.astype(np.float64))
    nt = seq // P
    cc = np.concatenate([c, c], 1).reshape(nt, P, P).transpose(1, 0, 2).reshape(P, -1)
    sn = np.concatenate([-s, s], 1).reshape(nt, P, P).transpose(1, 0, 2).reshape(P, -1)
    rope = (np.concatenate([cc, sn], 1) * UNSCALE).astype(np.float32)

    m, n = np.arange(P)[:, None], np.arange(seq)[None, :]
    seen = (n // CHUNK) >= (m // CHUNK)
    heads = []
    for h in range(4):
        log_g = np.log1p(-np.exp2(-5.0 - h))
        heads.append(np.where(seen, np.exp(log_g * np.abs(n - m)), 0.0) * P ** -0.5)
    decay = np.concatenate(heads, 1).astype(np.float32)

    blocks = -(-seq // CAP)
    small = np.zeros((P, 384 + blocks * CAP), np.float32)
    small[:, 0:128] = np.eye(P)
    small[:, 128:256] = np.triu(np.ones((P, P)), 1)
    small[:, 256:288] = np.arange(32)
    small[:, 288:320] = CAP * np.arange(32) - 1
    for g, w in enumerate(WINDOWS):
        small[:, 320 + 16 * g:336 + 16 * g] = w / np.minimum(np.arange(16) + 1, w)
    small[:, 384:] = np.arange(blocks * CAP) + 1
    return {"rope": rope, "decay": decay, "small": small}


def kernel(**inputs):
    import numpy as _np
    import concourse.bacc as _bacc
    from concourse import mybir as _mybir
    from concourse.bass_utils import run_bass_kernel_spmd as _run

    nc = _bacc.Bacc("TRN2", target_bir_lowering=False, num_devices=1)
    arrays, args = {}, []
    for name in _INS:
        a = _np.ascontiguousarray(inputs[name])
        arrays[f"in_{name}_dram"] = a
        args.append(nc.dram_tensor(f"in_{name}_dram", a.shape, _mybir.dt.from_np(a.dtype), kind="ExternalInput").ap())
    for name, a in shape_constants(inputs["x"].shape[1]).items():
        arrays[f"const_{name}_dram"] = a
        args.append(nc.dram_tensor(f"const_{name}_dram", a.shape, _mybir.dt.from_np(a.dtype), kind="ExternalInput").ap())
    shape = inputs["x"].shape
    args.append(nc.dram_tensor("out_0_dram", shape, _mybir.dt.float32, kind="ExternalOutput").ap())
    build_program(nc, *args)
    r = _run(nc, [arrays], core_ids=[0])
    return r.results[0]["out_0_dram"]
```
